# Optimizing a Trainium2 kernel written in Bass

```python
import jax
import jax.numpy as jnp
from jax import lax
import numpy as np

D_MODEL = 1024
BATCH = 1
SEQ = 256
DEPTH = 2

N_MIXERS = 4
ALPHA = (2 * DEPTH) ** 0.25
BETA = (8 * DEPTH) ** -0.25
LN_EPS = 1e-5
D_FF = 2816
FFN_HALF = 0.5

RET_HEADS = 4
RET_DK = D_MODEL // RET_HEADS
RET_DV = 2 * RET_DK
RET_CHUNK = 128
ROPE_BASE = 10000.0
RET_GN_EPS = 1e-5

S5_WIDTH = D_MODEL
S5_GROUP = 16
S5_GROUPS = S5_WIDTH // S5_GROUP
S5_STATE = 64
S5_CHUNK = 128
S5_DT_MIN = 1e-3
S5_DT_MAX = 1e-1

RW_HEAD = 64
RW_HEADS = D_MODEL // RW_HEAD
RW_DECAY_LORA = 64
RW_AAA_LORA = 64
RW_GATE_LORA = 128
RW_GN_EPS = 64e-5
RW_N_MIX = 6

LRU_WIDTH = D_MODEL
LRU_BLOCKS = 4
LRU_BLOCK = LRU_WIDTH // LRU_BLOCKS
CONV_WIDTH = 4
LRU_C = 8.0
LRU_A_MIN = 0.9
LRU_A_MAX = 0.999

kernel_name = 'hybrid_ret_s5_rwkv7_rglru_trunk'

def _n_occ(m):
    return len(range(m, DEPTH, N_MIXERS))

def layer_norm(x, g, b):
    xf = x.astype(jnp.float32)
    mu = jnp.mean(xf, -1, keepdims=True)
    var = jnp.mean(jnp.square(xf - mu), -1, keepdims=True)
    return ((xf - mu) * lax.rsqrt(var + LN_EPS) * g + b).astype(x.dtype)

def head_norm(y, eps):
    mu = jnp.mean(y, -1, keepdims=True)
    var = jnp.mean(jnp.square(y - mu), -1, keepdims=True)
    return (y - mu) * lax.rsqrt(var + eps)

def swiglu(x, w1, w3, w2):
    return (jax.nn.silu(x @ w1) * (x @ w3)) @ w2

def rotary(t):
    T, d = t.shape[1], t.shape[-1]
    half = d // 2
    inv = ROPE_BASE ** (-jnp.arange(half, dtype=jnp.float32) / half)
    ang = jnp.arange(T, dtype=jnp.float32)[:, None] * inv[None, :]
    cos = jnp.cos(ang)[None, :, None, :]
    sin = jnp.sin(ang)[None, :, None, :]
    t1, t2 = t[..., :half], t[..., half:]
    return jnp.concatenate([t1 * cos - t2 * sin, t1 * sin + t2 * cos], axis=-1)

def retention(x, w_in, w_out):
    B, T, _ = x.shape
    H, DK, DV, C = RET_HEADS, RET_DK, RET_DV, RET_CHUNK
    nc = T // C
    q, k, v, g = jnp.split(x @ w_in, [H * DK, 2 * H * DK, 2 * H * DK + H * DV], axis=-1)
    q = rotary(q.reshape(B, T, H, DK).astype(jnp.float32))
    k = rotary(k.reshape(B, T, H, DK).astype(jnp.float32)) * (DK ** -0.5)
    v = v.reshape(B, T, H, DV).astype(jnp.float32)
    log_gamma = jnp.log1p(-jnp.power(2.0, -5.0 - jnp.arange(H, dtype=jnp.float32)))
    pos = jnp.arange(C, dtype=jnp.float32)
    rel = pos[:, None] - pos[None, :]
    inner_decay = jnp.where(rel >= 0, jnp.exp(jnp.maximum(rel, 0.0)[None] * log_gamma[:, None, None]), 0.0)
    q_decay = jnp.exp((pos + 1.0)[:, None] * log_gamma)[..., None]
    k_decay = jnp.exp((C - 1.0 - pos)[:, None] * log_gamma)[..., None]
    chunk_decay = jnp.exp(C * log_gamma)[:, None, None]

    def to_chunks(t):
        return t.reshape(B, nc, C, H, t.shape[-1]).swapaxes(0, 1)

    def chunk_step(R, qkv):
        qc, kc, vc = qkv
        s = jnp.einsum('bihd,bjhd->bhij', qc, kc) * inner_decay
        inner = jnp.einsum('bhij,bjhe->bihe', s, vc)
        cross = jnp.einsum('bihd,bhde->bihe', qc * q_decay, R)
        R = R * chunk_decay + jnp.einsum('bjhd,bjhe->bhde', kc * k_decay, vc)
        return R, inner + cross

    R0 = jnp.zeros((B, H, DK, DV), jnp.float32)
    _, o = lax.scan(chunk_step, R0, (to_chunks(q), to_chunks(k), to_chunks(v)))
    o = head_norm(o.swapaxes(0, 1).reshape(B, T, H, DV), RET_GN_EPS).reshape(B, T, H * DV)
    o = jax.nn.silu(g.astype(jnp.float32)) * o
    return o.astype(x.dtype) @ w_out

def _complex_combine(e1, e2):
    a1r, a1i, b1r, b1i = e1
    a2r, a2i, b2r, b2i = e2
    return (a2r * a1r - a2i * a1i,
            a2r * a1i + a2i * a1r,
            a2r * b1r - a2i * b1i + b2r,
            a2r * b1i + a2i * b1r + b2i)

def s5_mixer(x, w_in, a_re, a_im, b_re, b_im, c_re, c_im, d_skip, log_step, w_glu, w_out):
    B, T, _ = x.shape
    G, P, N, C = S5_GROUPS, S5_GROUP, S5_STATE, S5_CHUNK
    nc = T // C
    f32 = jnp.float32
    a_re, a_im = a_re.astype(f32), a_im.astype(f32)
    b_re, b_im = b_re.astype(f32), b_im.astype(f32)
    c_re, c_im = c_re.astype(f32), c_im.astype(f32)
    u = (x @ w_in).astype(f32)
    dt = jnp.exp(log_step.astype(f32))[:, None]
    mag = jnp.exp(dt * a_re)
    abar_re = mag * jnp.cos(dt * a_im)
    abar_im = mag * jnp.sin(dt * a_im)
    den = a_re * a_re + a_im * a_im
    f_re = ((abar_re - 1.0) * a_re + abar_im * a_im) / den
    f_im = (abar_im * a_re - (abar_re - 1.0) * a_im) / den
    bb_re = f_re[..., None] * b_re - f_im[..., None] * b_im
    bb_im = f_re[..., None] * b_im + f_im[..., None] * b_re
    a_blk_re = jnp.broadcast_to(abar_re, (B, C, G, N))
    a_blk_im = jnp.broadcast_to(abar_im, (B, C, G, N))

    def chunk_step(h, u_blk):
        h_re, h_im = h
        bu_re = jnp.einsum('bcgp,gnp->bcgn', u_blk, bb_re)
        bu_im = jnp.einsum('bcgp,gnp->bcgn', u_blk, bb_im)
        p_re, p_im, s_re, s_im = lax.associative_scan(
            _complex_combine, (a_blk_re, a_blk_im, bu_re, bu_im), axis=1)
        st_re = p_re * h_re[:, None] - p_im * h_im[:, None] + s_re
        st_im = p_re * h_im[:, None] + p_im * h_re[:, None] + s_im
        y = jnp.einsum('bcgn,gpn->bcgp', st_re, c_re) - jnp.einsum('bcgn,gpn->bcgp', st_im, c_im)
        return (st_re[:, -1], st_im[:, -1]), y

    h0 = (jnp.zeros((B, G, N), f32), jnp.zeros((B, G, N), f32))
    u_chunks = u.reshape(B, nc, C, G, P).swapaxes(0, 1)
    _, y = lax.scan(chunk_step, h0, u_chunks)
    y = y.swapaxes(0, 1).reshape(B, T, G * P) + d_skip.astype(f32) * u
    act = jax.nn.gelu(y).astype(x.dtype)
    z = act * jax.nn.sigmoid(act @ w_glu)
    return z @ w_out

def rwkv7_mixer(x, mu, w_r, w_k, w_v, w0, w1, w2, a0, a1, a2, g1, g2,
                k_k, k_a, r_k, lnx_g, lnx_b, w_o):
    B, T, D = x.shape
    H, N = RW_HEADS, RW_HEAD
    f32 = jnp.float32
    xx = jnp.pad(x, ((0, 0), (1, 0), (0, 0)))[:, :-1] - x
    xr, xw, xk, xv, xa, xg = (x + xx * mu[i] for i in range(RW_N_MIX))
    r = (xr @ w_r).astype(f32)
    k = (xk @ w_k).astype(f32)
    v = (xv @ w_v).astype(f32)
    w = -jax.nn.softplus(-(w0 + jnp.tanh(xw @ w1) @ w2).astype(f32)) - 0.5
    decay = jnp.exp(-jnp.exp(w))
    a = jax.nn.sigmoid((a0 + (xa @ a1) @ a2).astype(f32))
    g = (jax.nn.sigmoid(xg @ g1) @ g2).astype(f32)
    heads = lambda t: t.reshape(B, T, H, N)
    r, k, v, decay, a = heads(r), heads(k), heads(v), heads(decay), heads(a)
    kk = k * k_k.astype(f32).reshape(H, N)
    kk = kk / jnp.maximum(jnp.sqrt(jnp.sum(kk * kk, -1, keepdims=True)), 1e-12)
    k = k * (1.0 + (a - 1.0) * k_a.astype(f32).reshape(H, N))

    def step(S, inp):
        r_t, w_t, k_t, v_t, kk_t, a_t = inp
        sa = jnp.einsum('bhvk,bhk->bhv', S, -kk_t)
        S = (S * w_t[:, :, None, :] + sa[..., None] * (kk_t * a_t)[:, :, None, :]
             + v_t[..., None] * k_t[:, :, None, :])
        return S, jnp.einsum('bhvk,bhk->bhv', S, r_t)

    xs = tuple(t.swapaxes(0, 1) for t in (r, decay, k, v, kk, a))
    S0 = jnp.zeros((B, H, N, N), f32)
    _, y = lax.scan(step, S0, xs)
    y = y.swapaxes(0, 1)
    y = head_norm(y, RW_GN_EPS) * lnx_g.astype(f32).reshape(H, N) + lnx_b.astype(f32).reshape(H, N)
    y = y + jnp.sum(r * k * r_k.astype(f32), -1, keepdims=True) * v
    y = (y.reshape(B, T, D) * g).astype(x.dtype)
    return y @ w_o

def _real_combine(e1, e2):
    a1, b1 = e1
    a2, b2 = e2
    return a2 * a1, a2 * b1 + b2

def rglru_block(x, w_in, conv_w, conv_b, w_a, b_a, w_x, b_x, lam, w_out):
    B, T, _ = x.shape
    f32 = jnp.float32
    gate, xr = jnp.split(x @ w_in, 2, axis=-1)
    gate = jax.nn.gelu(gate)
    xr = lax.conv_general_dilated(
        xr, conv_w.astype(xr.dtype)[:, None, :], window_strides=(1,),
        padding=[(CONV_WIDTH - 1, 0)], dimension_numbers=('NWC', 'WIO', 'NWC'),
        feature_group_count=LRU_WIDTH) + conv_b
    xb = xr.reshape(B, T, LRU_BLOCKS, LRU_BLOCK)
    gr = jnp.einsum('btki,kij->btkj', xb, w_a).reshape(B, T, LRU_WIDTH) + b_a
    gi = jnp.einsum('btki,kij->btkj', xb, w_x).reshape(B, T, LRU_WIDTH) + b_x
    r_t = jax.nn.sigmoid(gr.astype(f32))
    i_t = jax.nn.sigmoid(gi.astype(f32))
    log_a = -LRU_C * r_t * jax.nn.softplus(-lam.astype(f32))
    a_t = jnp.exp(log_a)
    inp = jnp.sqrt(-jnp.expm1(2.0 * log_a)) * (i_t * xr.astype(f32))
    _, h = lax.associative_scan(_real_combine, (a_t, inp), axis=1)
    y = (h * gate.astype(f32)).astype(x.dtype)
    return y @ w_out

def setup_inputs(seed: int = 0) -> dict:
    key = jax.random.key(seed)
    ks = iter(jax.random.split(key, 64))
    f32 = jnp.float32
    D = D_MODEL

    def nrm(shape, scale):
        return scale * jax.random.normal(next(ks), shape, f32)

    def unif(shape, lo, hi):
        return jax.random.uniform(next(ks), shape, f32, lo, hi)

    nA, nB, nC, nD = (_n_occ(m) for m in range(N_MIXERS))
    x = nrm((BATCH, SEQ, D), 1.0)
    ln_g = 1.0 + nrm((DEPTH, 3, D), 0.02)
    ln_b = nrm((DEPTH, 3, D), 0.02)
    ffn_w1 = nrm((DEPTH, 2, D, D_FF), D ** -0.5)
    ffn_w3 = nrm((DEPTH, 2, D, D_FF), D ** -0.5)
    ffn_w2 = nrm((DEPTH, 2, D_FF, D), BETA * D_FF ** -0.5)

    ret_w_in = nrm((nA, D, 2 * RET_HEADS * RET_DK + 2 * RET_HEADS * RET_DV), D ** -0.5)
    ret_w_out = nrm((nA, RET_HEADS * RET_DV, D), BETA * (RET_HEADS * RET_DV) ** -0.5)

    G, P, N = S5_GROUPS, S5_GROUP, S5_STATE
    s5_w_in = nrm((nB, D, S5_WIDTH), D ** -0.5)
    s5_a_re = -0.5 + nrm((nB, G, N), 0.01)
    s5_a_im = jnp.pi * jnp.arange(N, dtype=f32)[None, None, :] + nrm((nB, G, N), 0.01)
    s5_b_re = nrm((nB, G, N, P), (2 * P) ** -0.5)
    s5_b_im = nrm((nB, G, N, P), (2 * P) ** -0.5)
    s5_c_re = nrm((nB, G, P, N), N ** -0.5)
    s5_c_im = nrm((nB, G, P, N), N ** -0.5)
    s5_d = nrm((nB, S5_WIDTH), 1.0)
    s5_log_step = unif((nB, G), float(np.log(S5_DT_MIN)), float(np.log(S5_DT_MAX)))
    s5_w_glu = nrm((nB, S5_WIDTH, S5_WIDTH), S5_WIDTH ** -0.5)
    s5_w_out = nrm((nB, S5_WIDTH, D), BETA * S5_WIDTH ** -0.5)

    rw_mu = unif((nC, RW_N_MIX, D), 0.0, 1.0)
    rw_w_r = nrm((nC, D, D), D ** -0.5)
    rw_w_k = nrm((nC, D, D), D ** -0.5)
    rw_w_v = nrm((nC, D, D), D ** -0.5)
    decay_speed = -6.0 + 5.0 * (jnp.arange(D, dtype=f32) / (D - 1)) ** 0.85 + 0.5
    rw_w0 = decay_speed[None, :] + nrm((nC, D), 0.01)
    rw_w1 = nrm((nC, D, RW_DECAY_LORA), D ** -0.5)
    rw_w2 = nrm((nC, RW_DECAY_LORA, D), 0.1 * RW_DECAY_LORA ** -0.5)
    rw_a0 = nrm((nC, D), 0.1)
    rw_a1 = nrm((nC, D, RW_AAA_LORA), D ** -0.5)
    rw_a2 = nrm((nC, RW_AAA_LORA, D), 0.1 * RW_AAA_LORA ** -0.5)
    rw_g1 = nrm((nC, D, RW_GATE_LORA), D ** -0.5)
    rw_g2 = nrm((nC, RW_GATE_LORA, D), RW_GATE_LORA ** -0.5)
    rw_k_k = 0.85 + nrm((nC, D), 0.02)
    rw_k_a = 1.0 + nrm((nC, D), 0.02)
    rw_r_k = nrm((nC, RW_HEADS, RW_HEAD), 0.1)
    rw_lnx_g = 1.0 + nrm((nC, D), 0.02)
    rw_lnx_b = nrm((nC, D), 0.02)
    rw_w_o = nrm((nC, D, D), BETA * D ** -0.5)

    lru_w_in = nrm((nD, D, 2 * LRU_WIDTH), D ** -0.5)
    lru_conv_w = nrm((nD, CONV_WIDTH, LRU_WIDTH), CONV_WIDTH ** -0.5)
    lru_conv_b = nrm((nD, LRU_WIDTH), 0.02)
    lru_w_a = nrm((nD, LRU_BLOCKS, LRU_BLOCK, LRU_BLOCK), LRU_BLOCK ** -0.5)
    lru_b_a = nrm((nD, LRU_WIDTH), 0.02)
    lru_w_x = nrm((nD, LRU_BLOCKS, LRU_BLOCK, LRU_BLOCK), LRU_BLOCK ** -0.5)
    lru_b_x = nrm((nD, LRU_WIDTH), 0.02)
    p = unif((nD, LRU_WIDTH), LRU_A_MIN, LRU_A_MAX) ** (1.0 / LRU_C)
    lru_lambda = jnp.log(p) - jnp.log1p(-p)
    lru_w_out = nrm((nD, LRU_WIDTH, D), BETA * LRU_WIDTH ** -0.5)

    return {
        'x': x, 'ln_g': ln_g, 'ln_b': ln_b,
        'ffn_w1': ffn_w1, 'ffn_w3': ffn_w3, 'ffn_w2': ffn_w2,
        'ret_w_in': ret_w_in, 'ret_w_out': ret_w_out,
        's5_w_in': s5_w_in, 's5_a_re': s5_a_re, 's5_a_im': s5_a_im,
        's5_b_re': s5_b_re, 's5_b_im': s5_b_im, 's5_c_re': s5_c_re, 's5_c_im': s5_c_im,
        's5_d': s5_d, 's5_log_step': s5_log_step, 's5_w_glu': s5_w_glu, 's5_w_out': s5_w_out,
        'rw_mu': rw_mu, 'rw_w_r': rw_w_r, 'rw_w_k': rw_w_k, 'rw_w_v': rw_w_v,
        'rw_w0': rw_w0, 'rw_w1': rw_w1, 'rw_w2': rw_w2,
        'rw_a0': rw_a0, 'rw_a1': rw_a1, 'rw_a2': rw_a2,
        'rw_g1': rw_g1, 'rw_g2': rw_g2, 'rw_k_k': rw_k_k, 'rw_k_a': rw_k_a,
        'rw_r_k': rw_r_k, 'rw_lnx_g': rw_lnx_g, 'rw_lnx_b': rw_lnx_b, 'rw_w_o': rw_w_o,
        'lru_w_in': lru_w_in, 'lru_conv_w': lru_conv_w, 'lru_conv_b': lru_conv_b,
        'lru_w_a': lru_w_a, 'lru_b_a': lru_b_a, 'lru_w_x': lru_w_x, 'lru_b_x': lru_b_x,
        'lru_lambda': lru_lambda, 'lru_w_out': lru_w_out,
    }

def reference(x, ln_g, ln_b, ffn_w1, ffn_w3, ffn_w2, ret_w_in, ret_w_out,
              s5_w_in, s5_a_re, s5_a_im, s5_b_re, s5_b_im, s5_c_re, s5_c_im,
              s5_d, s5_log_step, s5_w_glu, s5_w_out,
              rw_mu, rw_w_r, rw_w_k, rw_w_v, rw_w0, rw_w1, rw_w2,
              rw_a0, rw_a1, rw_a2, rw_g1, rw_g2, rw_k_k, rw_k_a,
              rw_r_k, rw_lnx_g, rw_lnx_b, rw_w_o,
              lru_w_in, lru_conv_w, lru_conv_b, lru_w_a, lru_b_a, lru_w_x, lru_b_x,
              lru_lambda, lru_w_out):
    for i in range(DEPTH):
        m, j = i % N_MIXERS, i // N_MIXERS
        x = layer_norm(ALPHA * x + FFN_HALF * swiglu(x, ffn_w1[i, 0], ffn_w3[i, 0], ffn_w2[i, 0]),
                       ln_g[i, 0], ln_b[i, 0])
        if m == 0:
            y = retention(x, ret_w_in[j], ret_w_out[j])
        elif m == 1:
            y = s5_mixer(x, s5_w_in[j], s5_a_re[j], s5_a_im[j], s5_b_re[j], s5_b_im[j],
                         s5_c_re[j], s5_c_im[j], s5_d[j], s5_log_step[j], s5_w_glu[j], s5_w_out[j])
        elif m == 2:
            y = rwkv7_mixer(x, rw_mu[j], rw_w_r[j], rw_w_k[j], rw_w_v[j], rw_w0[j], rw_w1[j], rw_w2[j],
                            rw_a0[j], rw_a1[j], rw_a2[j], rw_g1[j], rw_g2[j], rw_k_k[j], rw_k_a[j],
                            rw_r_k[j], rw_lnx_g[j], rw_lnx_b[j], rw_w_o[j])
        else:
            y = rglru_block(x, lru_w_in[j], lru_conv_w[j], lru_conv_b[j], lru_w_a[j], lru_b_a[j],
                            lru_w_x[j], lru_b_x[j], lru_lambda[j], lru_w_out[j])
        x = layer_norm(ALPHA * x + y, ln_g[i, 1], ln_b[i, 1])
        x = layer_norm(ALPHA * x + FFN_HALF * swiglu(x, ffn_w1[i, 1], ffn_w3[i, 1], ffn_w2[i, 1]),
                       ln_g[i, 2], ln_b[i, 2])
    return x


_drawn_inputs = setup_inputs


def setup_inputs(seed=0):
    import zlib

    import numpy as np

    out = dict(_drawn_inputs(seed))
    spreads = {}
    factors = {'s5_a_re': 64.0,
     's5_a_im': 43.016,
     's5_b_re': 60.704,
     's5_b_im': 61.12,
     's5_c_re': 60.664,
     's5_c_im': 60.816,
     's5_log_step': 45.448}
    for name, (base, spread) in spreads.items():
        noise = np.random.default_rng([zlib.crc32(name.encode()), seed]).standard_normal(out[name].shape)
        drawn = base * np.exp(spread * noise) if base else spread * noise
        out[name] = jnp.asarray(drawn.astype(out[name].dtype))
    for name, factor in factors.items():
        out[name] = (out[name] * factor).astype(out[name].dtype)
    return out
```

```python
from contextlib import ExitStack

import concourse.bass as bass
from concourse import mybir

ALU = mybir.AluOpType
ACT = mybir.ActivationFunctionType
F32 = mybir.dt.float32
F32R = mybir.dt.float32r

P = 128
D = 1024
T = 256
NT = T // P
KD = D // P
DFF = 2816
KF = DFF // P
BLK = 256
NB_FFN = DFF // BLK
HEADS, DK, DV = 4, 256, 512
NB_RET = (2 * HEADS * DK + 2 * HEADS * DV) // 512
ALPHA = 4.0 ** 0.25
LN_EPS = 1e-5
GN_EPS = 1e-5
CH = 2048
RING = 4
PAIRS = 32
NPOW = 8
TURN = 6.283185307179586
TURN_PARTS = (6.28125, 1015 / 2 ** 19, -6.516827184555041e-07)
PI_DOWN = 3.1415925
BZ_STEPS = 8
ROUNDER = 12582912.0

CHUNK_FFN = [0, 65, 98, 143]
CHUNK_RET_IN, CHUNK_RET_OUT = 33, 57
CHUNK_S5_IN, CHUNK_GLU, CHUNK_S5_OUT = 131, 135, 139
N_CHUNKS = 176
U_FFN = [0, 24, 35, 50]
U_RET, U_LAST_HEAD, U_S5_IN, U_GLU = 11, 23, 46, 48

_r = _z = 0


def _take(n, split):
    global _r, _z
    at = (_r, _z)
    _r += n
    if split:
        _z += n
    return at


TR_X, TR_FFN = {}, {}
TR_X[0] = _take(4, True)
TR_FFN[0] = _take(NB_FFN, True)
TR_BT = _take(4, False)
TR_X[1] = _take(4, True)
TR_QK = _take(8, False)
TR_HEAD = _take(8, True)
TR_X[2] = _take(4, True)
TR_FFN[1] = _take(NB_FFN, True)
TR_X[3] = _take(4, True)
TR_FFN[2] = _take(NB_FFN, True)
TR_X[4] = _take(4, True)
TR_X[5] = _take(4, True)
TR_FFN[3] = _take(NB_FFN, True)


def n_out_used(n):
    count = 0
    for first, last in ((22, 32), (57, 64), (87, 97), (120, 130), (139, 142), (165, 175)):
        count += max(0, min(n, last - 1) - first + 1)
    return count


def n_u_done(u):
    return u + 1 - (u > U_LAST_HEAD)


def n_sil(u):
    f = max(f for f in range(4) if U_FFN[f] <= u)
    return NB_FFN * f + u - U_FFN[f] + 1


def build(nc, ins, out):
    ctx = ExitStack()
    with ctx:
        def sb(name, shape, dt=F32):
            return ctx.enter_context(nc.sbuf_tensor(name, shape, dt))

        def sem(name):
            return ctx.enter_context(nc.semaphore(name))

        raw = sb("raw", [P, RING, CH])
        w_hi_sb = sb("w_hi_sb", [P, RING, CH], F32R)
        w_lo_sb = sb("w_lo_sb", [P, RING, CH], F32R)
        xt_hi = sb("xt_hi", [P, KD, T], F32R)
        xt_lo = sb("xt_lo", [P, KD, T], F32R)
        gt_hi = sb("gt_hi", [P, KF, T], F32R)
        gt_lo = sb("gt_lo", [P, KF, T], F32R)
        x = sb("x", [P, NT, D])
        gb = sb("gb", [P, 2, D])
        sil = sb("sil", [P, NT, BLK])
        ident = sb("ident", [P, P])
        minus_half = sb("minus_half", [P, 1])
        unit = sb("unit", [P, 2, 4])
        stats = sb("stats", [P, NT, 20])
        s5_pow = sb("s5_pow", [P, 2, NPOW, PAIRS])
        s5_r = sb("s5_r", [P, PAIRS])
        s5_d = sb("s5_d", [P, KD])
        region = sb("region", [P, 10752])

        def carve(at, *dims):
            n = 1
            for d in dims:
                n *= d
            v = region[:, at:at + n]
            if len(dims) == 2:
                v = v.rearrange("p (a b) -> p a b", a=dims[0])
            if len(dims) == 3:
                v = v.rearrange("p (a b c) -> p a b c", a=dims[0], b=dims[1])
            return v

        qt = carve(0, 2 * HEADS, T)
        kt_ = carve(2048, 2 * HEADS, T)
        v_sb = carve(4096, NT, DV)
        g_sb = carve(5120, NT, DV)
        og = carve(6144, NT, DV)
        cossin = carve(7168, 2, NT, P)
        masks = carve(7680, HEADS, 2, P)
        s_sb = carve(8704, 3, P)
        rot = carve(9088, 2, 2, P)
        rtmp = carve(9600, 4, 2, P)
        tab = carve(0, 2, 2, 4 * T)
        bt = carve(4096, 2, 2, P)
        ct = carve(4608, 2, 3, 4 * 32)
        ut = carve(5376, KD, T)
        rotin = carve(7424, 4, 512)
        gs = carve(9472, 2, 512)
        prod = gb[:, :, :].rearrange("p a (b n) -> p (a b) n", b=2)
        small = carve(0, 24, PAIRS)
        b_in = carve(1024, 2, PAIRS, 16)
        bz = carve(2048, 2, PAIRS, 32)
        bt_tmp = carve(4096, 2, PAIRS, 16)
        bt_all = carve(5120, KD, 2, P)
        bmul = carve(7168, 2, PAIRS, 16)

        U = [ctx.enter_context(nc.psum_tensor(f"U{i}", [P, 512], F32)) for i in range(2)]
        TR = [ctx.enter_context(nc.psum_tensor(f"TR{i}", [P, 512], F32)) for i in range(2)]
        A = ctx.enter_context(nc.psum_tensor("A", [P, 2048], F32))
        bank = [A[:, 512 * i:512 * i + 512] for i in range(4)]
        acc = [A[:, 1024 * t:1024 * t + 1024] for t in range(2)]

        bt_dram = nc.dram_tensor("bt_dram", (KD, P, 2 * P), F32).ap()
        tab_dram = nc.dram_tensor("tab_dram", (KD, P, 2 * 4 * T), F32).ap()

        raw_in = [sem(f"raw_in{i}") for i in range(RING)]
        w_hi, w_lo, out_used = sem("w_hi"), sem("w_lo"), sem("out_used")
        u_done = [sem(f"u_done{i}") for i in range(2)]
        u_free = [sem(f"u_free{i}") for i in range(2)]
        sil_done = [sem(f"sil_done{i}") for i in range(2)]
        t_done = sem("t_done")
        t_free = [sem(f"t_free{i}") for i in range(2)]
        t_hi = sem("t_hi")
        x_in, x_ready, x_scaled = sem("x_in"), sem("x_ready"), sem("x_scaled")
        gb_in, const_in, small_in = sem("gb_in"), sem("const_in"), sem("small_in")
        ret_const_in = sem("ret_const_in")
        acc_done = sem("acc_done")
        out_done = sem("out_done")
        dve_chain, act_chain, pool_chain = sem("dve_chain"), sem("act_chain"), sem("pool_chain")
        rot_done, sc_done, sc_masked = sem("rot_done"), sem("sc_done"), sem("sc_masked")
        o_done, o_read, og_done = sem("o_done"), sem("o_read"), sem("og_done")
        var_ready, rstd_ready = sem("var_ready"), sem("rstd_ready")
        p_dt, p_theta, p_trig = sem("p_dt"), sem("p_theta"), sem("p_trig")
        p_f, bt_stored = sem("p_f"), sem("bt_stored")
        tab_built = sem("tab_built")
        tab_stored = [sem(f"tab_stored{i}") for i in range(2)]
        kt_in = [sem(f"kt_in{i}") for i in range(2)]
        ct_neg = sem("ct_neg")
        bu_done, bu_read = sem("bu_done"), sem("bu_read")
        g_re, g_im = sem("g_re"), sem("g_im")
        prod_done = [sem(f"prod_done{i}") for i in range(4)]
        prod_used = [sem(f"prod_used{i}") for i in range(4)]
        y_in, act_gelu, act_hi, act_split = sem("y_in"), sem("act_gelu"), sem("act_hi"), sem("act_split")
        z_done, z_hi, z_split = sem("z_done"), sem("z_hi"), sem("z_split")

        def gt_part(gt, b, i):
            v = gt[:, 2 * b:2 * b + 2, :] if isinstance(i, int) else gt[:, bass.ds(4 * i + 2 * b, 2), :]
            return v.rearrange("p a n -> p (a n)")

        block = ctx.enter_context(nc.Block())

        @block.sync
        def _(sp):
            def load(n, i=0, step=0):
                slot = n % RING
                if n >= RING:
                    sp.wait_ge(w_lo, n - RING + 1 + step * i)
                src = ins["wstream"][n] if step == 0 else \
                    ins["wstream"][bass.ds(n + step * i, 1), :, :].rearrange("a p n -> (a p) n")
                sp.dma_start(raw[:, slot, :], src).then_inc(raw_in[slot], 16)

            def loads(first, last):
                turns = (last - first) // RING
                with sp.Fori(0, turns) as i:
                    for k in range(RING):
                        load(first + k, i, RING)
                for n in range(first + turns * RING, last):
                    load(n)

            sp.dma_start(x[:, :, :], ins["x"].rearrange("(t p) d -> p t d", p=P)).then_inc(x_in, 16)
            sp.dma_start(ident[:, :], ins["ident"]).then_inc(const_in, 16)
            for n in range(RING):
                load(n)
            sp.dma_start(small[:, 0:3, :], ins["s5_a"]).then_inc(small_in, 16)
            sp.dma_start(b_in, ins["s5_b"]).then_inc(small_in, 16)
            sp.dma_start(s5_d[:, :], ins["s5_d"]).then_inc(small_in, 16)
            loads(RING, 100)
            with sp.Fori(0, KD // 2) as i:
                for b in range(2):
                    for k in range(RING):
                        load(100 + RING * b + k, i, 2 * RING)
                    sp.wait_ge(tab_built, 2 * i + b + 1)
                    sp.dma_start(tab_dram[bass.ds(2 * i + b, 1), :, :].rearrange("a p n -> (a p) n"),
                                 tab[:, b].rearrange("p a n -> p (a n)")).then_inc(tab_stored[b], 16)

            def load_kt(kt):
                b = kt % 2
                if kt < 2:
                    for c in range(2):
                        sp.wait_ge(tab_stored[c], 16 * KD // 2)
                    sp.wait_ge(bt_stored, 16)
                else:
                    sp.wait_ge(bu_read, 2 * (kt - 1))
                    for c in range(4):
                        sp.wait_ge(prod_used[c], 2 * (kt - 1))
                sp.dma_start(tab[:, b].rearrange("p a n -> p (a n)"), tab_dram[kt]).then_inc(kt_in[b], 16)
                sp.dma_start(bt[:, b].rearrange("p a n -> p (a n)"), bt_dram[kt]).then_inc(kt_in[b], 16)
                sp.dma_start(ct[:, b, 0:2, :], ins["s5_c"][kt]).then_inc(kt_in[b], 16)

            load_kt(0)
            load_kt(1)
            for n in range(132, 141):
                load(n)
            for kt in range(2, KD):
                load_kt(kt)
            loads(141, N_CHUNKS)
            sp.wait_ge(x_ready, 2 * 6)
            sp.dma_start(out.rearrange("(t p) d -> p t d", p=P), x[:, :, :]).then_inc(out_done, 16)
            sp.wait_ge(out_done, 16)

        @block.tensor
        def _(pe):
            def w_row(n, k, cols):
                at = n % RING
                return [w[:, at, k * cols[1] + cols[0]:k * cols[1] + cols[0] + 512]
                        for w in (w_hi_sb, w_lo_sb)]

            def product(o, a_hi, a_lo, b_hi, b_lo, start, stop):
                pe.matmul(o, a_hi, b_hi, start=start, stop=False)
                pe.matmul(o, a_hi, b_lo, start=False, stop=False)
                return pe.matmul(o, a_lo, b_hi, start=False, stop=stop)

            def in_pair(n, u, i=0, du=0, between=None, l=None):
                for t in range(NT):
                    if l is not None:
                        transpose_x(l, t)
                    if u >= 1:
                        pe.wait_ge(u_free[t], u + du * i)
                    for c in range(2):
                        if t == 0:
                            pe.wait_ge(w_lo, n + c + 1 + 2 * du * i)
                        if l is not None:
                            split_x(l, t, c)
                        for k in range(4):
                            kd = 4 * c + k
                            b_hi, b_lo = w_row(n + c, k, (0, 512))
                            tok = slice(P * t, P * t + P)
                            last = product(U[t][:, :], xt_hi[:, kd, tok], xt_lo[:, kd, tok], b_hi, b_lo,
                                           kd == 0, kd == KD - 1)
                            if kd == KD - 1:
                                last.then_inc(u_done[t], 1)
                    if t == 0 and between:
                        between()

            def out_chunks(ns, k0, k_last, between=None):
                for t in range(NT):
                    tok = slice(P * t, P * t + P)
                    for c, n in enumerate(ns):
                        if t == 0:
                            pe.wait_ge(w_lo, n + 1)
                        for k in range(2):
                            kf = k0 + 2 * c + k
                            for half in range(2):
                                b_hi, b_lo = w_row(n, k, (512 * half, 1024))
                                last = product(acc[t][:, 512 * half:512 * half + 512], gt_hi[:, kf, tok],
                                               gt_lo[:, kf, tok], b_hi, b_lo, kf == 0, kf == k_last)
                        if kf == k_last:
                            last.then_inc(acc_done, 1)
                        elif t == 1:
                            last.then_inc(out_used, 1)
                    if t == 0 and between:
                        between()

            def begin_tr(r, i=0, dr=0):
                if r >= 2:
                    pe.wait_ge(t_free[r % 2], r // 2 + dr * i)

            def transpose_x(l, t):
                if l == 0:
                    pe.wait_ge(x_in, 16)
                    pe.wait_ge(const_in, 16)
                else:
                    pe.wait_ge(x_ready, 2 * (l - 1) + t + 1)
                for h in range(2):
                    r = TR_X[l][0] + 2 * t + h
                    begin_tr(r)
                    for k in range(4):
                        last = pe.transpose(TR[r % 2][:, P * k:P * k + P],
                                            x[:, t, P * (4 * h + k):P * (4 * h + k) + P], ident[:, :])
                    last.then_inc(t_done, 1)

            def split_x(l, t, h):
                r = TR_X[l][0] + 2 * t + h
                pe.wait_ge(t_free[r % 2], r // 2 + 1)

            def transpose_g(f, b, i=0):
                r = TR_FFN[f][0] + b
                begin_tr(r, i, 1)
                for t in range(NT):
                    pe.wait_ge(u_free[t], U_FFN[f] + b + 1 + 2 * i)
                for j in range(2):
                    for t in range(NT):
                        last = pe.transpose(TR[r % 2][:, 256 * j + P * t:256 * j + P * t + P],
                                            sil[:, t, P * j:P * j + P], ident[:, :])
                last.then_inc(t_done, 1)

            def ffn(f, l, extra=None):
                n, u = CHUNK_FFN[f], U_FFN[f]
                in_pair(n, u, l=l)
                with pe.Fori(0, (NB_FFN - 1) // 2) as i:
                    for b in (1, 2):
                        in_pair(n + 2 * b, u + b, i, 2, between=lambda: transpose_g(f, b - 1, i))
                n += 2 * NB_FFN
                def gt_ready(b):
                    r = TR_FFN[f][0] + b
                    pe.wait_ge(t_free[r % 2], r // 2 + 1)
                gt_ready(NB_FFN - 3)
                gt_ready(NB_FFN - 2)
                out_chunks([n], 0, KF - 1, between=lambda: transpose_g(f, NB_FFN - 1))
                if extra:
                    extra()
                for p in range(5):
                    if p == 4:
                        gt_ready(NB_FFN - 1)
                    out_chunks([n + 1 + 2 * p, n + 2 + 2 * p], 2 + 4 * p, KF - 1)

            def transpose_b():
                pe.wait_ge(pool_chain, BZ_STEPS)
                for j in range(4):
                    r = TR_BT[0] + j
                    begin_tr(r)
                    for m in range(4):
                        kt, ri = (4 * j + m) // 2, m % 2
                        last = pe.transpose(TR[r % 2][:, P * m:P * m + P],
                                            bz[:, ri, 4 * kt:4 * kt + 4, :].rearrange("p a b -> p (a b)"),
                                            ident[:, :])
                    last.then_inc(t_done, 1)

            ffn(0, 0, extra=transpose_b)

            def transpose_qk(b, t):
                r = TR_QK[0] + 2 * b + t
                begin_tr(r)
                pe.wait_ge(rot_done, 2 * b + t + 1)
                for m in range(4):
                    last = pe.transpose(TR[r % 2][:, P * m:P * m + P], rot[:, m // 2, m % 2, :], ident[:, :])
                last.then_inc(t_done, 1)

            def scores(h):
                if h == 0:
                    for r in (TR_QK[0] + 6, TR_QK[0] + 7):
                        pe.wait_ge(t_free[r % 2], r // 2 + 1)
                else:
                    pe.wait_ge(sc_masked, h)
                for j, cols in ((0, slice(0, 256)), (1, slice(128, 256))):
                    o = bank[0][:, 0:256] if j == 0 else bank[0][:, 256:384]
                    for d in range(2):
                        last = pe.matmul(o, kt_[:, 2 * h + d, P * j:P * j + P], qt[:, 2 * h + d, cols],
                                         start=d == 0, stop=d == 1)
                last.then_inc(sc_done, 1)

            def o_bank(h, t):
                return U[t][:, :] if h == HEADS - 1 else bank[1 + t]

            def attend(h):
                pe.wait_ge(sc_masked, h + 1)
                for t in range(NT):
                    pe.wait_ge(u_free[t], U_RET + 4 + 2 * h + 1)
                if h == HEADS - 1:
                    for t in range(NT):
                        pe.wait_ge(u_free[t], U_LAST_HEAD)
                elif h >= 1:
                    pe.wait_ge(o_read, 2 * h)
                pe.matmul(o_bank(h, 0), s_sb[:, 0, :], v_sb[:, 0, :], start=True, stop=True).then_inc(o_done, 1)
                pe.matmul(o_bank(h, 1), s_sb[:, 1, :], v_sb[:, 0, :], start=True, stop=False)
                pe.matmul(o_bank(h, 1), s_sb[:, 2, :], v_sb[:, 1, :], start=False, stop=True).then_inc(o_done, 1)

            def transpose_head(h):
                for t in range(NT):
                    r = TR_HEAD[0] + 2 * h + t
                    begin_tr(r)
                    pe.wait_ge(og_done, 2 * h + t + 1)
                    for m in range(4):
                        last = pe.transpose(TR[r % 2][:, P * m:P * m + P], og[:, t, P * m:P * m + P], ident[:, :])
                    last.then_inc(t_done, 1)

            for b in range(NB_RET):
                def between_tiles():
                    if 1 <= b <= 4:
                        transpose_qk(b - 1, 1)
                    if b == 5:
                        scores(0)
                    if b >= 6 and b % 2 == 0:
                        attend(b // 2 - 3)
                    if b >= 7 and b % 2 == 1:
                        scores((b - 5) // 2)
                        transpose_head((b - 7) // 2)

                in_pair(CHUNK_RET_IN + 2 * b, U_RET + b, between=between_tiles, l=1 if b == 0 else None)
                if b < 4:
                    transpose_qk(b, 0)
            attend(HEADS - 1)
            for h in range(HEADS):
                if h == 1:
                    transpose_head(HEADS - 1)
                for t in range(NT):
                    r = TR_HEAD[0] + 2 * h + t
                    pe.wait_ge(t_free[r % 2], r // 2 + 1)
                if h == 0:
                    pe.wait_ge(o_read, 2 * (HEADS - 1))
                    pe.wait_ge(sc_masked, HEADS)
                out_chunks([CHUNK_RET_OUT + 2 * h, CHUNK_RET_OUT + 2 * h + 1], 4 * h, 4 * HEADS - 1)
            ffn(1, 2)

            ffn(2, 3)

            def columns_pair(n, u, first=None):
                for m in range(4):
                    h = m // 2
                    if m % 2 == 0:
                        pe.wait_ge(u_free[h], u)
                    for c in range(2):
                        if m == 0:
                            pe.wait_ge(w_lo, n + c + 1)
                        for k in range(4):
                            kd = 4 * c + k
                            at = (n + c) % RING
                            cols = slice(512 * k + P * m, 512 * k + P * m + P)
                            last = product(U[h][:, 256 * (m % 2):256 * (m % 2) + 256],
                                           w_hi_sb[:, at, cols], w_lo_sb[:, at, cols],
                                           xt_hi[:, kd, :], xt_lo[:, kd, :], kd == 0, kd == KD - 1)
                    if m % 2 == 1:
                        last.then_inc(u_done[h], 1)

            for t in range(NT):
                transpose_x(4, t)
            for t in range(NT):
                for h in range(2):
                    split_x(4, t, h)
            for b in range(2):
                columns_pair(CHUNK_S5_IN + 2 * b, U_S5_IN + b)

            def b_u(unit):
                kt, pp = unit // 2, unit % 2
                if pp == 0:
                    pe.wait_ge(kt_in[kt % 2], 48 * (kt // 2 + 1))
                pe.wait_ge(u_free[kt % 4 // 2], U_S5_IN + kt // 4 + 1)
                if unit >= 2:
                    pe.wait_ge(bu_read, unit - 1)
                for q in range(2):
                    for ri in range(2):
                        rows = slice(32 * (2 * pp + q), 32 * (2 * pp + q) + 32)
                        last = pe.matmul(bank[2 * (unit % 2) + q][:, 256 * ri:256 * ri + 256],
                                         bt[rows, kt % 2, ri, :], ut[rows, kt, :], start=True, stop=True)
                last.then_inc(bu_done, 1)

            def c_g(unit):
                kt, pp = unit // 2, unit % 2
                if pp == 0:
                    if kt >= 2:
                        pe.wait_ge(y_in, kt - 1)
                    else:
                        pe.wait_ge(u_free[kt], U_GLU)
                    pe.wait_ge(ct_neg, kt + 1)
                for m, part in enumerate((0, 1, 0, 2)):
                    pe.wait_ge(prod_done[m], unit + 1)
                    for q in range(2):
                        i = 2 * pp + q
                        last = pe.matmul(U[kt % 2][32 * i:32 * i + 32, 0:256],
                                         ct[:, kt % 2, part, 32 * i:32 * i + 32],
                                         prod[:, m, 256 * q:256 * q + 256], start=m == 0, stop=m == 3,
                                         skip_group_check=True)
                    last.then_inc(prod_used[m], 1)

            b_u(0)
            for unit in range(2 * KD):
                if unit + 1 < 2 * KD:
                    b_u(unit + 1)
                c_g(unit)
            pe.wait_ge(act_split, KD)
            for b in range(2):
                columns_pair(CHUNK_GLU + 2 * b, U_GLU + b)
            for p in range(2):
                pe.wait_ge(z_split, 2 * (p + 1))
                out_chunks([CHUNK_S5_OUT + 2 * p, CHUNK_S5_OUT + 2 * p + 1], 4 * p, KD - 1)
            ffn(3, 5)

        @block.scalar
        def _(act):
            def prep(n, i=0, step=0, used=True):
                if n >= N_CHUNKS:
                    return
                slot = n % RING
                act.wait_ge(raw_in[slot], 16 * (n // RING + 1) + 4 * step * i)
                if not used:
                    act.wait_ge(out_used, n_out_used(n - RING))
                act.activation(w_hi_sb[:, slot, :], raw[:, slot, :], ACT.Copy).then_inc(w_hi, 1)

            def split_x(l, t):
                for h in range(2):
                    r = TR_X[l][0] + 2 * t + h
                    act.wait_ge(t_done, r + 1)
                    act.activation(xt_hi[:, 4 * h:4 * h + 4, P * t:P * t + P],
                                   TR[r % 2][:, :].rearrange("p (k n) -> p k n", k=4), ACT.Copy)\
                       .then_inc(t_hi, 1)

            def scale_x(l, t):
                act.activation(x[:, t, :], x[:, t, :], ACT.Copy, scale=ALPHA).then_inc(x_scaled, 1)

            def load_gb(norm):
                if norm > 0:
                    act.wait_ge(x_ready, 2 * norm)
                for j, name in enumerate(("ln_g", "ln_b")):
                    act.dma_start(gb[:, j, :], ins[name][norm:norm + 1, :].to_broadcast([P, D]))\
                       .then_inc(gb_in, 16)

            def open_stage(l, n, norm):
                split_x(l, 0)
                if l == 0:
                    prep(0)
                    prep(1)
                scale_x(l, 0)
                if l > 0:
                    prep(n + 2, used=False)
                split_x(l, 1)
                scale_x(l, 1)
                if l == 0:
                    prep(n + 2)
                prep(n + 3)
                if norm is not None:
                    load_gb(norm)

            def silu_half(u, t, i=0):
                act.wait_ge(u_done[t], n_u_done(u) + 2 * i)
                act.activation(sil[:, t, :], U[t][:, 0:BLK], ACT.Silu).then_inc(sil_done[t], 1)

            def split_g(f, b, i=0):
                r = TR_FFN[f][0] + b
                act.wait_ge(t_done, r + 1 + 2 * i)
                act.activation(gt_part(gt_hi, b, i), TR[r % 2][:, :], ACT.Copy).then_inc(t_hi, 1)

            def ffn(f, l, norm, extra=None, late=None):
                n, u = CHUNK_FFN[f], U_FFN[f]
                open_stage(l, n, norm)
                silu_half(u, 0)
                if extra:
                    extra()
                with act.Fori(0, (NB_FFN - 1) // 2) as i:
                    for b in (1, 2):
                        silu_half(u + b - 1, 1, i)
                        prep(n + 2 * b + 2, i, 4)
                        prep(n + 2 * b + 3, i, 4)
                        split_g(f, b - 1, i)
                        silu_half(u + b, 0, i)
                n += 2 * NB_FFN
                silu_half(u + NB_FFN - 1, 1)
                prep(n + 2)
                prep(n + 3)
                split_g(f, NB_FFN - 1)
                if late:
                    late()
                for m in range(4, 13):
                    prep(n + m, used=False)

            def s5_exp_dt():
                act.wait_ge(small_in, 48)
                act.activation(small[:, 3, :], small[:, 2, :], ACT.Exp).then_inc(p_dt, 1)

            def s5_trig():
                act.wait_ge(p_theta, 1)
                act.activation(s5_r[:, :], small[:, 4, :], ACT.Exp)
                act.activation(small[:, 12, :], small[:, 10, :], ACT.Sin)
                act.activation(small[:, 13, :], small[:, 10, :], ACT.Sin, scale=0.5).then_inc(p_trig, 1)

            def store_bt():
                for j in range(4):
                    r = TR_BT[0] + j
                    act.wait_ge(t_done, r + 1)
                    act.activation(bt_all[:, 2 * j:2 * j + 2].rearrange("p k a n -> p (k a n)"),
                                   TR[r % 2][:, :], ACT.Copy).then_inc(t_free[r % 2], 1)
                for j in range(4):
                    r = TR_BT[0] + j
                    act.wait_ge(t_free[r % 2], r // 2 + 1)
                act.dma_start(bt_dram.rearrange("k p n -> p k n"),
                              bt_all.rearrange("p k a n -> p k (a n)")).then_inc(bt_stored, 16)

            def ret_constants():
                act.wait_ge(bt_stored, 16)
                act.dma_start(cossin.rearrange("p a t n -> p (a t n)"), ins["cossin"]).then_inc(ret_const_in, 16)
                act.dma_start(masks.rearrange("p h a n -> p (h a n)"), ins["masks"]).then_inc(ret_const_in, 16)

            load_gb(0)
            s5_exp_dt()
            ffn(0, 0, None, extra=s5_trig, late=store_bt)
            ret_constants()

            def move_qk(b, t):
                r = TR_QK[0] + 2 * b + t
                act.wait_ge(t_done, r + 1)
                dst = qt if b < 2 else kt_
                j = 4 * (b % 2)
                act.activation(dst[:, j:j + 4, P * t:P * t + P],
                               TR[r % 2][:, :].rearrange("p (k n) -> p k n", k=4), ACT.Copy)\
                   .then_inc(t_free[r % 2], 1)

            def take_vg(b, t):
                if b < 4:
                    return
                h = (b - 4) // 2
                act.wait_ge(u_done[t], n_u_done(U_RET + b))
                if b % 2 == 0:
                    if h >= 1:
                        act.wait_ge(o_done, 2 * h)
                    act.activation(v_sb[:, t, :], U[t][:, :], ACT.Copy).then_inc(u_free[t], 1)
                else:
                    if h >= 1:
                        act.wait_ge(og_done, 2 * (h - 1) + t + 1)
                    act.activation(g_sb[:, t, :], U[t][:, :], ACT.Silu).then_inc(u_free[t], 1)

            def split_head(h):
                for t in range(NT):
                    r = TR_HEAD[0] + 2 * h + t
                    act.wait_ge(t_done, r + 1)
                    act.activation(gt_hi[:, 4 * h:4 * h + 4, P * t:P * t + P],
                                   TR[r % 2][:, :].rearrange("p (k n) -> p k n", k=4), ACT.Copy)\
                       .then_inc(t_hi, 1)

            n = CHUNK_RET_IN
            open_stage(1, n, 1)
            take_vg(0, 0)
            for b in range(1, NB_RET):
                if b <= 4:
                    move_qk(b - 1, 0)
                take_vg(b - 1, 1)
                if b < 5:
                    act.wait_ge(u_done[1], n_u_done(U_RET + b - 1))
                prep(n + 2 * b + 2)
                prep(n + 2 * b + 3)
                if b <= 4:
                    move_qk(b - 1, 1)
                if b >= 7 and b % 2 == 1:
                    split_head((b - 7) // 2)
                take_vg(b, 0)
            take_vg(NB_RET - 1, 1)
            n = CHUNK_RET_OUT
            prep(n + 2)
            prep(n + 3)
            split_head(HEADS - 1)
            for m in range(4, 10):
                prep(n + m, used=False)
            ffn(1, 2, 2)

            ffn(2, 3, 3)
            n = CHUNK_S5_IN
            split_x(4, 0)
            prep(n + 2, used=False)
            split_x(4, 1)
            for t in range(NT):
                scale_x(4, t)
            prep(n + 3)

            def take_u(b, h):
                act.wait_ge(u_done[h], n_u_done(U_S5_IN + b))
                k = 4 * b + 2 * h
                act.activation(ut[:, k:k + 2, :].rearrange("p k n -> p (k n)"), U[h][:, :], ACT.Copy)\
                   .then_inc(u_free[h], 1)

            take_u(0, 0)
            take_u(0, 1)
            prep(n + 4)
            prep(n + 5)
            take_u(1, 0)
            take_u(1, 1)
            prep(n + 6)
            prep(n + 7)

            def negate_c(kt):
                act.wait_ge(kt_in[kt % 2], 48 * (kt // 2 + 1))
                act.activation(ct[:, kt % 2, 2, :], ct[:, kt % 2, 1, :], ACT.Copy, scale=-1.0).then_inc(ct_neg, 1)

            def gelu_y(kt):
                act.wait_ge(y_in, kt + 1)
                act.activation(ut[:, kt, :], sil[:, kt % 2, :], ACT.Gelu_apprx_tanh).then_inc(act_gelu, 1)
                act.wait_ge(act_gelu, kt + 1)
                act.activation(xt_hi[:, kt, :], ut[:, kt, :], ACT.Copy).then_inc(act_hi, 1)

            negate_c(0)
            negate_c(1)
            for kt in range(KD):
                gelu_y(kt)
                if kt + 2 < KD:
                    negate_c(kt + 2)
            for c in range(4):
                act.wait_ge(prod_used[c], 2 * KD)
            load_gb(4)

            def sigmoid(b, h):
                act.wait_ge(u_done[h], n_u_done(U_GLU + b))
                if b >= 1:
                    act.wait_ge(z_done, h + 1)
                act.activation(rotin[:, h, :], U[h][:, :], ACT.Sigmoid).then_inc(u_free[h], 1)

            def split_z(b, h):
                act.wait_ge(z_done, 2 * b + h + 1)
                k = 4 * b + 2 * h
                act.activation(gt_hi[:, k:k + 2, :].rearrange("p k n -> p (k n)"), gs[:, h, :], ACT.Copy)\
                   .then_inc(z_hi, 1)

            n = CHUNK_GLU
            for b in range(2):
                sigmoid(b, 0)
                split_z(b, 0)
                sigmoid(b, 1)
                prep(n + 2 * b + 4)
                prep(n + 2 * b + 5)
                split_z(b, 1)
            n = CHUNK_S5_OUT
            for m in range(4, 6):
                prep(n + m, used=False)
            ffn(3, 5, 5)

        @block.vector
        def _(dve):
            chain = [0]
            n_var = [0]

            def link(ins_):
                chain[0] += 1
                ins_.then_inc(dve_chain, 1)
                dve.wait_ge(dve_chain, chain[0])

            def prep(n, i=0, step=0):
                if n >= N_CHUNKS:
                    return
                slot = n % RING
                dve.wait_ge(w_hi, n + 1 + step * i)
                dve.tensor_tensor(w_lo_sb[:, slot, :], raw[:, slot, :], w_hi_sb[:, slot, :].bitcast(F32),
                                  ALU.subtract).then_inc(w_lo, 1)

            def split(dst, hi, r, z, i=0):
                dve.wait_ge(t_hi, z + 1 + 2 * i)
                src = TR[r % 2][:, :]
                if len(dst.shape) == 3:
                    src = src.rearrange("p (k n) -> p k n", k=4)
                dve.tensor_tensor(dst, src, hi.bitcast(F32), ALU.subtract).then_inc(t_free[r % 2], 1)

            def split_x(l, t):
                for h in range(2):
                    r, z = (v + 2 * t + h for v in TR_X[l])
                    split(xt_lo[:, 4 * h:4 * h + 4, P * t:P * t + P],
                          xt_hi[:, 4 * h:4 * h + 4, P * t:P * t + P], r, z)

            def norm(k, t, factor):
                xt = x[:, t, :]
                st = stats[:, t, :]
                dve.wait_ge(acc_done, 2 * k + t + 1)
                dve.wait_ge(x_scaled, 2 * k + t + 1)
                link(dve.scalar_tensor_tensor(out=xt, in0=acc[t], scalar=factor, in1=xt,
                                              op0=ALU.mult, op1=ALU.add))
                dve.bn_stats(st[:, 0:6], xt[:, 0:512])
                link(dve.bn_stats(st[:, 6:12], xt[:, 512:1024]))
                link(dve.bn_aggr(st[:, 12:14], st[:, 0:12]))
                n_var[0] += 1
                dve.tensor_scalar(st[:, 14:15], st[:, 13:14], LN_EPS, None, ALU.add).then_inc(var_ready, 1)
                dve.wait_ge(gb_in, 32 * (k + 1))
                link(dve.scalar_tensor_tensor(out=xt, in0=xt, scalar=st[:, 12:13], in1=gb[:, 0, :],
                                              op0=ALU.subtract, op1=ALU.mult))
                dve.wait_ge(rstd_ready, n_var[0])
                dve.scalar_tensor_tensor(out=xt, in0=xt, scalar=st[:, 15:16], in1=gb[:, 1, :],
                                         op0=ALU.mult, op1=ALU.add).then_inc(x_ready, 1)

            def open_stage(l, n, factor):
                for t in range(NT):
                    if l > 0:
                        norm(l - 1, t, factor)
                    split_x(l, t)
                    if l == 0 and t == 0:
                        prep(0)
                        prep(1)
                prep(n + 2)
                prep(n + 3)

            def gate(u, t, i=0):
                dve.wait_ge(sil_done[t], n_sil(u) + 2 * i)
                dve.tensor_tensor(sil[:, t, :], sil[:, t, :], U[t][:, BLK:2 * BLK], ALU.mult)\
                   .then_inc(u_free[t], 1)

            def split_g(f, b, i=0):
                r, z = (v + b for v in TR_FFN[f])
                split(gt_part(gt_lo, b, i), gt_part(gt_hi, b, i), r, z, i)

            def ffn(f, l, factor, extra=None, late=None):
                n, u = CHUNK_FFN[f], U_FFN[f]
                open_stage(l, n, factor)
                if extra:
                    extra()
                gate(u, 0)
                if late:
                    late()
                with dve.Fori(0, (NB_FFN - 1) // 2) as i:
                    for b in (1, 2):
                        gate(u + b - 1, 1, i)
                        prep(n + 2 * b + 2, i, 4)
                        prep(n + 2 * b + 3, i, 4)
                        split_g(f, b - 1, i)
                        gate(u + b, 0, i)
                n += 2 * NB_FFN
                gate(u + NB_FFN - 1, 1)
                prep(n + 2)
                prep(n + 3)
                split_g(f, NB_FFN - 1)
                for m in range(4, 13):
                    prep(n + m)

            are, aim, dt = small[:, 0, :], small[:, 1, :], small[:, 3, :]

            def tt(out_, a, b, op):
                return dve.tensor_tensor(out_, a, b, op)

            def s5_theta():
                dve.wait_ge(p_dt, 1)
                tt(small[:, 4, :], dt, are, ALU.mult)
                link(tt(small[:, 5, :], dt, aim, ALU.mult))
                link(dve.tensor_scalar(small[:, 6, :], small[:, 5, :], 1.0 / TURN, ROUNDER, ALU.mult, ALU.add))
                link(dve.tensor_scalar(small[:, 7, :], small[:, 6, :], ROUNDER, None, ALU.subtract))
                src = small[:, 5, :]
                for j, part in enumerate(TURN_PARTS):
                    link(dve.scalar_tensor_tensor(out=small[:, 8 + j, :], in0=small[:, 7, :], scalar=-part,
                                                  in1=src, op0=ALU.mult, op1=ALU.add))
                    src = small[:, 8 + j, :]
                dve.tensor_scalar(small[:, 10, :], small[:, 10, :], -PI_DOWN, PI_DOWN, ALU.max, ALU.min)\
                   .then_inc(p_theta, 1)

            def s5_factors():
                s = lambda j: small[:, j, :]
                dve.wait_ge(p_trig, 1)
                mag, sin, sin_half = s5_r[:, :], s(12), s(13)
                cos, am1, ai, den, t0, t1 = s(14), s(15), s(16), s(17), s(18), s(19)
                link(dve.scalar_tensor_tensor(out=t0, in0=sin_half, scalar=-2.0, in1=sin_half,
                                              op0=ALU.mult, op1=ALU.mult))
                link(dve.tensor_scalar(cos, t0, 1.0, None, ALU.add))
                tt(ai, mag, sin, ALU.mult)
                link(tt(am1, mag, cos, ALU.mult))
                link(dve.tensor_scalar(am1, am1, 1.0, None, ALU.subtract))
                tt(t0, are, are, ALU.mult)
                link(tt(t1, aim, aim, ALU.mult))
                link(tt(den, t0, t1, ALU.add))
                link(dve.reciprocal(den, den))
                tt(t0, am1, are, ALU.mult)
                link(tt(t1, ai, aim, ALU.mult))
                link(tt(t0, t0, t1, ALU.add))
                link(tt(s(20), t0, den, ALU.mult))
                tt(t0, ai, are, ALU.mult)
                link(tt(t1, am1, aim, ALU.mult))
                link(tt(t0, t0, t1, ALU.subtract))
                link(tt(s(21), t0, den, ALU.mult))
                dve.tensor_copy(s5_pow[:, 0, 0, :], cos)
                link(dve.tensor_scalar(s5_pow[:, 1, 0, :], sin, -1.0, None, ALU.mult))
                for k in range(1, NPOW):
                    c, ns = s5_pow[:, 0, k - 1, :], s5_pow[:, 1, k - 1, :]
                    tt(t0, c, c, ALU.mult)
                    tt(t1, ns, ns, ALU.mult)
                    link(dve.scalar_tensor_tensor(out=s5_pow[:, 1, k, :], in0=c, scalar=2.0, in1=ns,
                                                  op0=ALU.mult, op1=ALU.mult))
                    link(tt(s5_pow[:, 0, k, :], t0, t1, ALU.subtract))
                dve.tensor_copy(s(22), s(20)).then_inc(p_f, 1)

            ffn(0, 0, 0.5, extra=s5_theta, late=s5_factors)

            def rotate(b, t):
                if b >= 4:
                    return
                dve.wait_ge(u_done[t], n_u_done(U_RET + b))
                src = U[t][:, :].rearrange("p (h a n) -> p h a n", h=2, a=2)
                cos, sin = (cossin[:, j, t, :].unsqueeze(1).to_broadcast([P, 2, P]) for j in range(2))
                if b == 0 and t == 0:
                    dve.wait_ge(ret_const_in, 32)
                if b or t:
                    dve.wait_ge(rot_done, 2 * b + t)
                dve.tensor_tensor(rtmp[:, 0], src[:, :, 0], cos, ALU.mult)
                dve.tensor_tensor(rtmp[:, 1], src[:, :, 1], sin, ALU.mult)
                dve.tensor_tensor(rtmp[:, 2], src[:, :, 0], sin, ALU.mult)
                dve.tensor_tensor(rtmp[:, 3], src[:, :, 1], cos, ALU.mult).then_inc(u_free[t], 1)
                dve.wait_ge(u_free[t], U_RET + b + 1)
                if b or t:
                    dve.wait_ge(t_done, TR_QK[0] + 2 * b + t)
                dve.tensor_tensor(rot[:, :, 0, :], rtmp[:, 0], rtmp[:, 1], ALU.subtract)
                dve.tensor_tensor(rot[:, :, 1, :], rtmp[:, 2], rtmp[:, 3], ALU.add).then_inc(rot_done, 1)

            def mask_scores(h):
                dve.wait_ge(sc_done, h + 1)
                if h >= 1:
                    dve.wait_ge(o_done, 2 * h)
                dve.tensor_tensor(s_sb[:, 0:2, :].rearrange("p a n -> p (a n)"), bank[0][:, 0:256],
                                  masks[:, h].rearrange("p a n -> p (a n)"), ALU.mult)
                dve.tensor_tensor(s_sb[:, 2, :], bank[0][:, 256:384], masks[:, h, 0, :], ALU.mult)\
                   .then_inc(sc_masked, 1)

            def norm_head(h, t):
                o = U[t][:, :] if h == HEADS - 1 else bank[1 + t]
                st = stats[:, t, :]
                dve.wait_ge(o_done, 2 * h + t + 1)
                if h >= 1:
                    dve.wait_ge(t_done, TR_HEAD[0] + 2 * (h - 1) + t + 1)
                link(dve.bn_stats(st[:, 0:6], o))
                link(dve.bn_aggr(st[:, 12:14], st[:, 0:6]))
                n_var[0] += 1
                dve.tensor_scalar(st[:, 14:15], st[:, 13:14], GN_EPS, None, ALU.add).then_inc(var_ready, 1)
                dve.wait_ge(u_free[t], U_RET + 5 + 2 * h + 1)
                read = u_free[t] if h == HEADS - 1 else o_read
                dve.scalar_tensor_tensor(out=og[:, t, :], in0=o, scalar=st[:, 12:13], in1=g_sb[:, t, :],
                                         op0=ALU.subtract, op1=ALU.mult).then_inc(read, 1)
                dve.wait_ge(read, U_LAST_HEAD + 1 if h == HEADS - 1 else 2 * h + t + 1)
                dve.wait_ge(rstd_ready, n_var[0])
                dve.tensor_scalar(og[:, t, :], og[:, t, :], st[:, 15:16], None, ALU.mult).then_inc(og_done, 1)

            def split_head(h):
                for t in range(NT):
                    r, z = (v + 2 * h + t for v in TR_HEAD)
                    split(gt_lo[:, 4 * h:4 * h + 4, P * t:P * t + P],
                          gt_hi[:, 4 * h:4 * h + 4, P * t:P * t + P], r, z)

            n = CHUNK_RET_IN
            open_stage(1, n, 0.5)
            rotate(0, 0)
            for b in range(1, NB_RET):
                rotate(b - 1, 1)
                prep(n + 2 * b + 2)
                prep(n + 2 * b + 3)
                if b >= 5 and b % 2 == 1:
                    mask_scores((b - 5) // 2)
                if b >= 7 and b % 2 == 1:
                    split_head((b - 7) // 2)
                if b >= 6 and b % 2 == 0:
                    for t in range(NT):
                        norm_head(b // 2 - 3, t)
                rotate(b, 0)
            n = CHUNK_RET_OUT
            prep(n + 2)
            prep(n + 3)
            for t in range(NT):
                norm_head(HEADS - 1, t)
            split_head(HEADS - 1)
            for m in range(4, 10):
                prep(n + m)
            ffn(1, 2, 1.0)

            ffn(2, 3, 0.5)
            n = CHUNK_S5_IN
            open_stage(4, n, 0.5)
            for m in range(4, 8):
                prep(n + m)

            def turn_in(unit):
                kt, pp = unit // 2, unit % 2
                cos, nsin = (tab[:, kt % 2, j, 512 * pp:512 * pp + 512].rearrange("p (q n) -> p q n", q=2)
                             for j in range(2))
                at = 1024 * (unit % 2)
                re, im = (A[:, at:at + 1024].rearrange("p (q a n) -> p q a n", q=2, a=2)[:, :, j, :]
                          for j in range(2))
                m = [rotin[:, j, :].rearrange("p (q n) -> p q n", q=2) for j in range(4)]
                if pp == 0:
                    dve.wait_ge(kt_in[kt % 2], 48 * (kt // 2 + 1))
                dve.wait_ge(bu_done, unit + 1)
                if unit >= 1:
                    dve.wait_ge(g_im, unit)
                tt(m[0], re, cos, ALU.mult)
                tt(m[1], im, nsin, ALU.mult)
                tt(m[2], im, cos, ALU.mult)
                tt(m[3], re, nsin, ALU.mult).then_inc(bu_read, 1)
                dve.wait_ge(bu_read, unit + 1)
                tt(m[0], m[0], m[1], ALU.subtract)
                link(tt(m[2], m[2], m[3], ALU.add))
                for j, (done, used) in enumerate(((g_re, prod_done[1]), (g_im, prod_done[3]))):
                    if unit >= 1:
                        dve.wait_ge(used, unit)
                    for q in range(2):
                        pair = 4 * kt + 2 * pp + q
                        last = dve.tensor_tensor_scan(
                            gs[:, j, 256 * q:256 * q + 256], s5_r[:, pair:pair + 1].to_broadcast([P, T]),
                            m[2 * j][:, q, :], 0.0, ALU.mult, ALU.add)
                    last.then_inc(done, 1)

            def add_du(kt):
                dve.wait_ge(prod_used[3], 2 * kt + 2)
                if kt >= 2:
                    dve.wait_ge(act_gelu, kt - 1)
                dve.scalar_tensor_tensor(out=sil[:, kt % 2, :], in0=ut[:, kt, :], scalar=s5_d[:, kt:kt + 1],
                                         in1=U[kt % 2][:, 0:256], op0=ALU.mult, op1=ALU.add)\
                   .then_inc(y_in, 1)

            def split_act(kt):
                dve.wait_ge(act_hi, kt + 1)
                tt(xt_lo[:, kt, :], ut[:, kt, :], xt_hi[:, kt, :].bitcast(F32), ALU.subtract)\
                    .then_inc(act_split, 1)

            for unit in range(2 * KD):
                turn_in(unit)
                if unit >= 2 and unit % 2 == 0:
                    add_du(unit // 2 - 1)
                if unit >= 3 and unit % 2 == 1:
                    split_act((unit - 3) // 2)
            add_du(KD - 1)
            split_act(KD - 1)

            n = CHUNK_GLU
            for b in range(2):
                for h in range(2):
                    k = 4 * b + 2 * h
                    dve.wait_ge(u_free[h], U_GLU + b + 1)
                    tt(gs[:, h, :], ut[:, k:k + 2, :].rearrange("p k n -> p (k n)"), rotin[:, h, :], ALU.mult)\
                        .then_inc(z_done, 1)
                    if h == 1:
                        prep(n + 2 * b + 4)
                        prep(n + 2 * b + 5)
                    dve.wait_ge(z_hi, 2 * b + h + 1)
                    tt(gt_lo[:, k:k + 2, :].rearrange("p k n -> p (k n)"), gs[:, h, :],
                       gt_hi[:, k:k + 2, :].rearrange("p k n -> p (k n)").bitcast(F32), ALU.subtract)\
                        .then_inc(z_split, 1)
            n = CHUNK_S5_OUT
            for m in range(4, 6):
                prep(n + m)
            ffn(3, 5, 1.0)
            for t in range(NT):
                norm(5, t, 0.5)

        @block.gpsimd
        def _(pool):
            def tt(out_, a, b, op):
                return pool.tensor_tensor(out_, a, b, op)

            chain = [0]

            def link(ins_):
                chain[0] += 1
                ins_.then_inc(pool_chain, 1)
                pool.wait_ge(pool_chain, chain[0])

            n_var = [0]

            def rsqrt(norms):
                for _ in range(norms):
                    for t in range(NT):
                        n_var[0] += 1
                        pool.wait_ge(var_ready, n_var[0])
                        tt(stats[:, t, 15:16], stats[:, t, 14:15], minus_half[:, :], ALU.pow)\
                            .then_inc(rstd_ready, 1)

            pool.memset(minus_half[:, :], -0.5)
            pool.memset(unit[:, 0, :], 1.0)
            link(pool.memset(unit[:, 1, :], 0.0))
            link(pool.memset(bz.rearrange("p a b c -> p (a b c)"), 0.0))
            pool.wait_ge(p_f, 1)
            pool.wait_ge(small_in, 48)
            f_re, f_im = (small[:, j, :].unsqueeze(2).to_broadcast([P, PAIRS, 16]) for j in (20, 21))
            for ri, (other, op) in enumerate(((1, ALU.subtract), (0, ALU.add))):
                tt(bt_tmp[:, ri], f_re, b_in[:, ri], ALU.mult)
                link(tt(bmul[:, ri], f_im, b_in[:, other], ALU.mult))
                for g in range(2):
                    half = slice(64 * g, 64 * g + 64)
                    link(tt(bz[half, ri, :, 16 * g:16 * g + 16], bt_tmp[half, ri], bmul[half, ri], op))
            assert chain[0] == BZ_STEPS

            rsqrt(1 + HEADS + 1)
            pool.wait_ge(x_ready, 4)
            per_table = 3 * NPOW
            base = chain[0]

            def build_table(b, i):
                c, ns = (tab[:, b, j, :].rearrange("p (q t) -> p q t", q=4) for j in range(2))
                at = base + per_table * b + 2 * per_table * i
                if not isinstance(i, int):
                    pool.wait_ge(tab_stored[b], 16 * i)
                one, zero = (unit[:, j, :].unsqueeze(2) for j in range(2))
                tt(c[:, :, 0:1], one, one, ALU.mult)
                tt(ns[:, :, 0:1], zero, one, ALU.mult).then_inc(pool_chain, 1)
                for k in range(NPOW):
                    m = 1 << k
                    pairs = slice(4 * b, 4 * b + 4) if isinstance(i, int) else bass.ds(8 * i + 4 * b, 4)
                    pc, pns = (s5_pow[:, j, k, pairs].unsqueeze(2).to_broadcast([P, 4, m]) for j in range(2))
                    tmp = [rotin[:, j, 0:4 * m].rearrange("p (q t) -> p q t", q=4) for j in range(4)]
                    pool.wait_ge(pool_chain, at + 1 + 3 * k)
                    tt(tmp[0], c[:, :, 0:m], pc, ALU.mult)
                    tt(tmp[1], ns[:, :, 0:m], pns, ALU.mult)
                    tt(tmp[2], c[:, :, 0:m], pns, ALU.mult)
                    tt(tmp[3], ns[:, :, 0:m], pc, ALU.mult).then_inc(pool_chain, 1)
                    pool.wait_ge(pool_chain, at + 2 + 3 * k)
                    tt(c[:, :, m:2 * m], tmp[0], tmp[1], ALU.subtract).then_inc(pool_chain, 1)
                    tt(ns[:, :, m:2 * m], tmp[2], tmp[3], ALU.add)\
                        .then_inc(pool_chain if k < NPOW - 1 else tab_built, 1)

            for b in range(2):
                build_table(b, 0)
            rsqrt(1)
            with pool.Fori(1, KD // 2) as i:
                for b in range(2):
                    build_table(b, i)

            rsqrt(1)
            for step in range(2 * KD):
                kt, pp = step // 2, step % 2
                cos, nsin = (tab[:, kt % 2, j, 512 * pp:512 * pp + 512] for j in range(2))
                for m, (w, j) in enumerate(((cos, 0), (nsin, 0), (nsin, 1), (cos, 1))):
                    if m % 2 == 0:
                        pool.wait_ge((g_re, g_im)[j], step + 1)
                    if step >= 1:
                        pool.wait_ge(prod_used[m], step)
                    tt(prod[:, m, :], w, gs[:, j, :], ALU.mult).then_inc(prod_done[m], 1)
            rsqrt(2)


def _chunks_in(w):
    import numpy as np
    n = w.shape[1] // 512
    a = w.reshape(2, 4, 128, n, 512).transpose(3, 0, 2, 1, 4)
    return np.ascontiguousarray(a).reshape(2 * n, 128, 2048)


def _chunks_out(w):
    import numpy as np
    n = w.shape[0] // 256
    return np.ascontiguousarray(w.reshape(n, 2, 128, 1024).transpose(0, 2, 1, 3)).reshape(n, 128, 2048)


def _interleave(a, b, n):
    import numpy as np
    k = a.shape[0]
    return np.stack([a.reshape(k, -1, n), b.reshape(k, -1, n)], axis=2).reshape(k, -1)


def _lay_out(inp):
    import numpy as np
    f = np.float32
    parts = []

    def ffn(i, j):
        parts.append(_chunks_in(_interleave(inp["ffn_w1"][i, j], inp["ffn_w3"][i, j], 256)))
        parts.append(_chunks_out(inp["ffn_w2"][i, j]))

    ffn(0, 0)
    w = inp["ret_w_in"][0]
    parts.append(_chunks_in(w[:, :2048]))
    parts.append(_chunks_in(_interleave(w[:, 2048:4096], w[:, 4096:], 512)))
    parts.append(_chunks_out(inp["ret_w_out"][0]))
    ffn(0, 1)
    ffn(1, 0)
    parts.append(_chunks_in(inp["s5_w_in"][0]))
    parts.append(_chunks_in(inp["s5_w_glu"][0]))
    parts.append(_chunks_out(inp["s5_w_out"][0]))
    ffn(1, 1)

    def states(a):
        a = a.reshape(32, 2, 64, *a.shape[2:])
        return np.ascontiguousarray(np.moveaxis(a, 0, 2)).reshape(128, 32, *a.shape[3:])

    step = np.broadcast_to(inp["s5_log_step"][0][:, None], (64, 64))
    a_par = np.stack([states(inp["s5_a_re"][0]), states(inp["s5_a_im"][0]), states(step)], axis=1)
    b_par = np.stack([states(inp["s5_b_re"][0]), states(inp["s5_b_im"][0])], axis=1)
    c = np.zeros((8, 128, 2, 4, 32), f)
    for ri, name in enumerate(("s5_c_re", "s5_c_im")):
        cs = states(inp[name][0].transpose(0, 2, 1)).reshape(128, 8, 4, 16).transpose(1, 0, 2, 3)
        c[:, :64, ri, :, :16] = cs[:, :64]
        c[:, 64:, ri, :, 16:] = cs[:, 64:]

    half = 128
    inv = f(10000.0) ** (-np.arange(half, dtype=f) / f(half))
    ang = np.arange(256, dtype=f)[:, None] * inv[None, :]
    cossin = np.stack([np.cos(ang), np.sin(ang)]).astype(f)
    cossin = cossin.reshape(2, 2, 128, 128).transpose(2, 0, 1, 3).reshape(128, 512)
    lg = np.log1p(-np.power(2.0, -5.0 - np.arange(4, dtype=np.float64)))[:, None, None]
    j, i = np.arange(128.0)[:, None], np.arange(128.0)[None, :]
    inner = np.where(i >= j, np.exp(np.maximum(i - j, 0) * lg), 0.0)
    cross = np.exp((128 + i - j) * lg)
    masks = (np.stack([inner, cross], axis=1) / 16.0).astype(f)
    masks = masks.transpose(2, 0, 1, 3).reshape(128, 1024)
    return {
        "x": inp["x"][0], "wstream": np.concatenate(parts), "ident": np.eye(128, dtype=f),
        "ln_g": inp["ln_g"].reshape(6, 1024), "ln_b": inp["ln_b"].reshape(6, 1024),
        "s5_a": a_par, "s5_b": b_par, "s5_c": c.reshape(8, 128, 2, 128),
        "s5_d": inp["s5_d"][0].reshape(8, 128).T, "cossin": cossin, "masks": masks,
    }


def kernel(**inputs):
    import numpy as np
    import concourse.bacc as bacc
    from concourse.bass_utils import run_bass_kernel_spmd

    nc = bacc.Bacc("TRN2", target_bir_lowering=False, num_devices=1, dynamic_dma_scratch_size=1024)
    laid = {k: np.ascontiguousarray(v) for k, v in _lay_out({k: np.asarray(v) for k, v in inputs.items()}).items()}
    ins = {k: nc.dram_tensor(f"in_{k}", v.shape, F32, kind="ExternalInput").ap() for k, v in laid.items()}
    out = nc.dram_tensor("out", (T, D), F32, kind="ExternalOutput").ap()
    build(nc, ins, out)
    r = run_bass_kernel_spmd(nc, [{f"in_{k}": v for k, v in laid.items()}], core_ids=[0])
    return r.results[0]["out"].reshape(1, T, D)
```

```python
from contextlib import ExitStack

import concourse.bass as bass
from concourse import mybir

ALU = mybir.AluOpType
ACT = mybir.ActivationFunctionType
F32 = mybir.dt.float32
F32R = mybir.dt.float32r

P = 128
D = 1024
T = 256
NT = T // P
KD = D // P
DFF = 2816
KF = DFF // P
BLK = 256
NB_FFN = DFF // BLK
HEADS, DK, DV = 4, 256, 512
NB_RET = (2 * HEADS * DK + 2 * HEADS * DV) // 512
ALPHA = 4.0 ** 0.25
LN_EPS = 1e-5
GN_EPS = 1e-5
CH = 2048
RING = 4
PAIRS = 32
NC = T // 2
NPOW = 7
TURN = 6.283185307179586
TURN_PARTS = (6.28125, 1015 / 2 ** 19, -6.516827184555041e-07)
PI_DOWN = 3.1415925
ROUNDER = 12582912.0

CHUNK_FFN = [0, 65, 98, 143]
CHUNK_RET_IN, CHUNK_RET_OUT = 33, 57
CHUNK_S5_IN, CHUNK_GLU, CHUNK_S5_OUT = 131, 135, 139
N_CHUNKS = 176
U_FFN = [0, 24, 35, 48]
U_RET, U_LAST_HEAD, U_S5_IN = 11, 23, 46

_r = _z = 0


def _take(n, split):
    global _r, _z
    at = (_r, _z)
    _r += n
    if split:
        _z += n
    return at


TR_X, TR_FFN = {}, {}
TR_X[0] = _take(4, True)
TR_FFN[0] = _take(NB_FFN, True)
TR_BT = _take(9, False)
TR_X[1] = _take(4, True)
TR_QK = _take(8, False)
TR_HEAD = _take(8, True)
TR_X[2] = _take(4, True)
TR_FFN[1] = _take(NB_FFN, True)
TR_X[3] = _take(4, True)
TR_FFN[2] = _take(NB_FFN, True)
TR_X[4] = _take(4, True)
TR_X[5] = _take(4, True)
TR_FFN[3] = _take(NB_FFN, True)


def n_out_used(n):
    count = 0
    for first, last in ((22, 32), (57, 64), (87, 97), (120, 130), (139, 142), (165, 175)):
        count += max(0, min(n, last - 1) - first + 1)
    return count


def n_u_done(u):
    return u + 1 - (u > U_LAST_HEAD)


def n_sil(u):
    f = max(f for f in range(4) if U_FFN[f] <= u)
    return NB_FFN * f + u - U_FFN[f] + 1


def build(nc, ins, out):
    ctx = ExitStack()
    with ctx:
        def sb(name, shape, dt=F32):
            return ctx.enter_context(nc.sbuf_tensor(name, shape, dt))

        def sem(name):
            return ctx.enter_context(nc.semaphore(name))

        raw = sb("raw", [P, RING, CH])
        w_hi_sb = sb("w_hi_sb", [P, RING, CH], F32R)
        w_lo_sb = sb("w_lo_sb", [P, RING, CH], F32R)
        xt_hi = sb("xt_hi", [P, KD, T], F32R)
        xt_lo = sb("xt_lo", [P, KD, T], F32R)
        gt_hi = sb("gt_hi", [P, KF, T], F32R)
        gt_lo = sb("gt_lo", [P, KF, T], F32R)
        x = sb("x", [P, NT, D])
        gb = sb("gb", [P, 2, D])
        sil = sb("sil", [P, NT, BLK])
        ident = sb("ident", [P, P])
        minus_half = sb("minus_half", [P, 1])
        unit = sb("unit", [P, 2, 4])
        stats = sb("stats", [P, NT, 20])
        s5_pow = sb("s5_pow", [P, 2, NPOW + 1, PAIRS])
        s5_abar = sb("s5_abar", [P, 3, PAIRS])
        s5_t = sb("s5_t", [P, KD, 16])
        s5_d = sb("s5_d", [P, KD])
        region = sb("region", [P, 11536])

        def carve(at, *dims):
            n = 1
            for d in dims:
                n *= d
            v = region[:, at:at + n]
            if len(dims) == 1:
                return v
            if len(dims) == 2:
                v = v.rearrange("p (a b) -> p a b", a=dims[0])
            if len(dims) == 3:
                v = v.rearrange("p (a b c) -> p a b c", a=dims[0], b=dims[1])
            return v

        qt = carve(0, 2 * HEADS, T)
        kt_ = carve(2048, 2 * HEADS, T)
        v_sb = carve(4096, NT, DV)
        g_sb = carve(5120, NT, DV)
        og = carve(6144, NT, DV)
        cossin = carve(7168, 2, NT, P)
        masks = carve(7680, HEADS, 2, P)
        s_sb = carve(8704, 3, P)
        rot = carve(9088, 2, 2, P)
        rtmp = carve(9600, 4, 2, P)
        tab = carve(0, 2, 2, 4 * NC)
        bt = carve(2048, 2, 4, P)
        ct = carve(3072, 2, 4, 4 * 32)
        ut = carve(4096, KD, T)
        rotin = carve(6144, 4, 512)
        gs = carve(8192, 2, 512)
        upad = carve(9216, 4, T)
        h_sb = carve(10240, 2, 4, NC + 2)
        tm = carve(11280, P)
        bd_mask = carve(11408, P)
        prod = gb[:, :, :].rearrange("p a (b n) -> p (a b) n", b=2)
        small = carve(0, 24, PAIRS)
        c_cmp = carve(768, 2, PAIRS, 16)
        b_in = carve(1792, 2, PAIRS, 16)
        bz = carve(2816, 4, PAIRS, 32)
        bprod = carve(6912, 2, PAIRS, 16)
        bbar = carve(7936, 2, PAIRS, 16)
        ca = carve(8960, 2, PAIRS, 16)
        bt_out = carve(9984, 2, 512)

        U = [ctx.enter_context(nc.psum_tensor(f"U{i}", [P, 512], F32)) for i in range(2)]
        TR = [ctx.enter_context(nc.psum_tensor(f"TR{i}", [P, 512], F32)) for i in range(2)]
        A = ctx.enter_context(nc.psum_tensor("A", [P, 2048], F32))
        bank = [A[:, 512 * i:512 * i + 512] for i in range(4)]
        acc = [A[:, 1024 * t:1024 * t + 1024] for t in range(2)]

        bt_dram = nc.dram_tensor("bt_dram", (KD, P, 4 * P), F32).ap()
        ca_dram = nc.dram_tensor("ca_dram", (P, 2, KD, 4 * 16), F32).ap()
        tab_dram = nc.dram_tensor("tab_dram", (KD, P, 2 * 4 * NC), F32).ap()

        raw_in = [sem(f"raw_in{i}") for i in range(RING)]
        w_hi, w_lo, out_used = sem("w_hi"), sem("w_lo"), sem("out_used")
        u_done = [sem(f"u_done{i}") for i in range(2)]
        u_free = [sem(f"u_free{i}") for i in range(2)]
        sil_done = [sem(f"sil_done{i}") for i in range(2)]
        t_done = sem("t_done")
        t_free = [sem(f"t_free{i}") for i in range(2)]
        t_hi = sem("t_hi")
        x_in = [sem(f"x_in{t}") for t in range(NT)]
        x_ready, x_scaled = sem("x_ready"), sem("x_scaled")
        gb_in, const_in = sem("gb_in"), sem("const_in")
        small_in, b_landed = sem("small_in"), sem("b_landed")
        ret_const_in = sem("ret_const_in")
        acc_done = sem("acc_done")
        out_done = sem("out_done")
        dve_chain, pool_chain = sem("dve_chain"), sem("pool_chain")
        rot_done, sc_done, sc_masked = sem("rot_done"), sem("sc_done"), sem("sc_masked")
        o_done, o_read, og_done = sem("o_done"), sem("o_read"), sem("og_done")
        var_ready, rstd_ready = sem("var_ready"), sem("rstd_ready")
        p_dt, p_theta, p_trig = sem("p_dt"), sem("p_theta"), sem("p_trig")
        bz_ready = sem("bz_ready")
        p_f, p_ca, ca_stored = sem("p_f"), sem("p_ca"), sem("ca_stored")
        bt_out_free = [sem(f"bt_out_free{i}") for i in range(2)]
        tab_built = sem("tab_built")
        tab_stored = [sem(f"tab_stored{i}") for i in range(2)]
        bt_in, tab_in, ct_in = ([sem(f"{k}_in{i}") for i in range(2)] for k in ("bt", "tab", "ct"))
        upad_ready, h_re, h_im = sem("upad_ready"), sem("h_re"), sem("h_im")
        zeroed, tm_ready, y_done, mask_in = sem("zeroed"), sem("tm_ready"), sem("y_done"), sem("mask_in")
        bu_done, bu_read = sem("bu_done"), sem("bu_read")
        g_re, g_im = sem("g_re"), sem("g_im")
        prod_done = [sem(f"prod_done{i}") for i in range(4)]
        y_in, act_gelu, act_hi, act_split = sem("y_in"), sem("act_gelu"), sem("act_hi"), sem("act_split")
        glu_used, glu_done, sig_done = sem("glu_used"), sem("glu_done"), sem("sig_done")
        z_done, z_hi, z_split = sem("z_done"), sem("z_hi"), sem("z_split")

        def gt_part(gt, b, i):
            v = gt[:, 2 * b:2 * b + 2, :] if isinstance(i, int) else gt[:, bass.ds(4 * i + 2 * b, 2), :]
            return v.rearrange("p a n -> p (a n)")

        def by_parity(xt, h, t):
            return xt[:, 4 * h:4 * h + 4, :].rearrange("p k (a c) -> p k a c", a=2)[:, :, :, 64 * t:64 * t + 64]

        def from_parity(gt, k):
            return gt[:, k:k + 2, :].rearrange("p k (c a) -> p k a c", a=2)

        block = ctx.enter_context(nc.Block())

        @block.sync
        def _(sp):
            def load(n, i=0, step=0):
                slot = n % RING
                if n >= RING:
                    sp.wait_ge(w_lo, n - RING + 1 + step * i)
                src = ins["wstream"][n] if step == 0 else \
                    ins["wstream"][bass.ds(n + step * i, 1), :, :].rearrange("a p n -> (a p) n")
                sp.dma_start(raw[:, slot, :], src).then_inc(raw_in[slot], 16)

            def loads(first, last):
                turns = (last - first) // RING
                with sp.Fori(0, turns) as i:
                    for k in range(RING):
                        load(first + k, i, RING)
                for n in range(first + turns * RING, last):
                    load(n)

            sp.dma_start(small[:, 0:3, :], ins["s5_a"]).then_inc(small_in, 16)
            sp.dma_start(x[:, 0, :], ins["x"][0:P, :]).then_inc(x_in[0], 16)
            sp.dma_start(ident[:, :], ins["ident"]).then_inc(const_in, 16)
            load(0)
            load(1)
            sp.dma_start(x[:, 1, :], ins["x"][P:T, :]).then_inc(x_in[1], 16)
            load(2)
            load(3)
            sp.dma_start(b_in, ins["s5_b"]).then_inc(b_landed, 16)
            sp.dma_start(c_cmp, ins["s5_c_compact"]).then_inc(b_landed, 16)
            sp.dma_start(s5_d[:, :], ins["s5_d"]).then_inc(b_landed, 16)
            loads(RING, 100)
            with sp.Fori(0, KD // 2) as i:
                for b in range(2):
                    for k in range(RING):
                        load(100 + RING * b + k, i, 2 * RING)
                    sp.wait_ge(tab_built, 2 * i + b + 1)
                    sp.dma_start(tab_dram[bass.ds(2 * i + b, 1), :, :].rearrange("a p n -> (a p) n"),
                                 tab[:, b].rearrange("p a n -> p (a n)")).then_inc(tab_stored[b], 16)

            def load_bt(kt):
                b = kt % 2
                if kt >= 2:
                    sp.wait_ge(bu_done, kt - 1)
                sp.dma_start(bt[:, b].rearrange("p a n -> p (a n)"), bt_dram[kt]).then_inc(bt_in[b], 16)

            def load_tab(kt):
                b = kt % 2
                if kt >= 2:
                    sp.wait_ge(g_im, kt - 1)
                    for m in (3, 2):
                        sp.wait_ge(prod_done[m], kt - 1)
                sp.dma_start(tab[:, b].rearrange("p a n -> p (a n)"), tab_dram[kt]).then_inc(tab_in[b], 16)

            def load_ct(kt):
                b = kt % 2
                if kt >= 2:
                    sp.wait_ge(y_done, kt - 1)
                sp.dma_start(ct[:, b, 0:2, :], ins["s5_c"][kt]).then_inc(ct_in[b], 16)
                for g in range(2):
                    half = slice(64 * g, 64 * g + 64)
                    for ri in range(2):
                        sp.dma_start(ct[half, b, 2 + ri, :].rearrange("p (i g n) -> p i g n", i=4, g=2)[:, :, g, :],
                                     ca_dram[half, ri, kt, :].rearrange("p (i n) -> p i n", i=4))\
                          .then_inc(ct_in[b], 16)

            for c in range(2):
                sp.wait_ge(tab_stored[c], 16 * KD // 2)
                sp.wait_ge(bt_out_free[c], 16 * KD // 2)
            sp.wait_ge(ca_stored, 16)
            sp.wait_ge(zeroed, 1)
            sp.dma_start(bd_mask, ins["bd_mask"]).then_inc(mask_in, 16)
            for kt in range(2):
                load_bt(kt)
                load_tab(kt)
                load_ct(kt)
            for n in range(132, 141):
                load(n)
            load_bt(2)
            for kt in range(2, KD):
                if kt + 1 < KD:
                    load_bt(kt + 1)
                load_tab(kt)
                load_ct(kt)
            loads(141, N_CHUNKS)
            for t in range(NT):
                for h in range(2):
                    cols = slice(512 * h, 512 * h + 512)
                    sp.wait_ge(x_ready, 4 * 5 + 2 * t + h + 1)
                    sp.dma_start(out[P * t:P * t + P, cols], x[:, t, cols]).then_inc(out_done, 16)
            sp.wait_ge(out_done, 16 * 2 * NT)

        @block.tensor
        def _(pe):
            def w_row(n, k, cols):
                at = n % RING
                return [w[:, at, k * cols[1] + cols[0]:k * cols[1] + cols[0] + 512]
                        for w in (w_hi_sb, w_lo_sb)]

            def product(o, a_hi, a_lo, b_hi, b_lo, start, stop, **group):
                pe.matmul(o, a_hi, b_hi, start=start, stop=False, **group)
                pe.matmul(o, a_hi, b_lo, start=False, stop=False, **group)
                return pe.matmul(o, a_lo, b_hi, start=False, stop=stop, **group)

            def in_pair(n, u, i=0, du=0, between=None, l=None):
                for t in range(NT):
                    if l is not None:
                        transpose_x(l, t)
                    if u >= 1:
                        pe.wait_ge(u_free[t], u + du * i)
                    for c in range(2):
                        if t == 0:
                            pe.wait_ge(w_lo, n + c + 1 + 2 * du * i)
                        if l is not None:
                            split_x(l, t, c)
                        for k in range(4):
                            kd = 4 * c + k
                            b_hi, b_lo = w_row(n + c, k, (0, 512))
                            tok = slice(P * t, P * t + P)
                            last = product(U[t][:, :], xt_hi[:, kd, tok], xt_lo[:, kd, tok], b_hi, b_lo,
                                           kd == 0, kd == KD - 1)
                            if kd == KD - 1:
                                last.then_inc(u_done[t], 1)
                    if t == 0 and between:
                        between()

            def out_chunks(ns, k0, k_last, between=None):
                for t in range(NT):
                    tok = slice(P * t, P * t + P)
                    for half in range(2):
                        for c, n in enumerate(ns):
                            if t == 0 and half == 0:
                                pe.wait_ge(w_lo, n + 1)
                            for k in range(2):
                                kf = k0 + 2 * c + k
                                b_hi, b_lo = w_row(n, k, (512 * half, 1024))
                                last = product(acc[t][:, 512 * half:512 * half + 512], gt_hi[:, kf, tok],
                                               gt_lo[:, kf, tok], b_hi, b_lo, kf == 0, kf == k_last)
                            if kf == k_last:
                                last.then_inc(acc_done, 1)
                            elif t == 1 and half == 1:
                                last.then_inc(out_used, 1)
                    if t == 0 and between:
                        between()

            def begin_tr(r, i=0, dr=0):
                if r >= 2:
                    pe.wait_ge(t_free[r % 2], r // 2 + dr * i)

            def transpose_x(l, t):
                if l == 0:
                    pe.wait_ge(const_in, 16)
                    pe.wait_ge(x_in[t], 16)
                for h in range(2):
                    r = TR_X[l][0] + 2 * t + h
                    if l > 0:
                        pe.wait_ge(x_ready, 4 * (l - 1) + 2 * t + h + 1)
                    begin_tr(r)
                    for k in range(4):
                        last = pe.transpose(TR[r % 2][:, P * k:P * k + P],
                                            x[:, t, P * (4 * h + k):P * (4 * h + k) + P], ident[:, :])
                    last.then_inc(t_done, 1)

            def split_x(l, t, h):
                r = TR_X[l][0] + 2 * t + h
                pe.wait_ge(t_free[r % 2], r // 2 + 1)

            def transpose_g(f, b, i=0):
                r = TR_FFN[f][0] + b
                begin_tr(r, i, 1)
                for t in range(NT):
                    pe.wait_ge(u_free[t], U_FFN[f] + b + 1 + 2 * i)
                for j in range(2):
                    for t in range(NT):
                        last = pe.transpose(TR[r % 2][:, 256 * j + P * t:256 * j + P * t + P],
                                            sil[:, t, P * j:P * j + P], ident[:, :])
                last.then_inc(t_done, 1)

            def ffn(f, l, extra=None):
                n, u = CHUNK_FFN[f], U_FFN[f]
                in_pair(n, u, l=l)
                with pe.Fori(0, (NB_FFN - 1) // 2) as i:
                    for b in (1, 2):
                        in_pair(n + 2 * b, u + b, i, 2, between=lambda: transpose_g(f, b - 1, i))
                n += 2 * NB_FFN
                def gt_ready(b):
                    r = TR_FFN[f][0] + b
                    pe.wait_ge(t_free[r % 2], r // 2 + 1)
                gt_ready(NB_FFN - 3)
                gt_ready(NB_FFN - 2)
                out_chunks([n], 0, KF - 1, between=lambda: transpose_g(f, NB_FFN - 1))
                for p in range(5):
                    if p == 4:
                        gt_ready(NB_FFN - 1)
                    out_chunks([n + 1 + 2 * p, n + 2 + 2 * p], 2 + 4 * p, KF - 1)
                    if extra:
                        extra(p)

            def transpose_b(p):
                if p == 0:
                    pe.wait_ge(bz_ready, 1)
                if p == 4:
                    return
                for kt in (2 * p, 2 * p + 1):
                    r = TR_BT[0] + kt
                    begin_tr(r)
                    for m in range(4):
                        last = pe.transpose(TR[r % 2][:, P * m:P * m + P],
                                            bz[:, m, 4 * kt:4 * kt + 4, :].rearrange("p a b -> p (a b)"),
                                            ident[:, :])
                    last.then_inc(t_done, 1)
                if p < 3:
                    return
                r = TR_BT[0] + KD
                begin_tr(r)
                pe.wait_ge(p_ca, 1)
                for pair in range(PAIRS):
                    i, kt = pair % 4, pair // 4
                    for ri in range(2):
                        last = pe.matmul(TR[r % 2][32 * i:32 * i + 32, 16 * kt:16 * kt + 16],
                                         bz[:, 2 + ri, pair, :], c_cmp[:, ri, pair, :],
                                         start=ri == 0, stop=ri == 1)
                last.then_inc(t_done, 1)

            ffn(0, 0, extra=transpose_b)

            def transpose_qk(b, t):
                r = TR_QK[0] + 2 * b + t
                begin_tr(r)
                pe.wait_ge(rot_done, 2 * b + t + 1)
                for m in range(4):
                    last = pe.transpose(TR[r % 2][:, P * m:P * m + P], rot[:, m // 2, m % 2, :], ident[:, :])
                last.then_inc(t_done, 1)

            def scores(h):
                if h == 0:
                    for r in (TR_QK[0] + 6, TR_QK[0] + 7):
                        pe.wait_ge(t_free[r % 2], r // 2 + 1)
                else:
                    pe.wait_ge(sc_masked, h)
                for j, cols in ((0, slice(0, 256)), (1, slice(128, 256))):
                    o = bank[0][:, 0:256] if j == 0 else bank[0][:, 256:384]
                    for d in range(2):
                        last = pe.matmul(o, kt_[:, 2 * h + d, P * j:P * j + P], qt[:, 2 * h + d, cols],
                                         start=d == 0, stop=d == 1)
                last.then_inc(sc_done, 1)

            def o_bank(h, t):
                return U[t][:, :] if h == HEADS - 1 else bank[1 + t]

            def attend(h):
                pe.wait_ge(sc_masked, h + 1)
                for t in range(NT):
                    pe.wait_ge(u_free[t], U_RET + 4 + 2 * h + 1)
                if h == HEADS - 1:
                    for t in range(NT):
                        pe.wait_ge(u_free[t], U_LAST_HEAD)
                elif h >= 1:
                    pe.wait_ge(o_read, 2 * h)
                pe.matmul(o_bank(h, 0), s_sb[:, 0, :], v_sb[:, 0, :], start=True, stop=True).then_inc(o_done, 1)
                pe.matmul(o_bank(h, 1), s_sb[:, 1, :], v_sb[:, 0, :], start=True, stop=False)
                pe.matmul(o_bank(h, 1), s_sb[:, 2, :], v_sb[:, 1, :], start=False, stop=True).then_inc(o_done, 1)

            def transpose_head(h):
                for t in range(NT):
                    r = TR_HEAD[0] + 2 * h + t
                    begin_tr(r)
                    pe.wait_ge(og_done, 2 * h + t + 1)
                    for m in range(4):
                        last = pe.transpose(TR[r % 2][:, P * m:P * m + P], og[:, t, P * m:P * m + P], ident[:, :])
                    last.then_inc(t_done, 1)

            for b in range(NB_RET):
                def between_tiles():
                    if 1 <= b <= 4:
                        transpose_qk(b - 1, 1)
                    if b == 5:
                        scores(0)
                    if b >= 6 and b % 2 == 0:
                        attend(b // 2 - 3)
                    if b >= 7 and b % 2 == 1:
                        scores((b - 5) // 2)
                        transpose_head((b - 7) // 2)

                in_pair(CHUNK_RET_IN + 2 * b, U_RET + b, between=between_tiles, l=1 if b == 0 else None)
                if b < 4:
                    transpose_qk(b, 0)
            attend(HEADS - 1)
            for h in range(HEADS):
                if h == 1:
                    transpose_head(HEADS - 1)
                for t in range(NT):
                    r = TR_HEAD[0] + 2 * h + t
                    pe.wait_ge(t_free[r % 2], r // 2 + 1)
                if h == 0:
                    pe.wait_ge(o_read, 2 * (HEADS - 1))
                    pe.wait_ge(sc_masked, HEADS)
                out_chunks([CHUNK_RET_OUT + 2 * h, CHUNK_RET_OUT + 2 * h + 1], 4 * h, 4 * HEADS - 1)
            ffn(1, 2)

            ffn(2, 3)

            def columns_pair(n, u, middle=None):
                for m in range(4):
                    h = m // 2
                    if m == 2 and middle:
                        middle()
                    if m % 2 == 0:
                        pe.wait_ge(u_free[h], u)
                    for c in range(2):
                        if m == 0:
                            pe.wait_ge(w_lo, n + c + 1)
                        for k in range(4):
                            kd = 4 * c + k
                            at = (n + c) % RING
                            cols = slice(512 * k + P * m, 512 * k + P * m + P)
                            last = product(U[h][:, 256 * (m % 2):256 * (m % 2) + 256],
                                           w_hi_sb[:, at, cols], w_lo_sb[:, at, cols],
                                           xt_hi[:, kd, :], xt_lo[:, kd, :], kd == 0, kd == KD - 1)
                    if m % 2 == 1:
                        last.then_inc(u_done[h], 1)

            for t in range(NT):
                transpose_x(4, t)
            for t in range(NT):
                for h in range(2):
                    split_x(4, t, h)
            def b_u(kt):
                re_im = bank[2 * (kt % 2):2 * (kt % 2) + 2]
                pe.wait_ge(bt_in[kt % 2], 16 * (kt // 2 + 1))
                pe.wait_ge(upad_ready, kt + 1)
                if kt >= 2:
                    pe.wait_ge(bu_read, kt - 1)
                for ri in range(2):
                    for q in range(4):
                        o = re_im[ri][:, NC * q:NC * q + NC]
                        pe.matmul(o, bt[:, kt % 2, ri, :], upad[:, q, 0:NC], start=True, stop=False)
                        last = pe.matmul(o, bt[:, kt % 2, 2 + ri, :], upad[:, q, NC:T], start=False, stop=True)
                last.then_inc(bu_done, 1)

            def c_h(kt):
                y = U[kt % 2]
                if kt >= 2:
                    pe.wait_ge(y_in, kt - 1)
                else:
                    pe.wait_ge(u_free[kt], U_S5_IN + 2)
                pe.wait_ge(ct_in[kt % 2], 80 * (kt // 2 + 1))
                pe.wait_ge(tm_ready, kt + 1)
                pe.matmul(y[:, 0:NC], tm, ut[:, kt, 0:NC], start=True, stop=False, skip_group_check=True)
                for ri, ready in enumerate((h_re, h_im)):
                    pe.wait_ge(ready, kt + 1)
                    for i in range(4):
                        last = pe.matmul(y[32 * i:32 * i + 32, 0:NC], ct[:, kt % 2, 2 + ri, 32 * i:32 * i + 32],
                                         h_sb[:, ri, i, 0:NC], start=False, stop=ri == 1, skip_group_check=True)
                for i in range(4):
                    for ri in range(2):
                        last = pe.matmul(y[32 * i:32 * i + 32, NC:T], ct[:, kt % 2, ri, 32 * i:32 * i + 32],
                                         h_sb[:, ri, i, 1:NC + 1], start=ri == 0, stop=ri == 1,
                                         skip_group_check=True)
                last.then_inc(y_done, 1)

            columns_pair(CHUNK_S5_IN, U_S5_IN)
            columns_pair(CHUNK_S5_IN + 2, U_S5_IN + 1, middle=lambda: b_u(0))
            b_u(1)
            b_u(2)
            def glu(b, kds):
                for kd in kds:
                    n = CHUNK_GLU + 2 * (kd // 4) + b
                    if kd % 4 == 0:
                        pe.wait_ge(w_lo, n + 1)
                        if kd == 0:
                            pe.wait_ge(bu_read, KD - 1 + b)
                    pe.wait_ge(act_split, kd + 1)
                    at = n % RING
                    for m in range(4):
                        cols = slice(512 * (kd % 4) + P * m, 512 * (kd % 4) + P * m + P)
                        last = product(bank[2 * b + m // 2][:, 256 * (m % 2):256 * (m % 2) + 256],
                                       w_hi_sb[:, at, cols], w_lo_sb[:, at, cols],
                                       xt_hi[:, kd, :], xt_lo[:, kd, :], kd == 0 and m % 2 == 0, kd == KD - 1,
                                       skip_group_check=True)
                        if kd == KD - 1 and m % 2 == 1:
                            last.then_inc(glu_done, 1)
                    if kd == 3:
                        last.then_inc(glu_used, 1)

            for kt in range(KD):
                c_h(kt)
                if kt + 3 < KD:
                    b_u(kt + 3)
                if kt >= KD - 3 and kt < KD - 1:
                    glu(kt - (KD - 3), range(4))
            for b in range(2):
                glu(b, range(4, KD - 1))
            for b in range(2):
                glu(b, (KD - 1,))
            for p in range(2):
                pe.wait_ge(z_split, 2 * (p + 1))
                out_chunks([CHUNK_S5_OUT + 2 * p, CHUNK_S5_OUT + 2 * p + 1], 4 * p, KD - 1,
                           between=(lambda: pe.wait_ge(sig_done, 4)) if p == 0 else None)
            ffn(3, 5)

        @block.scalar
        def _(act):
            def prep(n, i=0, step=0, used=True):
                if n >= N_CHUNKS:
                    return
                slot = n % RING
                act.wait_ge(raw_in[slot], 16 * (n // RING + 1) + 4 * step * i)
                if not used:
                    act.wait_ge(out_used, n_out_used(n - RING))
                act.activation(w_hi_sb[:, slot, :], raw[:, slot, :], ACT.Copy).then_inc(w_hi, 1)

            def split_x(l, t):
                for h in range(2):
                    r = TR_X[l][0] + 2 * t + h
                    act.wait_ge(t_done, r + 1)
                    act.activation(xt_hi[:, 4 * h:4 * h + 4, P * t:P * t + P],
                                   TR[r % 2][:, :].rearrange("p (k n) -> p k n", k=4), ACT.Copy)\
                       .then_inc(t_hi, 1)

            def scale_x(l, t):
                act.activation(x[:, t, :], x[:, t, :], ACT.Copy, scale=ALPHA).then_inc(x_scaled, 1)

            def load_gb(norm):
                if norm > 0:
                    act.wait_ge(x_ready, 4 * norm)
                for j, name in enumerate(("ln_g", "ln_b")):
                    act.dma_start(gb[:, j, :], ins[name][norm:norm + 1, :].to_broadcast([P, D]))\
                       .then_inc(gb_in, 16)

            def open_stage(l, n, norm):
                if l == 0:
                    s5_exp_dt()
                split_x(l, 0)
                if l == 0:
                    prep(0)
                    prep(1)
                scale_x(l, 0)
                if l > 0:
                    prep(n + 2, used=False)
                split_x(l, 1)
                scale_x(l, 1)
                if l == 0:
                    prep(n + 2)
                prep(n + 3)
                if norm is not None:
                    load_gb(norm)

            def silu_half(u, t, i=0):
                act.wait_ge(u_done[t], n_u_done(u) + 2 * i)
                act.activation(sil[:, t, :], U[t][:, 0:BLK], ACT.Silu).then_inc(sil_done[t], 1)

            def split_g(f, b, i=0):
                r = TR_FFN[f][0] + b
                act.wait_ge(t_done, r + 1 + 2 * i)
                act.activation(gt_part(gt_hi, b, i), TR[r % 2][:, :], ACT.Copy).then_inc(t_hi, 1)

            def ffn(f, l, norm, extra=None, late=None):
                n, u = CHUNK_FFN[f], U_FFN[f]
                open_stage(l, n, norm)
                if extra:
                    extra()
                silu_half(u, 0)
                with act.Fori(0, (NB_FFN - 1) // 2) as i:
                    for b in (1, 2):
                        silu_half(u + b - 1, 1, i)
                        prep(n + 2 * b + 2, i, 4)
                        prep(n + 2 * b + 3, i, 4)
                        split_g(f, b - 1, i)
                        silu_half(u + b, 0, i)
                n += 2 * NB_FFN
                silu_half(u + NB_FFN - 1, 1)
                prep(n + 2)
                prep(n + 3)
                split_g(f, NB_FFN - 1)
                prep(n + 4, used=False)
                for p in range(4):
                    prep(n + 5 + 2 * p, used=False)
                    prep(n + 6 + 2 * p, used=False)
                    if late:
                        late(p)

            def s5_exp_dt():
                act.wait_ge(small_in, 16)
                act.activation(small[:, 3, :], small[:, 2, :], ACT.Exp).then_inc(p_dt, 1)

            def s5_trig():
                act.wait_ge(p_theta, 1)
                act.activation(small[:, 11, :], small[:, 4, :], ACT.Exp)
                act.activation(small[:, 12, :], small[:, 10, :], ACT.Sin)
                act.activation(small[:, 13, :], small[:, 10, :], ACT.Sin, scale=0.5).then_inc(p_trig, 1)

            def store_bt(p):
                for kt in (2 * p, 2 * p + 1):
                    r, b = TR_BT[0] + kt, kt % 2
                    act.wait_ge(t_done, r + 1)
                    if kt >= 2:
                        act.wait_ge(bt_out_free[b], 16 * (kt // 2))
                    act.activation(bt_out[:, b, :], TR[r % 2][:, :], ACT.Copy).then_inc(t_free[r % 2], 1)
                    act.wait_ge(t_free[r % 2], r // 2 + 1)
                    act.dma_start(bt_dram[kt], bt_out[:, b, :]).then_inc(bt_out_free[b], 16)
                if p < 3:
                    return
                r = TR_BT[0] + KD
                act.wait_ge(t_done, r + 1)
                act.activation(s5_t.rearrange("p k n -> p (k n)"), TR[r % 2][:, 0:16 * KD], ACT.Copy)\
                   .then_inc(t_free[r % 2], 1)
                act.wait_ge(p_ca, 2)
                act.dma_start(ca_dram.rearrange("p a k n -> p (a k n)"),
                              ca.rearrange("p a b n -> p (a b n)")).then_inc(ca_stored, 16)

            def ret_constants():
                for b in range(2):
                    act.wait_ge(bt_out_free[b], 16 * 4)
                act.wait_ge(ca_stored, 16)
                act.wait_ge(t_free[(TR_BT[0] + KD) % 2], (TR_BT[0] + KD) // 2 + 1)
                act.dma_start(cossin.rearrange("p a t n -> p (a t n)"), ins["cossin"]).then_inc(ret_const_in, 16)
                act.dma_start(masks.rearrange("p h a n -> p (h a n)"), ins["masks"]).then_inc(ret_const_in, 16)

            ffn(0, 0, 0, extra=s5_trig, late=store_bt)
            ret_constants()

            def move_qk(b, t):
                r = TR_QK[0] + 2 * b + t
                act.wait_ge(t_done, r + 1)
                dst = qt if b < 2 else kt_
                j = 4 * (b % 2)
                act.activation(dst[:, j:j + 4, P * t:P * t + P],
                               TR[r % 2][:, :].rearrange("p (k n) -> p k n", k=4), ACT.Copy)\
                   .then_inc(t_free[r % 2], 1)

            def take_vg(b, t):
                if b < 4:
                    return
                h = (b - 4) // 2
                act.wait_ge(u_done[t], n_u_done(U_RET + b))
                if b % 2 == 0:
                    if h >= 1:
                        act.wait_ge(o_done, 2 * h)
                    act.activation(v_sb[:, t, :], U[t][:, :], ACT.Copy).then_inc(u_free[t], 1)
                else:
                    if h >= 1:
                        act.wait_ge(og_done, 2 * (h - 1) + t + 1)
                    act.activation(g_sb[:, t, :], U[t][:, :], ACT.Silu).then_inc(u_free[t], 1)

            def split_head(h):
                for t in range(NT):
                    r = TR_HEAD[0] + 2 * h + t
                    act.wait_ge(t_done, r + 1)
                    act.activation(gt_hi[:, 4 * h:4 * h + 4, P * t:P * t + P],
                                   TR[r % 2][:, :].rearrange("p (k n) -> p k n", k=4), ACT.Copy)\
                       .then_inc(t_hi, 1)

            n = CHUNK_RET_IN
            open_stage(1, n, 1)
            take_vg(0, 0)
            for b in range(1, NB_RET):
                if b <= 4:
                    move_qk(b - 1, 0)
                take_vg(b - 1, 1)
                if b < 5:
                    act.wait_ge(u_done[1], n_u_done(U_RET + b - 1))
                prep(n + 2 * b + 2)
                prep(n + 2 * b + 3)
                if b <= 4:
                    move_qk(b - 1, 1)
                if b >= 7 and b % 2 == 1:
                    split_head((b - 7) // 2)
                take_vg(b, 0)
            take_vg(NB_RET - 1, 1)
            n = CHUNK_RET_OUT
            prep(n + 2)
            prep(n + 3)
            split_head(HEADS - 1)
            for m in range(4, 10):
                prep(n + m, used=False)
            ffn(1, 2, 2)

            ffn(2, 3, 3)
            n = CHUNK_S5_IN

            def split_by_parity(l, t):
                for h in range(2):
                    r = TR_X[l][0] + 2 * t + h
                    act.wait_ge(t_done, r + 1)
                    act.activation(by_parity(xt_hi, h, t),
                                   TR[r % 2][:, :].rearrange("p (k c a) -> p k a c", k=4, a=2), ACT.Copy)\
                       .then_inc(t_hi, 1)

            split_by_parity(4, 0)
            prep(n + 2, used=False)
            split_by_parity(4, 1)
            for t in range(NT):
                scale_x(4, t)
            prep(n + 3)

            def take_u(b, h):
                act.wait_ge(u_done[h], n_u_done(U_S5_IN + b))
                k = 4 * b + 2 * h
                act.activation(ut[:, k:k + 2, :].rearrange("p k n -> p (k n)"), U[h][:, :], ACT.Copy)\
                   .then_inc(u_free[h], 1)

            def pad_u(kt):
                if kt == 0:
                    act.wait_ge(u_free[0], U_S5_IN + 1)
                    act.wait_ge(zeroed, 1)
                else:
                    if kt == 2:
                        act.wait_ge(u_free[1], U_S5_IN + 2)
                    act.wait_ge(bu_done, kt)
                for i in range(4):
                    rows = slice(32 * i, 32 * i + 32)
                    last = act.activation(upad[rows, i, :], ut[rows, kt, :], ACT.Copy)
                last.then_inc(upad_ready, 1)

            take_u(0, 0)
            pad_u(0)
            take_u(0, 1)
            prep(n + 4)
            prep(n + 5)
            take_u(1, 0)
            pad_u(1)
            take_u(1, 1)
            pad_u(2)
            prep(n + 6)
            prep(n + 7)

            def gelu_y(kt):
                act.wait_ge(y_in, kt + 1)
                act.activation(ut[:, kt, :], sil[:, kt % 2, :], ACT.Gelu_apprx_tanh).then_inc(act_gelu, 1)
                act.wait_ge(act_gelu, kt + 1)
                act.activation(xt_hi[:, kt, :], ut[:, kt, :], ACT.Copy).then_inc(act_hi, 1)

            pad_u(3)
            for kt in range(KD):
                if kt + 4 < KD:
                    pad_u(kt + 4)
                gelu_y(kt)
            act.wait_ge(h_im, KD)
            act.wait_ge(h_re, KD)
            load_gb(4)
            n = CHUNK_GLU + 4
            for b in range(2):
                act.wait_ge(glu_used, b + 1)
                prep(n + b)

            def sigmoid(j):
                act.wait_ge(glu_done, j + 1)
                act.activation(rotin[:, j, :], bank[j], ACT.Sigmoid).then_inc(sig_done, 1)

            def split_z(j):
                act.wait_ge(z_done, j + 1)
                act.activation(from_parity(gt_hi, 2 * j),
                               rotin[:, j, :].rearrange("p (k a c) -> p k a c", k=2, a=2), ACT.Copy)\
                   .then_inc(z_hi, 1)

            for j in range(4):
                sigmoid(j)
                if j == 2:
                    prep(n + 2)
                split_z(j)
            prep(n + 3)
            n = CHUNK_S5_OUT
            for m in range(4, 6):
                prep(n + m, used=False)
            ffn(3, 5, 5)

        @block.vector
        def _(dve):
            chain = [0]
            n_var = [0]

            def link(ins_):
                chain[0] += 1
                ins_.then_inc(dve_chain, 1)
                dve.wait_ge(dve_chain, chain[0])

            def prep(n, i=0, step=0):
                if n >= N_CHUNKS:
                    return
                slot = n % RING
                dve.wait_ge(w_hi, n + 1 + step * i)
                dve.tensor_tensor(w_lo_sb[:, slot, :], raw[:, slot, :], w_hi_sb[:, slot, :].bitcast(F32),
                                  ALU.subtract).then_inc(w_lo, 1)

            def split(dst, hi, r, z, i=0):
                dve.wait_ge(t_hi, z + 1 + 2 * i)
                src = TR[r % 2][:, :]
                if len(dst.shape) == 3:
                    src = src.rearrange("p (k n) -> p k n", k=4)
                dve.tensor_tensor(dst, src, hi.bitcast(F32), ALU.subtract).then_inc(t_free[r % 2], 1)

            def split_x(l, t):
                for h in range(2):
                    r, z = (v + 2 * t + h for v in TR_X[l])
                    split(xt_lo[:, 4 * h:4 * h + 4, P * t:P * t + P],
                          xt_hi[:, 4 * h:4 * h + 4, P * t:P * t + P], r, z)

            def norm(k, t, factor):
                st = stats[:, t, :]
                halves = [slice(512 * h, 512 * h + 512) for h in range(2)]
                dve.wait_ge(x_scaled, 2 * k + t + 1)
                for h, cols in enumerate(halves):
                    dve.wait_ge(acc_done, 4 * k + 2 * t + h + 1)
                    link(dve.scalar_tensor_tensor(out=x[:, t, cols], in0=acc[t][:, cols], scalar=factor,
                                                  in1=x[:, t, cols], op0=ALU.mult, op1=ALU.add))
                    last = dve.bn_stats(st[:, 6 * h:6 * h + 6], x[:, t, cols])
                link(last)
                link(dve.bn_aggr(st[:, 12:14], st[:, 0:12]))
                n_var[0] += 1
                dve.tensor_scalar(st[:, 14:15], st[:, 13:14], LN_EPS, None, ALU.add).then_inc(var_ready, 1)
                dve.wait_ge(gb_in, 32 * (k + 1))
                for h, cols in enumerate(halves):
                    link(dve.scalar_tensor_tensor(out=x[:, t, cols], in0=x[:, t, cols], scalar=st[:, 12:13],
                                                  in1=gb[:, 0, cols], op0=ALU.subtract, op1=ALU.mult))
                    if h == 0:
                        dve.wait_ge(rstd_ready, n_var[0])
                    dve.scalar_tensor_tensor(out=x[:, t, cols], in0=x[:, t, cols], scalar=st[:, 15:16],
                                             in1=gb[:, 1, cols], op0=ALU.mult, op1=ALU.add)\
                       .then_inc(x_ready, 1)

            def open_stage(l, n, factor):
                for t in range(NT):
                    if l > 0:
                        norm(l - 1, t, factor)
                    split_x(l, t)
                    if l == 0 and t == 0:
                        prep(0)
                        prep(1)
                prep(n + 2)
                prep(n + 3)

            def gate(u, t, i=0):
                dve.wait_ge(sil_done[t], n_sil(u) + 2 * i)
                dve.tensor_tensor(sil[:, t, :], sil[:, t, :], U[t][:, BLK:2 * BLK], ALU.mult)\
                   .then_inc(u_free[t], 1)

            def split_g(f, b, i=0):
                r, z = (v + b for v in TR_FFN[f])
                split(gt_part(gt_lo, b, i), gt_part(gt_hi, b, i), r, z, i)

            def ffn(f, l, factor):
                n, u = CHUNK_FFN[f], U_FFN[f]
                open_stage(l, n, factor)
                gate(u, 0)
                with dve.Fori(0, (NB_FFN - 1) // 2) as i:
                    for b in (1, 2):
                        gate(u + b - 1, 1, i)
                        prep(n + 2 * b + 2, i, 4)
                        prep(n + 2 * b + 3, i, 4)
                        split_g(f, b - 1, i)
                        gate(u + b, 0, i)
                n += 2 * NB_FFN
                gate(u + NB_FFN - 1, 1)
                prep(n + 2)
                prep(n + 3)
                split_g(f, NB_FFN - 1)
                for m in range(4, 13):
                    prep(n + m)

            def tt(out_, a, b, op):
                return dve.tensor_tensor(out_, a, b, op)

            are, aim, dt = small[:, 0, :], small[:, 1, :], small[:, 3, :]

            def s5_theta():
                dve.wait_ge(small_in, 16)
                tt(small[:, 18, :], are, are, ALU.mult)
                link(tt(small[:, 19, :], aim, aim, ALU.mult))
                link(tt(small[:, 17, :], small[:, 18, :], small[:, 19, :], ALU.add))
                link(dve.reciprocal(small[:, 17, :], small[:, 17, :]))
                dve.wait_ge(p_dt, 1)
                tt(small[:, 4, :], dt, are, ALU.mult)
                link(tt(small[:, 5, :], dt, aim, ALU.mult))
                link(dve.tensor_scalar(small[:, 6, :], small[:, 5, :], 1.0 / TURN, ROUNDER, ALU.mult, ALU.add))
                link(dve.tensor_scalar(small[:, 7, :], small[:, 6, :], ROUNDER, None, ALU.subtract))
                src = small[:, 5, :]
                for j, part in enumerate(TURN_PARTS):
                    link(dve.scalar_tensor_tensor(out=small[:, 8 + j, :], in0=small[:, 7, :], scalar=-part,
                                                  in1=src, op0=ALU.mult, op1=ALU.add))
                    src = small[:, 8 + j, :]
                dve.tensor_scalar(small[:, 10, :], small[:, 10, :], -PI_DOWN, PI_DOWN, ALU.max, ALU.min)\
                   .then_inc(p_theta, 1)

            s5_theta()
            ffn(0, 0, 0.5)

            def rotate(b, t):
                if b >= 4:
                    return
                dve.wait_ge(u_done[t], n_u_done(U_RET + b))
                src = U[t][:, :].rearrange("p (h a n) -> p h a n", h=2, a=2)
                cos, sin = (cossin[:, j, t, :].unsqueeze(1).to_broadcast([P, 2, P]) for j in range(2))
                if b == 0 and t == 0:
                    dve.wait_ge(ret_const_in, 32)
                if b or t:
                    dve.wait_ge(rot_done, 2 * b + t)
                dve.tensor_tensor(rtmp[:, 0], src[:, :, 0], cos, ALU.mult)
                dve.tensor_tensor(rtmp[:, 1], src[:, :, 1], sin, ALU.mult)
                dve.tensor_tensor(rtmp[:, 2], src[:, :, 0], sin, ALU.mult)
                dve.tensor_tensor(rtmp[:, 3], src[:, :, 1], cos, ALU.mult).then_inc(u_free[t], 1)
                dve.wait_ge(u_free[t], U_RET + b + 1)
                if b or t:
                    dve.wait_ge(t_done, TR_QK[0] + 2 * b + t)
                dve.tensor_tensor(rot[:, :, 0, :], rtmp[:, 0], rtmp[:, 1], ALU.subtract)
                dve.tensor_tensor(rot[:, :, 1, :], rtmp[:, 2], rtmp[:, 3], ALU.add).then_inc(rot_done, 1)

            def mask_scores(h):
                dve.wait_ge(sc_done, h + 1)
                if h >= 1:
                    dve.wait_ge(o_done, 2 * h)
                dve.tensor_tensor(s_sb[:, 0:2, :].rearrange("p a n -> p (a n)"), bank[0][:, 0:256],
                                  masks[:, h].rearrange("p a n -> p (a n)"), ALU.mult)
                dve.tensor_tensor(s_sb[:, 2, :], bank[0][:, 256:384], masks[:, h, 0, :], ALU.mult)\
                   .then_inc(sc_masked, 1)

            def norm_head(h, t):
                o = U[t][:, :] if h == HEADS - 1 else bank[1 + t]
                st = stats[:, t, :]
                dve.wait_ge(o_done, 2 * h + t + 1)
                if h >= 1:
                    dve.wait_ge(t_done, TR_HEAD[0] + 2 * (h - 1) + t + 1)
                link(dve.bn_stats(st[:, 0:6], o))
                link(dve.bn_aggr(st[:, 12:14], st[:, 0:6]))
                n_var[0] += 1
                dve.tensor_scalar(st[:, 14:15], st[:, 13:14], GN_EPS, None, ALU.add).then_inc(var_ready, 1)
                dve.wait_ge(u_free[t], U_RET + 5 + 2 * h + 1)
                read = u_free[t] if h == HEADS - 1 else o_read
                dve.scalar_tensor_tensor(out=og[:, t, :], in0=o, scalar=st[:, 12:13], in1=g_sb[:, t, :],
                                         op0=ALU.subtract, op1=ALU.mult).then_inc(read, 1)
                dve.wait_ge(read, U_LAST_HEAD + 1 if h == HEADS - 1 else 2 * h + t + 1)
                dve.wait_ge(rstd_ready, n_var[0])
                dve.tensor_scalar(og[:, t, :], og[:, t, :], st[:, 15:16], None, ALU.mult).then_inc(og_done, 1)

            def split_head(h):
                for t in range(NT):
                    r, z = (v + 2 * h + t for v in TR_HEAD)
                    split(gt_lo[:, 4 * h:4 * h + 4, P * t:P * t + P],
                          gt_hi[:, 4 * h:4 * h + 4, P * t:P * t + P], r, z)

            n = CHUNK_RET_IN
            open_stage(1, n, 0.5)
            rotate(0, 0)
            for b in range(1, NB_RET):
                rotate(b - 1, 1)
                prep(n + 2 * b + 2)
                prep(n + 2 * b + 3)
                if b >= 5 and b % 2 == 1:
                    mask_scores((b - 5) // 2)
                if b >= 7 and b % 2 == 1:
                    split_head((b - 7) // 2)
                if b >= 6 and b % 2 == 0:
                    for t in range(NT):
                        norm_head(b // 2 - 3, t)
                rotate(b, 0)
            n = CHUNK_RET_OUT
            prep(n + 2)
            prep(n + 3)
            for t in range(NT):
                norm_head(HEADS - 1, t)
            split_head(HEADS - 1)
            for m in range(4, 10):
                prep(n + m)
            ffn(1, 2, 1.0)

            ffn(2, 3, 0.5)
            n = CHUNK_S5_IN
            for t in range(NT):
                norm(3, t, 0.5)
                for h in range(2):
                    r, z = (v + 2 * t + h for v in TR_X[4])
                    dve.wait_ge(t_hi, z + 1)
                    tt(by_parity(xt_lo, h, t), TR[r % 2][:, :].rearrange("p (k c a) -> p k a c", k=4, a=2),
                       by_parity(xt_hi, h, t).bitcast(F32), ALU.subtract).then_inc(t_free[r % 2], 1)
            for m in range(2, 6):
                prep(n + m)

            def turn_in(kt):
                cos, nsin = (tab[:, kt % 2, j, :] for j in range(2))
                re, im = bank[2 * (kt % 2)], bank[2 * (kt % 2) + 1]
                dve.wait_ge(tab_in[kt % 2], 16 * (kt // 2 + 1))
                dve.wait_ge(bu_done, kt + 1)
                if kt >= 1:
                    dve.wait_ge(g_im, kt)
                for m, (a, w) in enumerate(((re, cos), (im, nsin), (im, cos), (re, nsin))):
                    last = tt(rotin[:, m, :], a, w, ALU.mult)
                last.then_inc(bu_read, 1)

            def recur(kt):
                dve.wait_ge(bu_read, kt + 1)
                tt(rotin[:, 0, :], rotin[:, 0, :], rotin[:, 1, :], ALU.subtract)
                link(tt(rotin[:, 2, :], rotin[:, 2, :], rotin[:, 3, :], ALU.add))
                for j, (done, used) in enumerate(((g_re, prod_done[3]), (g_im, prod_done[2]))):
                    if kt >= 1:
                        dve.wait_ge(used, kt)
                    for q in range(4):
                        pair, at = 4 * kt + q, slice(NC * q, NC * q + NC)
                        last = dve.tensor_tensor_scan(
                            gs[:, j, at], s5_abar[:, 2, pair:pair + 1].to_broadcast([P, NC]),
                            rotin[:, 2 * j, at], 0.0, ALU.mult, ALU.add)
                    last.then_inc(done, 1)

            def turn_out_re(kt):
                dve.wait_ge(prod_done[1], kt + 1)
                if kt >= 1:
                    dve.wait_ge(y_done, kt)
                tt(h_sb[:, 0, :, 1:NC + 1], *(prod[:, m, :].rearrange("p (q n) -> p q n", q=4) for m in (0, 1)),
                   ALU.add).then_inc(h_re, 1)

            def add_du(kt):
                dve.wait_ge(y_done, kt + 1)
                if kt >= 2:
                    dve.wait_ge(act_gelu, kt - 1)
                dve.scalar_tensor_tensor(out=sil[:, kt % 2, :], in0=ut[:, kt, :], scalar=s5_d[:, kt:kt + 1],
                                         in1=U[kt % 2][:, 0:256], op0=ALU.mult, op1=ALU.add)\
                   .then_inc(y_in, 1)

            def split_act(kt):
                dve.wait_ge(act_hi, kt + 1)
                tt(xt_lo[:, kt, :], ut[:, kt, :], xt_hi[:, kt, :].bitcast(F32), ALU.subtract)\
                    .then_inc(act_split, 1)

            for kt in range(KD):
                turn_in(kt)
                if kt >= 1:
                    turn_out_re(kt - 1)
                recur(kt)
                if kt >= KD - 2:
                    prep(n + kt)
                if kt >= 2:
                    add_du(kt - 2)
                if kt >= 3:
                    split_act(kt - 3)
            turn_out_re(KD - 1)
            for kt in (KD - 2, KD - 1):
                add_du(kt)
                split_act(kt - 1)
            split_act(KD - 1)
            for b in range(2):
                prep(n + 8 + b)

            for j in range(4):
                z = rotin[:, j, :]
                dve.wait_ge(sig_done, j + 1)
                tt(z, ut[:, 2 * j:2 * j + 2, :].rearrange("p k n -> p (k n)"), z, ALU.mult).then_inc(z_done, 1)
                if j == 2:
                    prep(n + 10)
                dve.wait_ge(z_hi, j + 1)
                tt(from_parity(gt_lo, 2 * j), z.rearrange("p (k a c) -> p k a c", k=2, a=2),
                   from_parity(gt_hi, 2 * j).bitcast(F32), ALU.subtract).then_inc(z_split, 1)
            prep(n + 11)
            n = CHUNK_S5_OUT
            for m in range(4, 6):
                prep(n + m)
            ffn(3, 5, 1.0)
            for t in range(NT):
                norm(5, t, 0.5)

        @block.gpsimd
        def _(pool):
            def tt(out_, a, b, op):
                return pool.tensor_tensor(out_, a, b, op)

            chain = [0]

            def link(ins_):
                chain[0] += 1
                ins_.then_inc(pool_chain, 1)
                pool.wait_ge(pool_chain, chain[0])

            n_var = [0]

            def rsqrt(norms):
                for _ in range(norms):
                    for t in range(NT):
                        n_var[0] += 1
                        pool.wait_ge(var_ready, n_var[0])
                        tt(stats[:, t, 15:16], stats[:, t, 14:15], minus_half[:, :], ALU.pow)\
                            .then_inc(rstd_ready, 1)

            are, aim = small[:, 0, :], small[:, 1, :]

            def s5_factors():
                s = lambda j: small[:, j, :]
                pool.wait_ge(p_trig, 1)
                mag, sin, sin_half = s(11), s(12), s(13)
                cos, am1, den, t0, t1 = s(14), s(15), s(17), s(18), s(19)
                ar, ai = s5_abar[:, 0, :], s5_abar[:, 1, :]
                link(tt(t0, sin_half, sin_half, ALU.mult))
                link(pool.tensor_scalar(cos, t0, -2.0, 1.0, ALU.mult, ALU.add))
                tt(ai, mag, sin, ALU.mult)
                link(tt(ar, mag, cos, ALU.mult))
                link(pool.tensor_scalar(am1, ar, 1.0, None, ALU.subtract))
                tt(t0, am1, are, ALU.mult)
                link(tt(t1, ai, aim, ALU.mult))
                link(tt(t0, t0, t1, ALU.add))
                link(tt(s(20), t0, den, ALU.mult))
                tt(t0, ai, are, ALU.mult)
                link(tt(t1, am1, aim, ALU.mult))
                link(tt(t0, t0, t1, ALU.subtract))
                link(tt(s(21), t0, den, ALU.mult))
                pool.tensor_copy(s5_pow[:, 0, 0, :], cos)
                link(pool.tensor_scalar(s5_pow[:, 1, 0, :], sin, -1.0, None, ALU.mult))
                for k in range(1, NPOW + 1):
                    c, ns = s5_pow[:, 0, k - 1, :], s5_pow[:, 1, k - 1, :]
                    tt(t0, c, c, ALU.mult)
                    tt(t1, ns, ns, ALU.mult)
                    link(tt(s(22), c, ns, ALU.mult))
                    tt(s5_pow[:, 0, k, :], t0, t1, ALU.subtract)
                    link(tt(s5_pow[:, 1, k, :], s(22), s(22), ALU.add))
                tt(s5_abar[:, 2, :], mag, mag, ALU.mult).then_inc(p_f, 1)

            pool.memset(minus_half[:, :], -0.5)
            pool.memset(unit[:, 0, :], 1.0)
            link(pool.memset(unit[:, 1, :], 0.0))
            link(pool.memset(bz.rearrange("p a b c -> p (a b c)"), 0.0))
            s5_factors()
            pool.wait_ge(p_f, 1)
            pool.wait_ge(b_landed, 48)

            def times(factor, a, put, ops=(ALU.subtract, ALU.add)):
                f_re, f_im = (v.unsqueeze(2).to_broadcast([P, PAIRS, 16]) for v in factor)
                for ri, other in enumerate((1, 0)):
                    tt(bprod[:, 0], f_re, a[:, ri], ALU.mult)
                    link(tt(bprod[:, 1], f_im, a[:, other], ALU.mult))
                    put(ri, bprod[:, 0], bprod[:, 1], ops[ri])

            def put_diagonal(ri, a, b, op):
                for g in range(2):
                    half = slice(64 * g, 64 * g + 64)
                    step = tt(bz[half, ri, :, 16 * g:16 * g + 16], a[half], b[half], op)
                link(step)

            abar = (s5_abar[:, 0, :], s5_abar[:, 1, :])
            times((small[:, 20, :], small[:, 21, :]), b_in,
                  lambda ri, a, b, op: link(tt(bbar[:, ri], a, b, op)))
            times(abar, bbar, put_diagonal)
            for ri in range(2):
                for g in range(2):
                    half = slice(64 * g, 64 * g + 64)
                    step = pool.tensor_copy(bz[half, 2 + ri, :, 16 * g:16 * g + 16], bbar[half, ri])
            step.then_inc(bz_ready, 1)
            pool.wait_ge(bz_ready, 1)
            zeros = unit[:, 1, 0:1].unsqueeze(2).to_broadcast([P, PAIRS, 16])
            tt(c_cmp[:, 1], zeros, c_cmp[:, 1], ALU.subtract).then_inc(p_ca, 1)
            pool.wait_ge(p_ca, 1)
            tt(bprod[:, 0], abar[0].unsqueeze(2).to_broadcast([P, PAIRS, 16]), c_cmp[:, 0], ALU.mult)
            link(tt(bprod[:, 1], abar[1].unsqueeze(2).to_broadcast([P, PAIRS, 16]), c_cmp[:, 1], ALU.mult))
            link(tt(ca[:, 0], bprod[:, 0], bprod[:, 1], ALU.add))
            tt(bprod[:, 0], abar[1].unsqueeze(2).to_broadcast([P, PAIRS, 16]), c_cmp[:, 0], ALU.mult)
            link(tt(bprod[:, 1], abar[0].unsqueeze(2).to_broadcast([P, PAIRS, 16]), c_cmp[:, 1], ALU.mult))
            tt(ca[:, 1], bprod[:, 0], bprod[:, 1], ALU.subtract).then_inc(p_ca, 1)

            rsqrt(1 + HEADS + 1)
            pool.wait_ge(x_ready, 8)
            pool.memset(ct.rearrange("p a b n -> p (a b n)"), 0.0)
            pool.memset(upad.rearrange("p q n -> p (q n)"), 0.0)
            pool.memset(h_sb[:, :, :, 0:1], 0.0).then_inc(zeroed, 1)
            per_table = 3 * NPOW
            base = chain[0]

            def build_table(b, i):
                c, ns = (tab[:, b, j, :].rearrange("p (q t) -> p q t", q=4) for j in range(2))
                at = base + per_table * b + 2 * per_table * i
                if not isinstance(i, int):
                    pool.wait_ge(tab_stored[b], 16 * i)
                one, zero = (unit[:, j, :].unsqueeze(2) for j in range(2))
                tt(c[:, :, 0:1], one, one, ALU.mult)
                tt(ns[:, :, 0:1], zero, one, ALU.mult).then_inc(pool_chain, 1)
                for k in range(NPOW):
                    m = 1 << k
                    pairs = slice(4 * b, 4 * b + 4) if isinstance(i, int) else bass.ds(8 * i + 4 * b, 4)
                    pc, pns = (s5_pow[:, j, k + 1, pairs].unsqueeze(2).to_broadcast([P, 4, m]) for j in range(2))
                    tmp = [rotin[:, j, 0:4 * m].rearrange("p (q t) -> p q t", q=4) for j in range(4)]
                    pool.wait_ge(pool_chain, at + 1 + 3 * k)
                    tt(tmp[0], c[:, :, 0:m], pc, ALU.mult)
                    tt(tmp[1], ns[:, :, 0:m], pns, ALU.mult)
                    tt(tmp[2], c[:, :, 0:m], pns, ALU.mult)
                    tt(tmp[3], ns[:, :, 0:m], pc, ALU.mult).then_inc(pool_chain, 1)
                    pool.wait_ge(pool_chain, at + 2 + 3 * k)
                    tt(c[:, :, m:2 * m], tmp[0], tmp[1], ALU.subtract).then_inc(pool_chain, 1)
                    tt(ns[:, :, m:2 * m], tmp[2], tmp[3], ALU.add)\
                        .then_inc(pool_chain if k < NPOW - 1 else tab_built, 1)

            for b in range(2):
                build_table(b, 0)
            rsqrt(1)
            with pool.Fori(1, KD // 2) as i:
                for b in range(2):
                    build_table(b, i)

            rsqrt(1)
            pool.wait_ge(mask_in, 16)
            for kt in range(KD):
                cos, nsin = (tab[:, kt % 2, j, :] for j in range(2))
                for m, w, j in ((0, cos, 0), (3, nsin, 0), (1, nsin, 1), (2, cos, 1)):
                    if m in (0, 1):
                        pool.wait_ge((g_re, g_im)[j], kt + 1)
                    if kt >= 1:
                        pool.wait_ge((h_re, h_re, h_im, h_im)[m], kt)
                    tt(prod[:, m, :], w, gs[:, j, :], ALU.mult).then_inc(prod_done[m], 1)
                if kt >= 1:
                    pool.wait_ge(y_done, kt)
                tt(tm.rearrange("p (b n) -> p b n", b=8), s5_t[:, kt, :].unsqueeze(1).to_broadcast([P, 8, 16]),
                   bd_mask.rearrange("p (b n) -> p b n", b=8), ALU.mult).then_inc(tm_ready, 1)
                pool.wait_ge(prod_done[3], kt + 1)
                pool.wait_ge(prod_done[2], kt + 1)
                tt(h_sb[:, 1, :, 1:NC + 1], *(prod[:, m, :].rearrange("p (q n) -> p q n", q=4) for m in (3, 2)),
                   ALU.subtract).then_inc(h_im, 1)
            rsqrt(2)


def _chunks_in(w):
    import numpy as np
    n = w.shape[1] // 512
    a = w.reshape(2, 4, 128, n, 512).transpose(3, 0, 2, 1, 4)
    return np.ascontiguousarray(a).reshape(2 * n, 128, 2048)


def _chunks_out(w):
    import numpy as np
    n = w.shape[0] // 256
    return np.ascontiguousarray(w.reshape(n, 2, 128, 1024).transpose(0, 2, 1, 3)).reshape(n, 128, 2048)


def _interleave(a, b, n):
    import numpy as np
    k = a.shape[0]
    return np.stack([a.reshape(k, -1, n), b.reshape(k, -1, n)], axis=2).reshape(k, -1)


def _lay_out(inp):
    import numpy as np
    f = np.float32
    parts = []

    def ffn(i, j):
        parts.append(_chunks_in(_interleave(inp["ffn_w1"][i, j], inp["ffn_w3"][i, j], 256)))
        parts.append(_chunks_out(inp["ffn_w2"][i, j]))

    ffn(0, 0)
    w = inp["ret_w_in"][0]
    parts.append(_chunks_in(w[:, :2048]))
    parts.append(_chunks_in(_interleave(w[:, 2048:4096], w[:, 4096:], 512)))
    parts.append(_chunks_out(inp["ret_w_out"][0]))
    ffn(0, 1)
    ffn(1, 0)
    parts.append(_chunks_in(inp["s5_w_in"][0]))
    parts.append(_chunks_in(inp["s5_w_glu"][0])[[0, 2, 1, 3]])
    parts.append(_chunks_out(inp["s5_w_out"][0]))
    ffn(1, 1)

    def states(a):
        a = a.reshape(32, 2, 64, *a.shape[2:])
        return np.ascontiguousarray(np.moveaxis(a, 0, 2)).reshape(128, 32, *a.shape[3:])

    step = np.broadcast_to(inp["s5_log_step"][0][:, None], (64, 64))
    a_par = np.stack([states(inp["s5_a_re"][0]), states(inp["s5_a_im"][0]), states(step)], axis=1)
    b_par = np.stack([states(inp["s5_b_re"][0]), states(inp["s5_b_im"][0])], axis=1)
    c_compact = np.stack([states(inp[k][0].transpose(0, 2, 1)) for k in ("s5_c_re", "s5_c_im")], axis=1)
    c = np.zeros((8, 128, 2, 4, 32), f)
    for ri, name in enumerate(("s5_c_re", "s5_c_im")):
        cs = states(inp[name][0].transpose(0, 2, 1)).reshape(128, 8, 4, 16).transpose(1, 0, 2, 3)
        c[:, :64, ri, :, :16] = cs[:, :64]
        c[:, 64:, ri, :, 16:] = cs[:, 64:]

    half = 128
    inv = f(10000.0) ** (-np.arange(half, dtype=f) / f(half))
    ang = np.arange(256, dtype=f)[:, None] * inv[None, :]
    cossin = np.stack([np.cos(ang), np.sin(ang)]).astype(f)
    cossin = cossin.reshape(2, 2, 128, 128).transpose(2, 0, 1, 3).reshape(128, 512)
    lg = np.log1p(-np.power(2.0, -5.0 - np.arange(4, dtype=np.float64)))[:, None, None]
    j, i = np.arange(128.0)[:, None], np.arange(128.0)[None, :]
    inner = np.where(i >= j, np.exp(np.maximum(i - j, 0) * lg), 0.0)
    cross = np.exp((128 + i - j) * lg)
    masks = (np.stack([inner, cross], axis=1) / 16.0).astype(f)
    masks = masks.transpose(2, 0, 1, 3).reshape(128, 1024)
    groups = np.arange(128) // 16
    return {
        "s5_c_compact": c_compact, "bd_mask": (groups[:, None] == groups[None, :]).astype(f),
        "x": inp["x"][0], "wstream": np.concatenate(parts), "ident": np.eye(128, dtype=f),
        "ln_g": inp["ln_g"].reshape(6, 1024), "ln_b": inp["ln_b"].reshape(6, 1024),
        "s5_a": a_par, "s5_b": b_par, "s5_c": c.reshape(8, 128, 2, 128),
        "s5_d": inp["s5_d"][0].reshape(8, 128).T, "cossin": cossin, "masks": masks,
    }


def kernel(**inputs):
    import numpy as np
    import concourse.bacc as bacc
    from concourse.bass_utils import run_bass_kernel_spmd

    nc = bacc.Bacc("TRN2", target_bir_lowering=False, num_devices=1, dynamic_dma_scratch_size=1024)
    laid = {k: np.ascontiguousarray(v) for k, v in _lay_out({k: np.asarray(v) for k, v in inputs.items()}).items()}
    ins = {k: nc.dram_tensor(f"in_{k}", v.shape, F32, kind="ExternalInput").ap() for k, v in laid.items()}
    out = nc.dram_tensor("out", (T, D), F32, kind="ExternalOutput").ap()
    build(nc, ins, out)
    r = run_bass_kernel_spmd(nc, [{f"in_{k}": v for k, v in laid.items()}], core_ids=[0])
    return r.results[0]["out"].reshape(1, T, D)
```

```python
from contextlib import ExitStack

import concourse.bass as bass
from concourse import mybir

ALU = mybir.AluOpType
ACT = mybir.ActivationFunctionType
F32 = mybir.dt.float32
F32R = mybir.dt.float32r

P = 128
D = 1024
T = 256
NT = T // P
KD = D // P
DFF = 2816
KF = DFF // P
BLK = 256
NB_FFN = DFF // BLK
HEADS, DK, DV = 4, 256, 512
NB_RET = (2 * HEADS * DK + 2 * HEADS * DV) // 512
ALPHA = 4.0 ** 0.25
LN_EPS = 1e-5
GN_EPS = 1e-5
CH = 2048
RING = 4
PAIRS = 32
NC = T // 2
NPOW = 7
TURN = 6.283185307179586
TURN_PARTS = (6.28125, 1015 / 2 ** 19, -6.516827184555041e-07)
PI_DOWN = 3.1415925
ROUNDER = 12582912.0

CHUNK_FFN = [0, 65, 98, 143]
CHUNK_RET_IN, CHUNK_RET_OUT = 33, 57
CHUNK_S5_IN, CHUNK_GLU, CHUNK_S5_OUT = 131, 135, 139
N_CHUNKS = 176
U_FFN = [0, 24, 35, 48]
U_RET, U_LAST_HEAD, U_S5_IN = 11, 23, 46

_r = _z = 0


def _take(n, split):
    global _r, _z
    at = (_r, _z)
    _r += n
    if split:
        _z += n
    return at


TR_X, TR_FFN = {}, {}
TR_X[0] = _take(4, True)
TR_FFN[0] = _take(NB_FFN, True)
TR_BT = _take(9, False)
TR_X[1] = _take(4, True)
TR_QK = _take(8, False)
TR_HEAD = _take(8, True)
TR_X[2] = _take(4, True)
TR_FFN[1] = _take(NB_FFN, True)
TR_X[3] = _take(4, True)
TR_FFN[2] = _take(NB_FFN, True)
TR_X[4] = _take(4, True)
TR_U = _take(2, False)
TR_X[5] = _take(4, True)
TR_FFN[3] = _take(NB_FFN, True)


def n_out_used(n):
    count = 0
    for first, last in ((22, 32), (57, 64), (87, 97), (120, 130), (139, 142), (165, 175)):
        count += max(0, min(n, last - 1) - first + 1)
    return count


def n_u_done(u):
    return u + 1 - (u > U_LAST_HEAD)


def n_sil(u):
    f = max(f for f in range(4) if U_FFN[f] <= u)
    return NB_FFN * f + u - U_FFN[f] + 1


def build(nc, ins, out):
    ctx = ExitStack()
    with ctx:
        def sb(name, shape, dt=F32):
            return ctx.enter_context(nc.sbuf_tensor(name, shape, dt))

        def sem(name):
            return ctx.enter_context(nc.semaphore(name))

        raw = sb("raw", [P, RING, CH])
        w_hi_sb = sb("w_hi_sb", [P, RING, CH], F32R)
        w_lo_sb = sb("w_lo_sb", [P, RING, CH], F32R)
        xt_hi = sb("xt_hi", [P, KD, T], F32R)
        xt_lo = sb("xt_lo", [P, KD, T], F32R)
        gt_hi = sb("gt_hi", [P, KF, T], F32R)
        gt_lo = sb("gt_lo", [P, KF, T], F32R)
        x = sb("x", [P, NT, D])
        gb = sb("gb", [P, 2, D])
        sil = sb("sil", [P, NT, BLK])
        ident = sb("ident", [P, P])
        minus_half = sb("minus_half", [P, 1])
        unit = sb("unit", [P, 2, 4])
        stats = sb("stats", [P, NT, 20])
        s5_pow = sb("s5_pow", [P, 2, NPOW + 1, PAIRS])
        s5_abar = sb("s5_abar", [P, 3, PAIRS])
        s5_t = sb("s5_t", [P, KD, 16])
        s5_d = sb("s5_d", [P, KD])
        region = sb("region", [P, 11536])

        def carve(at, *dims):
            n = 1
            for d in dims:
                n *= d
            v = region[:, at:at + n]
            if len(dims) == 1:
                return v
            if len(dims) == 2:
                v = v.rearrange("p (a b) -> p a b", a=dims[0])
            if len(dims) == 3:
                v = v.rearrange("p (a b c) -> p a b c", a=dims[0], b=dims[1])
            return v

        qt = carve(0, 2 * HEADS, T)
        kt_ = carve(2048, 2 * HEADS, T)
        v_sb = carve(4096, NT, DV)
        g_sb = carve(5120, NT, DV)
        og = carve(6144, NT, DV)
        cossin = carve(7168, 2, NT, P)
        masks = carve(7680, HEADS, 2, P)
        s_sb = carve(8704, 3, P)
        rot = [carve(9088, 2, 2, P), carve(10624, 2, 2, P)]
        rtmp = carve(9600, 4, 2, P)
        tab = carve(0, 2, 2, 4 * NC)
        bt = carve(2048, 2, 4, P)
        ct = carve(3072, 2, 4, 4 * 32)
        ut = carve(4096, KD, T)
        rotin = carve(6144, 4, 512)
        gs = carve(8192, 2, 512)
        upad = carve(9216, 2, 4, NC)
        h_sb = carve(10240, 2, 4, NC + 2)
        bd_mask = carve(11408, P)
        pow_room = s5_pow[:, :, :, :].rearrange("p a k n -> p (a k n)")
        tm = [pow_room[:, P * i:P * i + P] for i in range(4)] + [carve(11280, P)]
        prod = gb[:, :, :].rearrange("p a (b n) -> p (a b) n", b=2)
        small = carve(0, 24, PAIRS)
        c_cmp = carve(768, 2, PAIRS, 16)
        b_in = carve(1792, 2, PAIRS, 16)
        bz = carve(2816, 4, PAIRS, 32)
        bprod = carve(6912, 2, PAIRS, 16)
        bbar = carve(7936, 2, PAIRS, 16)
        ca = carve(8960, 2, PAIRS, 16)
        bt_out = carve(9984, 2, 512)

        U = [ctx.enter_context(nc.psum_tensor(f"U{i}", [P, 512], F32)) for i in range(2)]
        TR = [ctx.enter_context(nc.psum_tensor(f"TR{i}", [P, 512], F32)) for i in range(2)]
        A = ctx.enter_context(nc.psum_tensor("A", [P, 2048], F32))
        bank = [A[:, 512 * i:512 * i + 512] for i in range(4)]
        acc = [A[:, 1024 * t:1024 * t + 1024] for t in range(2)]

        bt_dram = nc.dram_tensor("bt_dram", (KD, P, 4 * P), F32).ap()
        ca_dram = nc.dram_tensor("ca_dram", (P, 2, KD, 4 * 16), F32).ap()
        tab_dram = nc.dram_tensor("tab_dram", (KD, P, 2 * 4 * NC), F32).ap()

        raw_in = [sem(f"raw_in{i}") for i in range(RING)]
        start_in = [sem(f"start_in{i}") for i in range(2)]
        warm_ready = sem("warm_ready")
        start_hi, start_lo = sem("start_hi"), sem("start_lo")
        w_hi, w_lo, out_used = sem("w_hi"), sem("w_lo"), sem("out_used")
        u_done = [sem(f"u_done{i}") for i in range(2)]
        u_free = [sem(f"u_free{i}") for i in range(2)]
        sil_done = [sem(f"sil_done{i}") for i in range(2)]
        t_done = sem("t_done")
        t_free = [sem(f"t_free{i}") for i in range(2)]
        t_hi = sem("t_hi")
        x_in = [sem(f"x_in{t}") for t in range(NT)]
        x_ready, x_scaled = sem("x_ready"), sem("x_scaled")
        gb_in, const_in = sem("gb_in"), sem("const_in")
        small_in, b_landed = sem("small_in"), sem("b_landed")
        ret_const_in = sem("ret_const_in")
        acc_done = sem("acc_done")
        out_done = sem("out_done")
        dve_chain, pool_chain = sem("dve_chain"), sem("pool_chain")
        rot_done, sc_done, sc_masked = sem("rot_done"), sem("sc_done"), sem("sc_masked")
        o_done, o_read, og_done = sem("o_done"), sem("o_read"), sem("og_done")
        var_ready, rstd_ready = sem("var_ready"), sem("rstd_ready")
        p_dt, p_theta, p_trig = sem("p_dt"), sem("p_theta"), sem("p_trig")
        bz_ready = sem("bz_ready")
        p_f, p_ca, ca_stored = sem("p_f"), sem("p_ca"), sem("ca_stored")
        bt_out_free = [sem(f"bt_out_free{i}") for i in range(2)]
        tab_built = sem("tab_built")
        tab_stored = [sem(f"tab_stored{i}") for i in range(2)]
        bt_in, tab_in, ct_in = ([sem(f"{k}_in{i}") for i in range(2)] for k in ("bt", "tab", "ct"))
        upad_ready, h_re, h_im = sem("upad_ready"), sem("h_re"), sem("h_im")
        zeroed, tm_ready, y_done, mask_in = sem("zeroed"), sem("tm_ready"), sem("y_done"), sem("mask_in")
        bu_done, bu_read = sem("bu_done"), sem("bu_read")
        g_re, g_im = sem("g_re"), sem("g_im")
        prod_done = [sem(f"prod_done{i}") for i in range(4)]
        y_in, act_gelu, act_hi, act_split = sem("y_in"), sem("act_gelu"), sem("act_hi"), sem("act_split")
        glu_used, glu_done, sig_done = sem("glu_used"), sem("glu_done"), sem("sig_done")
        z_done, z_hi, z_split = sem("z_done"), sem("z_hi"), sem("z_split")

        def gt_part(gt, b, i):
            v = gt[:, 2 * b:2 * b + 2, :] if isinstance(i, int) else gt[:, bass.ds(4 * i + 2 * b, 2), :]
            return v.rearrange("p a n -> p (a n)")

        def by_parity(src, k):
            return src.rearrange("p (k c a) -> p k a c", k=k, a=2)

        def from_parity(gt, k):
            return gt[:, k:k + 2, :].rearrange("p k (c a) -> p k a c", a=2)

        block = ctx.enter_context(nc.Block())

        @block.sync
        def _(sp):
            def load(n, i=0, step=0):
                slot = n % RING
                if n >= RING:
                    sp.wait_ge(w_lo, n - RING + 1 + step * i)
                src = ins["wstream"][n] if step == 0 else \
                    ins["wstream"][bass.ds(n + step * i, 1), :, :].rearrange("a p n -> (a p) n")
                sp.dma_start(raw[:, slot, :], src).then_inc(raw_in[slot], 16)

            def loads(first, last):
                turns = (last - first) // RING
                with sp.Fori(0, turns) as i:
                    for k in range(RING):
                        load(first + k, i, RING)
                for n in range(first + turns * RING, last):
                    load(n)

            sp.dma_start(small[:, 0:3, :], ins["s5_a"]).then_inc(small_in, 16)
            sp.dma_start(x[:, 0, :], ins["x"][0:P, :]).then_inc(x_in[0], 16)
            sp.dma_start(ident[:, :], ins["ident"]).then_inc(const_in, 16)
            for n in range(2):
                sp.dma_start(raw[:, n, 0:CH // 2], ins["wstream"][n][:, 0:CH // 2]).then_inc(start_in[n], 16)
                sp.dma_start(raw[:, n, CH // 2:CH], ins["wstream"][n][:, CH // 2:CH]).then_inc(raw_in[n], 16)
            sp.dma_start(x[:, 1, :], ins["x"][P:T, :]).then_inc(x_in[1], 16)
            load(2)
            load(3)
            sp.dma_start(b_in, ins["s5_b"]).then_inc(b_landed, 16)
            sp.dma_start(c_cmp, ins["s5_c_compact"]).then_inc(b_landed, 16)
            sp.dma_start(s5_d[:, :], ins["s5_d"]).then_inc(b_landed, 16)
            sp.dma_start(bd_mask, ins["bd_mask"]).then_inc(mask_in, 16)
            loads(RING, 100)
            with sp.Fori(0, KD // 2) as i:
                for b in range(2):
                    for k in range(RING):
                        load(100 + RING * b + k, i, 2 * RING)
                    sp.wait_ge(tab_built, 2 * i + b + 1)
                    sp.dma_start(tab_dram[bass.ds(2 * i + b, 1), :, :].rearrange("a p n -> (a p) n"),
                                 tab[:, b].rearrange("p a n -> p (a n)")).then_inc(tab_stored[b], 16)

            def load_bt(kt):
                b = kt % 2
                if kt >= 2:
                    sp.wait_ge(bu_done, kt - 1)
                sp.dma_start(bt[:, b].rearrange("p a n -> p (a n)"), bt_dram[kt]).then_inc(bt_in[b], 16)

            def load_tab(kt):
                b = kt % 2
                if kt >= 2:
                    sp.wait_ge(g_im, kt - 1)
                    for m in (3, 2):
                        sp.wait_ge(prod_done[m], kt - 1)
                sp.dma_start(tab[:, b].rearrange("p a n -> p (a n)"), tab_dram[kt]).then_inc(tab_in[b], 16)

            def load_ct(kt):
                b = kt % 2
                if kt >= 2:
                    sp.wait_ge(y_done, kt - 1)
                sp.dma_start(ct[:, b, 0:2, :], ins["s5_c"][kt]).then_inc(ct_in[b], 16)
                for g in range(2):
                    half = slice(64 * g, 64 * g + 64)
                    for ri in range(2):
                        sp.dma_start(ct[half, b, 2 + ri, :].rearrange("p (i g n) -> p i g n", i=4, g=2)[:, :, g, :],
                                     ca_dram[half, ri, kt, :].rearrange("p (i n) -> p i n", i=4))\
                          .then_inc(ct_in[b], 16)

            for c in range(2):
                sp.wait_ge(tab_stored[c], 16 * KD // 2)
                sp.wait_ge(bt_out_free[c], 16 * KD // 2)
            sp.wait_ge(ca_stored, 16)
            sp.wait_ge(zeroed, 1)
            for kt in range(2):
                load_bt(kt)
                load_tab(kt)
                load_ct(kt)
            for n in range(132, 141):
                load(n)
            load_bt(2)
            for kt in range(2, KD):
                if kt + 1 < KD:
                    load_bt(kt + 1)
                load_tab(kt)
                load_ct(kt)
            loads(141, N_CHUNKS)
            for t in range(NT):
                for h in range(2):
                    cols = slice(512 * h, 512 * h + 512)
                    sp.wait_ge(x_ready, 4 * 5 + 2 * t + h + 1)
                    sp.dma_start(out[P * t:P * t + P, cols], x[:, t, cols]).then_inc(out_done, 16)
            sp.wait_ge(out_done, 16 * 2 * NT)

        @block.tensor
        def _(pe):
            def w_row(n, k, cols):
                at = n % RING
                return [w[:, at, k * cols[1] + cols[0]:k * cols[1] + cols[0] + 512]
                        for w in (w_hi_sb, w_lo_sb)]

            def product(o, a_hi, a_lo, b_hi, b_lo, start, stop, **group):
                pe.matmul(o, a_hi, b_hi, start=start, stop=False, **group)
                pe.matmul(o, a_hi, b_lo, start=False, stop=False, **group)
                return pe.matmul(o, a_lo, b_hi, start=False, stop=stop, **group)

            def in_pair(n, u, i=0, du=0, between=None, l=None, middle=None):
                for t in range(NT):
                    if l == 0 and t == 0:
                        transpose_x(0, 0)
                        warm_up(8)
                    if u >= 1:
                        pe.wait_ge(u_free[t], u + du * i)
                    for c in range(2):
                        if t == 0:
                            if l == 0:
                                pe.wait_ge(start_lo, c + 1)
                            else:
                                pe.wait_ge(w_lo, n + c + 1 + 2 * du * i)
                        if l is not None:
                            split_x(l, t, c)
                        for k in range(4):
                            if t == 0 and l == 0 and k == 2:
                                pe.wait_ge(w_lo, n + c + 1)
                            kd = 4 * c + k
                            b_hi, b_lo = w_row(n + c, k, (0, 512))
                            tok = slice(P * t, P * t + P)
                            last = product(U[t][:, :], xt_hi[:, kd, tok], xt_lo[:, kd, tok], b_hi, b_lo,
                                           kd == 0, kd == KD - 1)
                            if kd == KD - 1:
                                last.then_inc(u_done[t], 1)
                            if l and t == 0 and kd >= KD - 2:
                                transpose_x(l, 1, (kd - KD + 2,))
                        if l == 0 and t == 0 and c == 0:
                            transpose_x(0, 1)
                        if middle and t == 0 and c == 0:
                            middle()
                    if t == 0 and between:
                        between()

            def out_chunks(ns, k0, k_last, between=None, next_x=None):
                for t in range(NT):
                    tok = slice(P * t, P * t + P)
                    for half in range(2):
                        for c, n in enumerate(ns):
                            if t == 0 and half == 0:
                                pe.wait_ge(w_lo, n + 1)
                            for k in range(2):
                                kf = k0 + 2 * c + k
                                b_hi, b_lo = w_row(n, k, (512 * half, 1024))
                                last = product(acc[t][:, 512 * half:512 * half + 512], gt_hi[:, kf, tok],
                                               gt_lo[:, kf, tok], b_hi, b_lo, kf == 0, kf == k_last)
                                if next_x and t == 1 and half == 1 and kf in (k_last - 2, k_last - 1):
                                    transpose_x(next_x, 0, (kf - k_last + 2,))
                            if kf == k_last:
                                last.then_inc(acc_done, 1)
                            elif t == 1 and half == 1:
                                last.then_inc(out_used, 1)
                    if t == 0 and between:
                        between()

            def begin_tr(r, i=0, dr=0):
                if r >= 2:
                    pe.wait_ge(t_free[r % 2], r // 2 + dr * i)

            def transpose_x(l, t, halves=(0, 1)):
                if l == 0:
                    pe.wait_ge(const_in, 16)
                    pe.wait_ge(x_in[t], 16)
                for h in halves:
                    r = TR_X[l][0] + 2 * t + h
                    if l > 0:
                        pe.wait_ge(x_ready, 4 * (l - 1) + 2 * t + h + 1)
                    begin_tr(r)
                    for k in range(4):
                        last = pe.transpose(TR[r % 2][:, P * k:P * k + P],
                                            x[:, t, P * (4 * h + k):P * (4 * h + k) + P], ident[:, :])
                    last.then_inc(t_done, 1)

            def split_x(l, t, h):
                r = TR_X[l][0] + 2 * t + h
                pe.wait_ge(t_free[r % 2], r // 2 + 1)

            def transpose_g(f, b, i=0):
                r = TR_FFN[f][0] + b
                begin_tr(r, i, 1)
                for t in range(NT):
                    pe.wait_ge(u_free[t], U_FFN[f] + b + 1 + 2 * i)
                for j in range(2):
                    for t in range(NT):
                        last = pe.transpose(TR[r % 2][:, 256 * j + P * t:256 * j + P * t + P],
                                            sil[:, t, P * j:P * j + P], ident[:, :])
                last.then_inc(t_done, 1)

            def ffn(f, l, extra=None):
                n, u = CHUNK_FFN[f], U_FFN[f]
                in_pair(n, u, l=l)
                with pe.Fori(0, (NB_FFN - 1) // 2) as i:
                    for b in (1, 2):
                        in_pair(n + 2 * b, u + b, i, 2, between=lambda: transpose_g(f, b - 1, i))
                n += 2 * NB_FFN
                def gt_ready(b):
                    r = TR_FFN[f][0] + b
                    pe.wait_ge(t_free[r % 2], r // 2 + 1)
                gt_ready(NB_FFN - 3)
                gt_ready(NB_FFN - 2)
                out_chunks([n], 0, KF - 1, between=lambda: transpose_g(f, NB_FFN - 1))
                for p in range(5):
                    if p == 4:
                        gt_ready(NB_FFN - 1)
                    last_pair = p == 4
                    out_chunks([n + 1 + 2 * p, n + 2 + 2 * p], 2 + 4 * p, KF - 1,
                               between=extra if last_pair else None,
                               next_x=(l + 1 if f != 1 else 3) if last_pair and f < 3 else None)
                    if extra and not last_pair:
                        extra(p)

            def transpose_b(p=4):
                if p == 0:
                    pe.wait_ge(bz_ready, 1)
                for kt in (2 * p, 2 * p + 1) if p < 4 else ():
                    r = TR_BT[0] + kt
                    begin_tr(r)
                    for m in range(4):
                        last = pe.transpose(TR[r % 2][:, P * m:P * m + P],
                                            bz[:, m, 4 * kt:4 * kt + 4, :].rearrange("p a b -> p (a b)"),
                                            ident[:, :])
                    last.then_inc(t_done, 1)
                if p < 4:
                    return
                r = TR_BT[0] + KD
                begin_tr(r)
                pe.wait_ge(p_ca, 1)
                for pair in range(PAIRS):
                    i, kt = pair % 4, pair // 4
                    for ri in range(2):
                        last = pe.matmul(TR[r % 2][32 * i:32 * i + 32, 16 * kt:16 * kt + 16],
                                         bz[:, 2 + ri, pair, :], c_cmp[:, ri, pair, :],
                                         start=ri == 0, stop=ri == 1)
                last.then_inc(t_done, 1)

            def warm_up(n):
                for _ in range(n):
                    pe.matmul(U[1][:, 0:BLK], sil[:, 0, 0:P], sil[:, 0, :], start=True, stop=True)

            pe.wait_ge(warm_ready, 1)
            warm_up(4)
            ffn(0, 0, extra=transpose_b)

            def transpose_qk(b, t):
                r = TR_QK[0] + 2 * b + t
                begin_tr(r)
                pe.wait_ge(rot_done, 2 * b + t + 1)
                for m in range(4):
                    last = pe.transpose(TR[r % 2][:, P * m:P * m + P], rot[t][:, m // 2, m % 2, :], ident[:, :])
                last.then_inc(t_done, 1)

            def scores(h):
                if h == 0:
                    for r in (TR_QK[0] + 6, TR_QK[0] + 7):
                        pe.wait_ge(t_free[r % 2], r // 2 + 1)
                else:
                    pe.wait_ge(sc_masked, h)
                for j, cols in ((0, slice(0, 256)), (1, slice(128, 256))):
                    o = bank[0][:, 0:256] if j == 0 else bank[0][:, 256:384]
                    for d in range(2):
                        last = pe.matmul(o, kt_[:, 2 * h + d, P * j:P * j + P], qt[:, 2 * h + d, cols],
                                         start=d == 0, stop=d == 1)
                last.then_inc(sc_done, 1)

            def o_bank(h, t):
                return U[t][:, :] if h == HEADS - 1 else bank[1 + t]

            def attend(h):
                pe.wait_ge(sc_masked, h + 1)
                for t in range(NT):
                    pe.wait_ge(u_free[t], U_RET + 4 + 2 * h + 1)
                if h == HEADS - 1:
                    for t in range(NT):
                        pe.wait_ge(u_free[t], U_LAST_HEAD)
                elif h >= 1:
                    pe.wait_ge(o_read, 2 * h)
                pe.matmul(o_bank(h, 0), s_sb[:, 0, :], v_sb[:, 0, :], start=True, stop=True).then_inc(o_done, 1)
                pe.matmul(o_bank(h, 1), s_sb[:, 1, :], v_sb[:, 0, :], start=True, stop=False)
                pe.matmul(o_bank(h, 1), s_sb[:, 2, :], v_sb[:, 1, :], start=False, stop=True).then_inc(o_done, 1)

            def transpose_head(h):
                for t in range(NT):
                    r = TR_HEAD[0] + 2 * h + t
                    begin_tr(r)
                    pe.wait_ge(og_done, 2 * h + t + 1)
                    for m in range(4):
                        last = pe.transpose(TR[r % 2][:, P * m:P * m + P], og[:, t, P * m:P * m + P], ident[:, :])
                    last.then_inc(t_done, 1)

            for b in range(NB_RET):
                def between_tiles():
                    if 1 <= b <= 4:
                        transpose_qk(b - 1, 1)
                    if b == 5:
                        scores(0)
                    if b >= 6 and b % 2 == 0:
                        attend(b // 2 - 3)
                    if b >= 7 and b % 2 == 1:
                        scores((b - 5) // 2)
                        transpose_head((b - 7) // 2)

                in_pair(CHUNK_RET_IN + 2 * b, U_RET + b, between=between_tiles, l=1 if b == 0 else None,
                        middle=(lambda: transpose_qk(b - 1, 0)) if 1 <= b <= 4 else None)
            attend(HEADS - 1)
            for h in range(HEADS):
                if h == 1:
                    transpose_head(HEADS - 1)
                for t in range(NT):
                    r = TR_HEAD[0] + 2 * h + t
                    pe.wait_ge(t_free[r % 2], r // 2 + 1)
                if h == 0:
                    pe.wait_ge(o_read, 2 * (HEADS - 1))
                    pe.wait_ge(sc_masked, HEADS)
                out_chunks([CHUNK_RET_OUT + 2 * h, CHUNK_RET_OUT + 2 * h + 1], 4 * h, 4 * HEADS - 1,
                           next_x=2 if h == HEADS - 1 else None)
            ffn(1, 2)

            ffn(2, 3)

            def columns_pair(n, u, before):
                for m in range(4):
                    h = m // 2
                    if m in before:
                        before[m]()
                    if m % 2 == 0:
                        pe.wait_ge(u_free[h], u)
                    for c in range(2):
                        if m == 0:
                            pe.wait_ge(w_lo, n + c + 1)
                        for k in range(4):
                            kd = 4 * c + k
                            at = (n + c) % RING
                            cols = slice(512 * k + P * m, 512 * k + P * m + P)
                            last = product(U[h][:, 256 * (m % 2):256 * (m % 2) + 256],
                                           w_hi_sb[:, at, cols], w_lo_sb[:, at, cols],
                                           xt_hi[:, kd, :], xt_lo[:, kd, :], kd == 0, kd == KD - 1)
                    if m % 2 == 1:
                        last.then_inc(u_done[h], 1)

            def transpose_u(t):
                r = TR_U[0] + t
                begin_tr(r)
                pe.wait_ge(u_free[t], U_S5_IN + 1)
                for k in range(4):
                    last = pe.transpose(TR[r % 2][:, P * k:P * k + P], gs[:, t, P * k:P * k + P], ident[:, :])
                last.then_inc(t_done, 1)

            def b_u(kt):
                pe.wait_ge(bt_in[kt % 2], 16 * (kt // 2 + 1))
                pe.wait_ge(upad_ready, kt + 1)
                if kt >= 2:
                    pe.wait_ge(bu_read, kt - 1)
                for ri in range(2):
                    for a in range(2):
                        last = pe.matmul(bank[2 * (kt % 2) + ri], bt[:, kt % 2, 2 * a + ri, :],
                                         upad[:, a].rearrange("p q n -> p (q n)"), start=a == 0, stop=a == 1)
                last.then_inc(bu_done, 1)

            def c_h(kt):
                y = U[kt % 2]
                if kt >= 2:
                    pe.wait_ge(y_in, kt - 1)
                else:
                    pe.wait_ge(u_free[kt], U_S5_IN + 2)
                pe.wait_ge(ct_in[kt % 2], 80 * (kt // 2 + 1))
                pe.wait_ge(tm_ready, kt + 1)
                pe.matmul(y[:, 0:NC], tm[kt % 5], ut[:, kt, 0:NC], start=True, stop=False, skip_group_check=True)
                for ri, ready in enumerate((h_re, h_im)):
                    pe.wait_ge(ready, kt + 1)
                    for i in range(4):
                        last = pe.matmul(y[32 * i:32 * i + 32, 0:NC], ct[:, kt % 2, 2 + ri, 32 * i:32 * i + 32],
                                         h_sb[:, ri, i, 0:NC], start=False, stop=ri == 1, skip_group_check=True)
                for i in range(4):
                    for ri in range(2):
                        last = pe.matmul(y[32 * i:32 * i + 32, NC:T], ct[:, kt % 2, ri, 32 * i:32 * i + 32],
                                         h_sb[:, ri, i, 1:NC + 1], start=ri == 0, stop=ri == 1,
                                         skip_group_check=True)
                last.then_inc(y_done, 1)

            in_pair(CHUNK_S5_IN, U_S5_IN, l=4)
            transpose_u(0)
            columns_pair(CHUNK_S5_IN + 2, U_S5_IN + 1,
                         {1: lambda: transpose_u(1), 2: lambda: b_u(0), 3: lambda: b_u(1)})
            def glu(b, kds):
                for kd in kds:
                    n = CHUNK_GLU + 2 * (kd // 4) + b
                    if kd % 4 == 0:
                        pe.wait_ge(w_lo, n + 1)
                        if kd == 0:
                            pe.wait_ge(bu_read, KD - 1 + b)
                    pe.wait_ge(act_split, kd + 1)
                    at = n % RING
                    for m in range(4):
                        cols = slice(512 * (kd % 4) + P * m, 512 * (kd % 4) + P * m + P)
                        last = product(bank[2 * b + m // 2][:, 256 * (m % 2):256 * (m % 2) + 256],
                                       w_hi_sb[:, at, cols], w_lo_sb[:, at, cols],
                                       xt_hi[:, kd, :], xt_lo[:, kd, :], kd == 0 and m % 2 == 0, kd == KD - 1,
                                       skip_group_check=True)
                        if kd == KD - 1 and m % 2 == 1:
                            last.then_inc(glu_done, 1)
                    if kd == 3:
                        last.then_inc(glu_used, 1)

            b_u(2)
            for kt in range(KD):
                c_h(kt)
                if kt + 3 < KD:
                    b_u(kt + 3)
                if kt >= KD - 3 and kt < KD - 1:
                    glu(kt - (KD - 3), range(4))
            for b in range(2):
                glu(b, range(4, KD))
            for p in range(2):
                pe.wait_ge(z_split, 2 * (p + 1))
                out_chunks([CHUNK_S5_OUT + 2 * p, CHUNK_S5_OUT + 2 * p + 1], 4 * p, KD - 1,
                           between=(lambda: pe.wait_ge(sig_done, 4)) if p == 0 else None,
                           next_x=5 if p == 1 else None)
            ffn(3, 5)

        @block.scalar
        def _(act):
            def prep(n, i=0, step=0, used=True):
                if n >= N_CHUNKS:
                    return
                slot = n % RING
                act.wait_ge(raw_in[slot], 16 * (n // RING + 1) + 4 * step * i)
                if not used:
                    act.wait_ge(out_used, n_out_used(n - RING))
                act.activation(w_hi_sb[:, slot, :], raw[:, slot, :], ACT.Copy).then_inc(w_hi, 1)

            def split_x(l, t):
                for h in range(2):
                    r = TR_X[l][0] + 2 * t + h
                    act.wait_ge(t_done, r + 1)
                    act.activation(xt_hi[:, 4 * h:4 * h + 4, P * t:P * t + P],
                                   TR[r % 2][:, :].rearrange("p (k n) -> p k n", k=4), ACT.Copy)\
                       .then_inc(t_hi, 1)

            def scale_x(l, t):
                act.activation(x[:, t, :], x[:, t, :], ACT.Copy, scale=ALPHA).then_inc(x_scaled, 1)

            def load_gb(norm):
                if norm > 0:
                    act.wait_ge(x_ready, 4 * norm)
                for j, name in enumerate(("ln_g", "ln_b")):
                    act.dma_start(gb[:, j, :], ins[name][norm:norm + 1, :].to_broadcast([P, D]))\
                       .then_inc(gb_in, 16)

            def open_stage(l, n, norm):
                if l == 0:
                    s5_exp_dt()
                    s5_trig()
                split_x(l, 0)
                if l == 0:
                    for m in range(2):
                        act.wait_ge(start_in[m], 16)
                        act.activation(w_hi_sb[:, m, 0:CH // 2], raw[:, m, 0:CH // 2], ACT.Copy).then_inc(start_hi, 1)
                        act.wait_ge(raw_in[m], 16)
                        act.activation(w_hi_sb[:, m, CH // 2:CH], raw[:, m, CH // 2:CH], ACT.Copy).then_inc(w_hi, 1)
                scale_x(l, 0)
                if l > 0:
                    prep(n + 2, used=False)
                if l == 1:
                    ret_constants()
                split_x(l, 1)
                scale_x(l, 1)
                if l == 0:
                    prep(n + 2)
                prep(n + 3)
                if norm is not None:
                    load_gb(norm)

            def silu_half(u, t, i=0):
                act.wait_ge(u_done[t], n_u_done(u) + 2 * i)
                act.activation(sil[:, t, :], U[t][:, 0:BLK], ACT.Silu).then_inc(sil_done[t], 1)

            def split_g(f, b, i=0):
                r = TR_FFN[f][0] + b
                act.wait_ge(t_done, r + 1 + 2 * i)
                act.activation(gt_part(gt_hi, b, i), TR[r % 2][:, :], ACT.Copy).then_inc(t_hi, 1)

            def ffn(f, l, norm, late=None):
                n, u = CHUNK_FFN[f], U_FFN[f]
                open_stage(l, n, norm)
                silu_half(u, 0)
                with act.Fori(0, (NB_FFN - 1) // 2) as i:
                    for b in (1, 2):
                        silu_half(u + b - 1, 1, i)
                        prep(n + 2 * b + 2, i, 4)
                        prep(n + 2 * b + 3, i, 4)
                        split_g(f, b - 1, i)
                        silu_half(u + b, 0, i)
                n += 2 * NB_FFN
                silu_half(u + NB_FFN - 1, 1)
                prep(n + 2)
                prep(n + 3)
                split_g(f, NB_FFN - 1)
                prep(n + 4, used=False)
                for p in range(4):
                    prep(n + 5 + 2 * p, used=False)
                    prep(n + 6 + 2 * p, used=False)
                    if late:
                        late(p)

            def s5_exp_dt():
                act.wait_ge(small_in, 16)
                act.activation(small[:, 3, :], small[:, 2, :], ACT.Exp).then_inc(p_dt, 1)

            def s5_trig():
                act.wait_ge(p_theta, 1)
                act.activation(small[:, 11, :], small[:, 4, :], ACT.Exp)
                act.activation(small[:, 12, :], small[:, 10, :], ACT.Sin)
                act.activation(small[:, 13, :], small[:, 10, :], ACT.Sin, scale=0.5).then_inc(p_trig, 1)

            def store_bt(p):
                for kt in (2 * p, 2 * p + 1):
                    r, b = TR_BT[0] + kt, kt % 2
                    act.wait_ge(t_done, r + 1)
                    if kt >= 2:
                        act.wait_ge(bt_out_free[b], 16 * (kt // 2))
                    act.activation(bt_out[:, b, :], TR[r % 2][:, :], ACT.Copy).then_inc(t_free[r % 2], 1)
                    act.wait_ge(t_free[r % 2], r // 2 + 1)
                    act.dma_start(bt_dram[kt], bt_out[:, b, :]).then_inc(bt_out_free[b], 16)
                if p < 3:
                    return
                r = TR_BT[0] + KD
                act.wait_ge(t_done, r + 1)
                act.activation(s5_t.rearrange("p k n -> p (k n)"), TR[r % 2][:, 0:16 * KD], ACT.Copy)\
                   .then_inc(t_free[r % 2], 1)
                act.wait_ge(p_ca, 2)
                act.dma_start(ca_dram.rearrange("p a k n -> p (a k n)"),
                              ca.rearrange("p a b n -> p (a b n)")).then_inc(ca_stored, 16)

            def ret_constants():
                for b in range(2):
                    act.wait_ge(bt_out_free[b], 16 * 4)
                act.wait_ge(ca_stored, 16)
                act.wait_ge(t_free[(TR_BT[0] + KD) % 2], (TR_BT[0] + KD) // 2 + 1)
                act.dma_start(cossin.rearrange("p a t n -> p (a t n)"), ins["cossin"]).then_inc(ret_const_in, 16)
                act.dma_start(masks.rearrange("p h a n -> p (h a n)"), ins["masks"]).then_inc(ret_const_in, 16)

            ffn(0, 0, 0, late=store_bt)
            def move_qk(b, t):
                r = TR_QK[0] + 2 * b + t
                act.wait_ge(t_done, r + 1)
                dst = qt if b < 2 else kt_
                j = 4 * (b % 2)
                act.activation(dst[:, j:j + 4, P * t:P * t + P],
                               TR[r % 2][:, :].rearrange("p (k n) -> p k n", k=4), ACT.Copy)\
                   .then_inc(t_free[r % 2], 1)

            def take_vg(b, t):
                if b < 4:
                    return
                h = (b - 4) // 2
                act.wait_ge(u_done[t], n_u_done(U_RET + b))
                if b % 2 == 0:
                    if h >= 1:
                        act.wait_ge(o_done, 2 * h)
                    act.activation(v_sb[:, t, :], U[t][:, :], ACT.Copy).then_inc(u_free[t], 1)
                else:
                    if h >= 1:
                        act.wait_ge(og_done, 2 * (h - 1) + t + 1)
                    act.activation(g_sb[:, t, :], U[t][:, :], ACT.Silu).then_inc(u_free[t], 1)

            def split_head(h):
                for t in range(NT):
                    r = TR_HEAD[0] + 2 * h + t
                    act.wait_ge(t_done, r + 1)
                    act.activation(gt_hi[:, 4 * h:4 * h + 4, P * t:P * t + P],
                                   TR[r % 2][:, :].rearrange("p (k n) -> p k n", k=4), ACT.Copy)\
                       .then_inc(t_hi, 1)

            n = CHUNK_RET_IN
            open_stage(1, n, 1)
            take_vg(0, 0)
            for b in range(1, NB_RET):
                if b <= 4:
                    move_qk(b - 1, 0)
                take_vg(b - 1, 1)
                if b < 5:
                    act.wait_ge(u_done[1], n_u_done(U_RET + b - 1))
                prep(n + 2 * b + 2)
                prep(n + 2 * b + 3)
                if b <= 4:
                    move_qk(b - 1, 1)
                if b >= 7 and b % 2 == 1:
                    split_head((b - 7) // 2)
                take_vg(b, 0)
            take_vg(NB_RET - 1, 1)
            n = CHUNK_RET_OUT
            prep(n + 2)
            prep(n + 3)
            split_head(HEADS - 1)
            for m in range(4, 10):
                prep(n + m, used=False)
            ffn(1, 2, 2)

            ffn(2, 3, 3)
            n = CHUNK_S5_IN

            open_stage(4, n, None)
            for t in range(NT):
                act.wait_ge(u_done[t], n_u_done(U_S5_IN))
                act.activation(gs[:, t, :], U[t][:, :], ACT.Copy).then_inc(u_free[t], 1)
            for t in range(NT):
                r = TR_U[0] + t
                act.wait_ge(t_done, r + 1)
                act.activation(ut[:, 0:4, :].rearrange("p k (a c) -> p k a c", a=2)[:, :, :, 64 * t:64 * t + 64],
                               by_parity(TR[r % 2][:, :], 4), ACT.Copy).then_inc(t_free[r % 2], 1)

            def pad_u(kt):
                if kt == 0:
                    for r in (TR_U[0], TR_U[0] + 1):
                        act.wait_ge(t_free[r % 2], r // 2 + 1)
                    act.wait_ge(zeroed, 1)
                else:
                    if kt == 4:
                        for h in range(2):
                            act.wait_ge(u_free[h], U_S5_IN + 2)
                    act.wait_ge(bu_done, kt)
                for i in range(4):
                    rows = slice(32 * i, 32 * i + 32)
                    last = act.activation(upad[rows, :, i, :], ut[rows, kt, :].rearrange("p (a n) -> p a n", a=2),
                                          ACT.Copy)
                last.then_inc(upad_ready, 1)

            pad_u(0)
            prep(n + 4)
            prep(n + 5)
            for h in range(2):
                act.wait_ge(u_done[h], n_u_done(U_S5_IN + 1))
                act.activation(ut[:, 4 + 2 * h:6 + 2 * h, :].rearrange("p k (a c) -> p k a c", a=2),
                               by_parity(U[h][:, :], 2), ACT.Copy)\
                   .then_inc(u_free[h], 1)
                pad_u(h + 1)
            prep(n + 6)
            prep(n + 7)

            def gelu_y(kt):
                act.wait_ge(y_in, kt + 1)
                act.activation(ut[:, kt, :], sil[:, kt % 2, :], ACT.Gelu_apprx_tanh).then_inc(act_gelu, 1)
                act.wait_ge(act_gelu, kt + 1)
                act.activation(xt_hi[:, kt, :], ut[:, kt, :], ACT.Copy).then_inc(act_hi, 1)

            pad_u(3)
            for kt in range(KD):
                if kt + 4 < KD:
                    pad_u(kt + 4)
                if kt == KD - 2:
                    act.wait_ge(glu_used, 1)
                    prep(CHUNK_GLU + 4)
                gelu_y(kt)
            act.wait_ge(h_im, KD)
            act.wait_ge(h_re, KD)
            load_gb(4)
            n = CHUNK_GLU + 4
            act.wait_ge(glu_used, 2)
            prep(n + 1)

            def sigmoid(j):
                act.wait_ge(glu_done, j + 1)
                act.activation(rotin[:, j, :], bank[j], ACT.Sigmoid).then_inc(sig_done, 1)

            def split_z(j):
                act.wait_ge(z_done, j + 1)
                act.activation(from_parity(gt_hi, 2 * j),
                               rotin[:, j, :].rearrange("p (k a c) -> p k a c", k=2, a=2), ACT.Copy)\
                   .then_inc(z_hi, 1)

            for j in range(4):
                sigmoid(j)
                if j == 2:
                    prep(n + 2)
                split_z(j)
            prep(n + 3)
            n = CHUNK_S5_OUT
            for m in range(4, 6):
                prep(n + m, used=False)
            ffn(3, 5, 5)

        @block.vector
        def _(dve):
            chain = [0]
            n_var = [0]

            def link(ins_):
                chain[0] += 1
                ins_.then_inc(dve_chain, 1)
                dve.wait_ge(dve_chain, chain[0])

            def prep(n, i=0, step=0):
                if n >= N_CHUNKS:
                    return
                slot = n % RING
                dve.wait_ge(w_hi, n + 1 + step * i)
                dve.tensor_tensor(w_lo_sb[:, slot, :], raw[:, slot, :], w_hi_sb[:, slot, :].bitcast(F32),
                                  ALU.subtract).then_inc(w_lo, 1)

            def split(dst, hi, r, z, i=0):
                dve.wait_ge(t_hi, z + 1 + 2 * i)
                src = TR[r % 2][:, :]
                if len(dst.shape) == 3:
                    src = src.rearrange("p (k n) -> p k n", k=4)
                dve.tensor_tensor(dst, src, hi.bitcast(F32), ALU.subtract).then_inc(t_free[r % 2], 1)

            def split_x(l, t):
                for h in range(2):
                    r, z = (v + 2 * t + h for v in TR_X[l])
                    split(xt_lo[:, 4 * h:4 * h + 4, P * t:P * t + P],
                          xt_hi[:, 4 * h:4 * h + 4, P * t:P * t + P], r, z)

            halves = [slice(512 * h, 512 * h + 512) for h in range(2)]

            def norm_sum(k, t, h, factor):
                cols = halves[h]
                if h == 0:
                    dve.wait_ge(x_scaled, 2 * k + t + 1)
                dve.wait_ge(acc_done, 4 * k + 2 * t + h + 1)
                link(dve.scalar_tensor_tensor(out=x[:, t, cols], in0=acc[t][:, cols], scalar=factor,
                                              in1=x[:, t, cols], op0=ALU.mult, op1=ALU.add))
                return dve.bn_stats(stats[:, t, 6 * h:6 * h + 6], x[:, t, cols])

            def norm_end(k, t, statistics):
                st = stats[:, t, :]
                link(statistics)
                link(dve.bn_aggr(st[:, 12:14], st[:, 0:12]))
                n_var[0] += 1
                dve.tensor_scalar(st[:, 14:15], st[:, 13:14], LN_EPS, None, ALU.add).then_inc(var_ready, 1)
                dve.wait_ge(gb_in, 32 * (k + 1))
                at = chain[0]
                for cols in halves:
                    chain[0] += 1
                    dve.scalar_tensor_tensor(out=x[:, t, cols], in0=x[:, t, cols], scalar=st[:, 12:13],
                                             in1=gb[:, 0, cols], op0=ALU.subtract, op1=ALU.mult)\
                       .then_inc(dve_chain, 1)
                dve.wait_ge(rstd_ready, n_var[0])
                for h, cols in enumerate(halves):
                    dve.wait_ge(dve_chain, at + h + 1)
                    dve.scalar_tensor_tensor(out=x[:, t, cols], in0=x[:, t, cols], scalar=st[:, 15:16],
                                             in1=gb[:, 1, cols], op0=ALU.mult, op1=ALU.add)\
                       .then_inc(x_ready, 1)

            def norm(k, factor, split_0=None):
                norm_sum(k, 0, 0, factor)
                norm_end(k, 0, norm_sum(k, 0, 1, factor))
                norm_sum(k, 1, 0, factor)
                if split_0:
                    split_0()
                norm_end(k, 1, norm_sum(k, 1, 1, factor))

            def open_stage(l, n, factor, first_read):
                if l > 0:
                    norm(l - 1, factor, split_0=lambda: split_x(l, 0))
                else:
                    split_x(0, 0)
                    for m in range(2):
                        for half, done, lo in ((0, start_hi, start_lo), (1, w_hi, w_lo)):
                            cols = slice(CH // 2 * half, CH // 2 * (half + 1))
                            dve.wait_ge(done, m + 1)
                            dve.tensor_tensor(w_lo_sb[:, m, cols], raw[:, m, cols], w_hi_sb[:, m, cols].bitcast(F32),
                                              ALU.subtract).then_inc(lo, 1)
                split_x(l, 1)
                if l > 0:
                    dve.wait_ge(w_lo, n + 2)
                prep(n + 2)
                first_read()
                prep(n + 3)

            def gate(u, t, i=0):
                dve.wait_ge(sil_done[t], n_sil(u) + 2 * i)
                dve.tensor_tensor(sil[:, t, :], sil[:, t, :], U[t][:, BLK:2 * BLK], ALU.mult)\
                   .then_inc(u_free[t], 1)

            def split_g(f, b, i=0):
                r, z = (v + b for v in TR_FFN[f])
                split(gt_part(gt_lo, b, i), gt_part(gt_hi, b, i), r, z, i)

            def ffn(f, l, factor):
                n, u = CHUNK_FFN[f], U_FFN[f]
                open_stage(l, n, factor, lambda: gate(u, 0))
                with dve.Fori(0, (NB_FFN - 1) // 2) as i:
                    for b in (1, 2):
                        gate(u + b - 1, 1, i)
                        prep(n + 2 * b + 2, i, 4)
                        prep(n + 2 * b + 3, i, 4)
                        split_g(f, b - 1, i)
                        gate(u + b, 0, i)
                n += 2 * NB_FFN
                gate(u + NB_FFN - 1, 1)
                prep(n + 2)
                prep(n + 3)
                split_g(f, NB_FFN - 1)
                for m in range(4, 12):
                    prep(n + m)

            def tt(out_, a, b, op):
                return dve.tensor_tensor(out_, a, b, op)

            are, aim, dt = small[:, 0, :], small[:, 1, :], small[:, 3, :]

            def s5_theta():
                dve.wait_ge(small_in, 16)
                tt(small[:, 18, :], are, are, ALU.mult)
                link(tt(small[:, 19, :], aim, aim, ALU.mult))
                link(tt(small[:, 17, :], small[:, 18, :], small[:, 19, :], ALU.add))
                link(dve.reciprocal(small[:, 17, :], small[:, 17, :]))
                dve.wait_ge(p_dt, 1)
                tt(small[:, 4, :], dt, are, ALU.mult)
                link(tt(small[:, 5, :], dt, aim, ALU.mult))
                link(dve.tensor_scalar(small[:, 6, :], small[:, 5, :], 1.0 / TURN, ROUNDER, ALU.mult, ALU.add))
                link(dve.tensor_scalar(small[:, 7, :], small[:, 6, :], ROUNDER, None, ALU.subtract))
                src = small[:, 5, :]
                for j, part in enumerate(TURN_PARTS):
                    link(dve.scalar_tensor_tensor(out=small[:, 8 + j, :], in0=small[:, 7, :], scalar=-part,
                                                  in1=src, op0=ALU.mult, op1=ALU.add))
                    src = small[:, 8 + j, :]
                dve.tensor_scalar(small[:, 10, :], small[:, 10, :], -PI_DOWN, PI_DOWN, ALU.max, ALU.min)\
                   .then_inc(p_theta, 1)

            dve.memset(sil[:, 0, :], 0.0).then_inc(warm_ready, 1)
            s5_theta()
            ffn(0, 0, 0.5)

            def rotate(b, t):
                if b >= 4:
                    return
                dve.wait_ge(u_done[t], n_u_done(U_RET + b))
                src = U[t][:, :].rearrange("p (h a n) -> p h a n", h=2, a=2)
                cos, sin = (cossin[:, j, t, :].unsqueeze(1).to_broadcast([P, 2, P]) for j in range(2))
                if b == 0 and t == 0:
                    dve.wait_ge(ret_const_in, 32)
                if b or t:
                    dve.wait_ge(rot_done, 2 * b + t)
                dve.tensor_tensor(rtmp[:, 0], src[:, :, 0], cos, ALU.mult)
                dve.tensor_tensor(rtmp[:, 1], src[:, :, 1], sin, ALU.mult)
                dve.tensor_tensor(rtmp[:, 2], src[:, :, 0], sin, ALU.mult)
                dve.tensor_tensor(rtmp[:, 3], src[:, :, 1], cos, ALU.mult).then_inc(u_free[t], 1)
                dve.wait_ge(u_free[t], U_RET + b + 1)
                if b:
                    dve.wait_ge(t_done, TR_QK[0] + 2 * b + t - 1)
                dve.tensor_tensor(rot[t][:, :, 0, :], rtmp[:, 0], rtmp[:, 1], ALU.subtract)
                dve.tensor_tensor(rot[t][:, :, 1, :], rtmp[:, 2], rtmp[:, 3], ALU.add).then_inc(rot_done, 1)

            def mask_scores(h):
                dve.wait_ge(sc_done, h + 1)
                if h >= 1:
                    dve.wait_ge(o_done, 2 * h)
                dve.tensor_tensor(s_sb[:, 0:2, :].rearrange("p a n -> p (a n)"), bank[0][:, 0:256],
                                  masks[:, h].rearrange("p a n -> p (a n)"), ALU.mult)
                dve.tensor_tensor(s_sb[:, 2, :], bank[0][:, 256:384], masks[:, h, 0, :], ALU.mult)\
                   .then_inc(sc_masked, 1)

            def norm_head(h, t):
                o = U[t][:, :] if h == HEADS - 1 else bank[1 + t]
                st = stats[:, t, :]
                dve.wait_ge(o_done, 2 * h + t + 1)
                if h >= 1:
                    dve.wait_ge(t_done, TR_HEAD[0] + 2 * (h - 1) + t + 1)
                link(dve.bn_stats(st[:, 0:6], o))
                link(dve.bn_aggr(st[:, 12:14], st[:, 0:6]))
                n_var[0] += 1
                dve.tensor_scalar(st[:, 14:15], st[:, 13:14], GN_EPS, None, ALU.add).then_inc(var_ready, 1)
                dve.wait_ge(u_free[t], U_RET + 5 + 2 * h + 1)
                read = u_free[t] if h == HEADS - 1 else o_read
                dve.scalar_tensor_tensor(out=og[:, t, :], in0=o, scalar=st[:, 12:13], in1=g_sb[:, t, :],
                                         op0=ALU.subtract, op1=ALU.mult).then_inc(read, 1)
                dve.wait_ge(read, U_LAST_HEAD + 1 if h == HEADS - 1 else 2 * h + t + 1)
                dve.wait_ge(rstd_ready, n_var[0])
                dve.tensor_scalar(og[:, t, :], og[:, t, :], st[:, 15:16], None, ALU.mult).then_inc(og_done, 1)

            def split_head(h):
                for t in range(NT):
                    r, z = (v + 2 * h + t for v in TR_HEAD)
                    split(gt_lo[:, 4 * h:4 * h + 4, P * t:P * t + P],
                          gt_hi[:, 4 * h:4 * h + 4, P * t:P * t + P], r, z)

            n = CHUNK_RET_IN
            open_stage(1, n, 0.5, lambda: rotate(0, 0))
            for b in range(1, NB_RET):
                rotate(b - 1, 1)
                prep(n + 2 * b + 2)
                prep(n + 2 * b + 3)
                if b >= 5 and b % 2 == 1:
                    mask_scores((b - 5) // 2)
                if b >= 7 and b % 2 == 1:
                    split_head((b - 7) // 2)
                if b >= 6 and b % 2 == 0:
                    for t in range(NT):
                        norm_head(b // 2 - 3, t)
                rotate(b, 0)
            n = CHUNK_RET_OUT
            prep(n + 2)
            prep(n + 3)
            for t in range(NT):
                norm_head(HEADS - 1, t)
            split_head(HEADS - 1)
            for m in range(4, 9):
                prep(n + m)
            ffn(1, 2, 1.0)

            ffn(2, 3, 0.5)
            n = CHUNK_S5_IN
            open_stage(4, n, 0.5, lambda: None)
            prep(n + 4)
            prep(n + 5)

            def turn_in(kt):
                cos, nsin = (tab[:, kt % 2, j, :] for j in range(2))
                re, im = bank[2 * (kt % 2)], bank[2 * (kt % 2) + 1]
                dve.wait_ge(tab_in[kt % 2], 16 * (kt // 2 + 1))
                dve.wait_ge(bu_done, kt + 1)
                if kt >= 1:
                    dve.wait_ge(g_im, kt)
                for m, (a, w) in enumerate(((re, cos), (im, nsin), (im, cos), (re, nsin))):
                    last = tt(rotin[:, m, :], a, w, ALU.mult)
                last.then_inc(bu_read, 1)

            def recur(kt):
                dve.wait_ge(bu_read, kt + 1)
                tt(rotin[:, 0, :], rotin[:, 0, :], rotin[:, 1, :], ALU.subtract)
                link(tt(rotin[:, 2, :], rotin[:, 2, :], rotin[:, 3, :], ALU.add))
                for j, (done, used) in enumerate(((g_re, prod_done[3]), (g_im, prod_done[2]))):
                    if kt >= 1:
                        dve.wait_ge(used, kt)
                    for q in range(4):
                        pair, at = 4 * kt + q, slice(NC * q, NC * q + NC)
                        last = dve.tensor_tensor_scan(
                            gs[:, j, at], s5_abar[:, 2, pair:pair + 1].to_broadcast([P, NC]),
                            rotin[:, 2 * j, at], 0.0, ALU.mult, ALU.add)
                    last.then_inc(done, 1)

            def turn_out_re(kt):
                dve.wait_ge(prod_done[1], kt + 1)
                if kt >= 1:
                    dve.wait_ge(y_done, kt)
                tt(h_sb[:, 0, :, 1:NC + 1], *(prod[:, m, :].rearrange("p (q n) -> p q n", q=4) for m in (0, 1)),
                   ALU.add).then_inc(h_re, 1)

            def add_du(kt):
                dve.wait_ge(y_done, kt + 1)
                if kt >= 2:
                    dve.wait_ge(act_gelu, kt - 1)
                dve.scalar_tensor_tensor(out=sil[:, kt % 2, :], in0=ut[:, kt, :], scalar=s5_d[:, kt:kt + 1],
                                         in1=U[kt % 2][:, 0:256], op0=ALU.mult, op1=ALU.add)\
                   .then_inc(y_in, 1)

            def split_act(kt):
                dve.wait_ge(act_hi, kt + 1)
                tt(xt_lo[:, kt, :], ut[:, kt, :], xt_hi[:, kt, :].bitcast(F32), ALU.subtract)\
                    .then_inc(act_split, 1)

            for kt in range(KD):
                turn_in(kt)
                if kt >= 1:
                    turn_out_re(kt - 1)
                recur(kt)
                if kt == KD - 1:
                    prep(n + 6)
                if kt >= 2:
                    add_du(kt - 2)
                if kt >= 3:
                    split_act(kt - 3)
            turn_out_re(KD - 1)
            prep(n + 7)
            for kt in (KD - 2, KD - 1):
                add_du(kt)
                split_act(kt - 1)
                if kt == KD - 2:
                    prep(n + 8)
            split_act(KD - 1)
            prep(n + 9)

            for j in range(4):
                z = rotin[:, j, :]
                dve.wait_ge(sig_done, j + 1)
                tt(z, ut[:, 2 * j:2 * j + 2, :].rearrange("p k n -> p (k n)"), z, ALU.mult).then_inc(z_done, 1)
                if j == 2:
                    prep(n + 10)
                dve.wait_ge(z_hi, j + 1)
                tt(from_parity(gt_lo, 2 * j), z.rearrange("p (k a c) -> p k a c", k=2, a=2),
                   from_parity(gt_hi, 2 * j).bitcast(F32), ALU.subtract).then_inc(z_split, 1)
            prep(n + 11)
            prep(CHUNK_S5_OUT + 4)
            ffn(3, 5, 1.0)
            norm(5, 0.5)

        @block.gpsimd
        def _(pool):
            def tt(out_, a, b, op):
                return pool.tensor_tensor(out_, a, b, op)

            chain = [0]

            def link(ins_):
                chain[0] += 1
                ins_.then_inc(pool_chain, 1)
                pool.wait_ge(pool_chain, chain[0])

            n_var = [0]

            def prep(n):
                slot = n % RING
                pool.wait_ge(w_hi, n + 1)
                pool.wait_ge(w_lo, n)
                tt(w_lo_sb[:, slot, :], raw[:, slot, :], w_hi_sb[:, slot, :].bitcast(F32), ALU.subtract)\
                    .then_inc(w_lo, 1)

            def rsqrt(norms):
                for _ in range(norms):
                    for t in range(NT):
                        n_var[0] += 1
                        pool.wait_ge(var_ready, n_var[0])
                        tt(stats[:, t, 15:16], stats[:, t, 14:15], minus_half[:, :], ALU.pow)\
                            .then_inc(rstd_ready, 1)

            are, aim = small[:, 0, :], small[:, 1, :]

            def s5_factors():
                s = lambda j: small[:, j, :]
                pool.wait_ge(p_trig, 1)
                mag, sin, sin_half = s(11), s(12), s(13)
                cos, am1, den, t0, t1 = s(14), s(15), s(17), s(18), s(19)
                ar, ai = s5_abar[:, 0, :], s5_abar[:, 1, :]
                link(tt(t0, sin_half, sin_half, ALU.mult))
                link(pool.tensor_scalar(cos, t0, -2.0, 1.0, ALU.mult, ALU.add))
                tt(ai, mag, sin, ALU.mult)
                link(tt(ar, mag, cos, ALU.mult))
                link(pool.tensor_scalar(am1, ar, 1.0, None, ALU.subtract))
                tt(t0, am1, are, ALU.mult)
                link(tt(t1, ai, aim, ALU.mult))
                link(tt(t0, t0, t1, ALU.add))
                link(tt(s(20), t0, den, ALU.mult))
                tt(t0, ai, are, ALU.mult)
                link(tt(t1, am1, aim, ALU.mult))
                link(tt(t0, t0, t1, ALU.subtract))
                link(tt(s(21), t0, den, ALU.mult))
                pool.tensor_copy(s5_pow[:, 0, 0, :], cos)
                link(pool.tensor_scalar(s5_pow[:, 1, 0, :], sin, -1.0, None, ALU.mult))
                for k in range(1, NPOW + 1):
                    c, ns = s5_pow[:, 0, k - 1, :], s5_pow[:, 1, k - 1, :]
                    tt(t0, c, c, ALU.mult)
                    tt(t1, ns, ns, ALU.mult)
                    link(tt(s(22), c, ns, ALU.mult))
                    tt(s5_pow[:, 0, k, :], t0, t1, ALU.subtract)
                    link(tt(s5_pow[:, 1, k, :], s(22), s(22), ALU.add))
                tt(s5_abar[:, 2, :], mag, mag, ALU.mult).then_inc(p_f, 1)

            pool.memset(minus_half[:, :], -0.5)
            pool.memset(unit[:, 0, :], 1.0)
            link(pool.memset(unit[:, 1, :], 0.0))
            link(pool.memset(bz.rearrange("p a b c -> p (a b c)"), 0.0))
            s5_factors()
            pool.wait_ge(p_f, 1)
            pool.wait_ge(b_landed, 48)

            def times(factor, a, put, ops=(ALU.subtract, ALU.add)):
                f_re, f_im = (v.unsqueeze(2).to_broadcast([P, PAIRS, 16]) for v in factor)
                for ri, other in enumerate((1, 0)):
                    tt(bprod[:, 0], f_re, a[:, ri], ALU.mult)
                    link(tt(bprod[:, 1], f_im, a[:, other], ALU.mult))
                    put(ri, bprod[:, 0], bprod[:, 1], ops[ri])

            def put_diagonal(ri, a, b, op):
                for g in range(2):
                    half = slice(64 * g, 64 * g + 64)
                    step = tt(bz[half, ri, :, 16 * g:16 * g + 16], a[half], b[half], op)
                link(step)

            abar = (s5_abar[:, 0, :], s5_abar[:, 1, :])
            times((small[:, 20, :], small[:, 21, :]), b_in,
                  lambda ri, a, b, op: link(tt(bbar[:, ri], a, b, op)))
            times(abar, bbar, put_diagonal)
            for ri in range(2):
                for g in range(2):
                    half = slice(64 * g, 64 * g + 64)
                    step = pool.tensor_copy(bz[half, 2 + ri, :, 16 * g:16 * g + 16], bbar[half, ri])
            step.then_inc(bz_ready, 1)
            pool.wait_ge(bz_ready, 1)
            zeros = unit[:, 1, 0:1].unsqueeze(2).to_broadcast([P, PAIRS, 16])
            tt(c_cmp[:, 1], zeros, c_cmp[:, 1], ALU.subtract).then_inc(p_ca, 1)
            pool.wait_ge(p_ca, 1)
            tt(bprod[:, 0], abar[0].unsqueeze(2).to_broadcast([P, PAIRS, 16]), c_cmp[:, 0], ALU.mult)
            link(tt(bprod[:, 1], abar[1].unsqueeze(2).to_broadcast([P, PAIRS, 16]), c_cmp[:, 1], ALU.mult))
            link(tt(ca[:, 0], bprod[:, 0], bprod[:, 1], ALU.add))
            tt(bprod[:, 0], abar[1].unsqueeze(2).to_broadcast([P, PAIRS, 16]), c_cmp[:, 0], ALU.mult)
            link(tt(bprod[:, 1], abar[0].unsqueeze(2).to_broadcast([P, PAIRS, 16]), c_cmp[:, 1], ALU.mult))
            tt(ca[:, 1], bprod[:, 0], bprod[:, 1], ALU.subtract).then_inc(p_ca, 1)

            prep(CHUNK_RET_IN + 1)
            rsqrt(1 + HEADS)
            prep(CHUNK_FFN[1] + 1)
            rsqrt(1)
            pool.wait_ge(x_ready, 8)
            pool.memset(ct.rearrange("p a b n -> p (a b n)"), 0.0)
            pool.memset(upad.rearrange("p a q n -> p (a q n)"), 0.0)
            pool.memset(h_sb[:, :, :, 0:1], 0.0).then_inc(zeroed, 1)
            per_table = 3 * NPOW
            base = chain[0]

            def build_table(b, i):
                c, ns = (tab[:, b, j, :].rearrange("p (q t) -> p q t", q=4) for j in range(2))
                at = base + per_table * b + 2 * per_table * i
                if not isinstance(i, int):
                    pool.wait_ge(tab_stored[b], 16 * i)
                one, zero = (unit[:, j, :].unsqueeze(2) for j in range(2))
                tt(c[:, :, 0:1], one, one, ALU.mult)
                tt(ns[:, :, 0:1], zero, one, ALU.mult).then_inc(pool_chain, 1)
                for k in range(NPOW):
                    m = 1 << k
                    pairs = slice(4 * b, 4 * b + 4) if isinstance(i, int) else bass.ds(8 * i + 4 * b, 4)
                    pc, pns = (s5_pow[:, j, k + 1, pairs].unsqueeze(2).to_broadcast([P, 4, m]) for j in range(2))
                    tmp = [rotin[:, j, 0:4 * m].rearrange("p (q t) -> p q t", q=4) for j in range(4)]
                    pool.wait_ge(pool_chain, at + 1 + 3 * k)
                    tt(tmp[0], c[:, :, 0:m], pc, ALU.mult)
                    tt(tmp[1], ns[:, :, 0:m], pns, ALU.mult)
                    tt(tmp[2], c[:, :, 0:m], pns, ALU.mult)
                    tt(tmp[3], ns[:, :, 0:m], pc, ALU.mult).then_inc(pool_chain, 1)
                    pool.wait_ge(pool_chain, at + 2 + 3 * k)
                    tt(c[:, :, m:2 * m], tmp[0], tmp[1], ALU.subtract).then_inc(pool_chain, 1)
                    tt(ns[:, :, m:2 * m], tmp[2], tmp[3], ALU.add)\
                        .then_inc(pool_chain if k < NPOW - 1 else tab_built, 1)

            for b in range(2):
                build_table(b, 0)
            prep(CHUNK_FFN[2] + 1)
            rsqrt(1)
            with pool.Fori(1, KD // 2) as i:
                for b in range(2):
                    build_table(b, i)

            prep(CHUNK_S5_IN + 1)
            rsqrt(1)
            def make_tm(kt):
                if kt >= 5:
                    pool.wait_ge(y_done, kt - 4)
                tt(tm[kt % 5].rearrange("p (b n) -> p b n", b=8), s5_t[:, kt, :].unsqueeze(1).to_broadcast([P, 8, 16]),
                   bd_mask.rearrange("p (b n) -> p b n", b=8), ALU.mult).then_inc(tm_ready, 1)

            pool.wait_ge(mask_in, 16)
            pool.wait_ge(tab_built, KD)
            for kt in range(5):
                make_tm(kt)
            for kt in range(KD):
                cos, nsin = (tab[:, kt % 2, j, :] for j in range(2))
                for m, w, j in ((0, cos, 0), (3, nsin, 0), (1, nsin, 1), (2, cos, 1)):
                    if m in (0, 1):
                        pool.wait_ge((g_re, g_im)[j], kt + 1)
                    if kt >= 1:
                        pool.wait_ge((h_re, h_re, h_im, h_im)[m], kt)
                    tt(prod[:, m, :], w, gs[:, j, :], ALU.mult).then_inc(prod_done[m], 1)
                if kt >= 1:
                    pool.wait_ge(y_done, kt)
                if 5 <= kt + 1 < KD:
                    make_tm(kt + 1)
                pool.wait_ge(prod_done[3], kt + 1)
                pool.wait_ge(prod_done[2], kt + 1)
                tt(h_sb[:, 1, :, 1:NC + 1], *(prod[:, m, :].rearrange("p (q n) -> p q n", q=4) for m in (3, 2)),
                   ALU.subtract).then_inc(h_im, 1)
            prep(CHUNK_FFN[3] + 1)
            rsqrt(2)


def _chunks_in(w):
    import numpy as np
    n = w.shape[1] // 512
    a = w.reshape(2, 4, 128, n, 512).transpose(3, 0, 2, 1, 4)
    return np.ascontiguousarray(a).reshape(2 * n, 128, 2048)


def _chunks_out(w):
    import numpy as np
    n = w.shape[0] // 256
    return np.ascontiguousarray(w.reshape(n, 2, 128, 1024).transpose(0, 2, 1, 3)).reshape(n, 128, 2048)


def _interleave(a, b, n):
    import numpy as np
    k = a.shape[0]
    return np.stack([a.reshape(k, -1, n), b.reshape(k, -1, n)], axis=2).reshape(k, -1)


def _lay_out(inp):
    import numpy as np
    f = np.float32
    parts = []

    def ffn(i, j):
        parts.append(_chunks_in(_interleave(inp["ffn_w1"][i, j], inp["ffn_w3"][i, j], 256)))
        parts.append(_chunks_out(inp["ffn_w2"][i, j]))

    ffn(0, 0)
    w = inp["ret_w_in"][0]
    parts.append(_chunks_in(w[:, :2048]))
    parts.append(_chunks_in(_interleave(w[:, 2048:4096], w[:, 4096:], 512)))
    parts.append(_chunks_out(inp["ret_w_out"][0]))
    ffn(0, 1)
    ffn(1, 0)
    parts.append(_chunks_in(inp["s5_w_in"][0]))
    parts.append(_chunks_in(inp["s5_w_glu"][0])[[0, 2, 1, 3]])
    parts.append(_chunks_out(inp["s5_w_out"][0]))
    ffn(1, 1)

    def states(a):
        a = a.reshape(32, 2, 64, *a.shape[2:])
        return np.ascontiguousarray(np.moveaxis(a, 0, 2)).reshape(128, 32, *a.shape[3:])

    step = np.broadcast_to(inp["s5_log_step"][0][:, None], (64, 64))
    a_par = np.stack([states(inp["s5_a_re"][0]), states(inp["s5_a_im"][0]), states(step)], axis=1)
    b_par = np.stack([states(inp["s5_b_re"][0]), states(inp["s5_b_im"][0])], axis=1)
    c_compact = np.stack([states(inp[k][0].transpose(0, 2, 1)) for k in ("s5_c_re", "s5_c_im")], axis=1)
    c = np.zeros((8, 128, 2, 4, 32), f)
    for ri, name in enumerate(("s5_c_re", "s5_c_im")):
        cs = states(inp[name][0].transpose(0, 2, 1)).reshape(128, 8, 4, 16).transpose(1, 0, 2, 3)
        c[:, :64, ri, :, :16] = cs[:, :64]
        c[:, 64:, ri, :, 16:] = cs[:, 64:]

    half = 128
    inv = f(10000.0) ** (-np.arange(half, dtype=f) / f(half))
    ang = np.arange(256, dtype=f)[:, None] * inv[None, :]
    cossin = np.stack([np.cos(ang), np.sin(ang)]).astype(f)
    cossin = cossin.reshape(2, 2, 128, 128).transpose(2, 0, 1, 3).reshape(128, 512)
    lg = np.log1p(-np.power(2.0, -5.0 - np.arange(4, dtype=np.float64)))[:, None, None]
    j, i = np.arange(128.0)[:, None], np.arange(128.0)[None, :]
    inner = np.where(i >= j, np.exp(np.maximum(i - j, 0) * lg), 0.0)
    cross = np.exp((128 + i - j) * lg)
    masks = (np.stack([inner, cross], axis=1) / 16.0).astype(f)
    masks = masks.transpose(2, 0, 1, 3).reshape(128, 1024)
    groups = np.arange(128) // 16
    return {
        "s5_c_compact": c_compact, "bd_mask": (groups[:, None] == groups[None, :]).astype(f),
        "x": inp["x"][0], "wstream": np.concatenate(parts), "ident": np.eye(128, dtype=f),
        "ln_g": inp["ln_g"].reshape(6, 1024), "ln_b": inp["ln_b"].reshape(6, 1024),
        "s5_a": a_par, "s5_b": b_par, "s5_c": c.reshape(8, 128, 2, 128),
        "s5_d": inp["s5_d"][0].reshape(8, 128).T, "cossin": cossin, "masks": masks,
    }


def kernel(**inputs):
    import numpy as np
    import concourse.bacc as bacc
    from concourse.bass_utils import run_bass_kernel_spmd

    nc = bacc.Bacc("TRN2", target_bir_lowering=False, num_devices=1, dynamic_dma_scratch_size=1024)
    laid = {k: np.ascontiguousarray(v) for k, v in _lay_out({k: np.asarray(v) for k, v in inputs.items()}).items()}
    ins = {k: nc.dram_tensor(f"in_{k}", v.shape, F32, kind="ExternalInput").ap() for k, v in laid.items()}
    out = nc.dram_tensor("out", (T, D), F32, kind="ExternalOutput").ap()
    build(nc, ins, out)
    r = run_bass_kernel_spmd(nc, [{f"in_{k}": v for k, v in laid.items()}], core_ids=[0])
    return r.results[0]["out"].reshape(1, T, D)
```
